# Optimizing a Trainium2 kernel written in Bass

```python
import jax, jax.numpy as jnp
from jax import lax
import numpy as np

D_MODEL = 1024
BATCH = 1
SEQ = 512
DEPTH = 1
DEC_BATCH = 8
DEC_SEQ = 1
PAST_LEN = 4096
PAGE_SIZE = 128

HEAD_DIM = 64
ATTN_SCALE = HEAD_DIM ** -0.5
N_HEADS_A = 8
WIDTH_A = N_HEADS_A * HEAD_DIM
SB_BIAS_HI = -5.0
SB_BIAS_LO = -8.0
DILATED_GROUPS = ((128, 1), (512, 4), (2048, 16))
N_GROUPS_B = len(DILATED_GROUPS)
HEADS_PER_GROUP_B = 4
N_HEADS_B = N_GROUPS_B * HEADS_PER_GROUP_B
WIDTH_B = N_HEADS_B * HEAD_DIM
WIDTH_B_OUT = HEADS_PER_GROUP_B * HEAD_DIM
IN_WIDTH = 3 * WIDTH_A + 3 * WIDTH_B + 2 * D_MODEL
Q_BLOCK = 128
N_EXPERT_GROUPS = 4
EXPERTS_PER_GROUP = 8
N_EXPERTS = N_EXPERT_GROUPS * EXPERTS_PER_GROUP
D_EXPERT = 512
TOP_K_INNER = 2
RMS_EPS = 1e-6

kernel_name = "hybrid_stickbreak_dilated_hmoe_step"

def rmsnorm(x, g):
    xf = x.astype(jnp.float32)
    y = xf * lax.rsqrt(jnp.mean(xf * xf, axis=-1, keepdims=True) + RMS_EPS)
    return (y * g.astype(jnp.float32)).astype(x.dtype)

def alibi_slopes():
    i = jnp.arange(N_HEADS_B, dtype=jnp.float32) + 1.0
    return jnp.exp2(-8.0 * i / N_HEADS_B).reshape(N_GROUPS_B, HEADS_PER_GROUP_B)

def split_projection(h, w_in):
    lead = h.shape[:-1]
    p = h @ w_in
    offs = [WIDTH_A, 2 * WIDTH_A, 3 * WIDTH_A, 3 * WIDTH_A + WIDTH_B, 3 * WIDTH_A + 2 * WIDTH_B,
            3 * WIDTH_A + 3 * WIDTH_B, 3 * WIDTH_A + 3 * WIDTH_B + D_MODEL]
    qa, ka, va, qb, kb, vb, gate_a, gate_b = jnp.split(p, offs, axis=-1)

    def heads_a(t):
        return t.reshape(*lead, N_HEADS_A, HEAD_DIM)

    def heads_b(t):
        return t.reshape(*lead, N_GROUPS_B, HEADS_PER_GROUP_B, HEAD_DIM)

    return heads_a(qa), heads_a(ka), heads_a(va), heads_b(qb), heads_b(kb), heads_b(vb), gate_a, gate_b

def stick_breaking_weights(z, valid):
    log_keep = jnp.where(valid, jax.nn.log_sigmoid(-z), 0.0)
    later = lax.cumsum(log_keep, axis=z.ndim - 1, reverse=True) - log_keep
    return jnp.where(valid, jnp.exp(jax.nn.log_sigmoid(z) + later), 0.0)

def stick_breaking_prompt(q, k, v, b_sb):
    b, s, h, dh = q.shape
    nqb = s // Q_BLOCK
    qblk = jnp.moveaxis(q.reshape(b, nqb, Q_BLOCK, h, dh), 1, 0)
    key_pos = jnp.arange(s)
    bias = b_sb.astype(jnp.float32)[:, None, None]

    def one_block(args):
        qb, start = args
        valid = key_pos[None, :] < (start + jnp.arange(Q_BLOCK))[:, None]
        z = jnp.einsum('bqhd,bkhd->bhqk', qb, k, preferred_element_type=jnp.float32) * ATTN_SCALE + bias
        a = stick_breaking_weights(z, valid)
        return jnp.einsum('bhqk,bkhd->bqhd', a.astype(v.dtype), v, preferred_element_type=jnp.float32)

    o = lax.map(one_block, (qblk, jnp.arange(nqb) * Q_BLOCK))
    return jnp.moveaxis(o, 0, 1).reshape(b, s, h, dh)

def stick_breaking_sample(q, k_new, v_new, cache_k, cache_v, page_table, b_sb):
    bd, t, h, dh = q.shape
    past = page_table.shape[1] * PAGE_SIZE
    k_past = cache_k[page_table].reshape(bd, past, h, dh)
    v_past = cache_v[page_table].reshape(bd, past, h, dh)
    bias = b_sb.astype(jnp.float32)[:, None, None]
    z = jnp.concatenate([
        jnp.einsum('bqhd,bkhd->bhqk', q, k_past, preferred_element_type=jnp.float32),
        jnp.einsum('bqhd,bkhd->bhqk', q, k_new, preferred_element_type=jnp.float32)], axis=-1) * ATTN_SCALE + bias
    qpos = past + jnp.arange(t)
    valid = jnp.arange(past + t)[None, :] < qpos[:, None]
    a = stick_breaking_weights(z, valid).astype(v_new.dtype)
    return (jnp.einsum('bhqk,bkhd->bqhd', a[..., :past], v_past, preferred_element_type=jnp.float32)
            + jnp.einsum('bhqk,bkhd->bqhd', a[..., past:], v_new, preferred_element_type=jnp.float32))

def dilated_group_prompt(q, k, v, window, dilation, slopes):
    b, s, h, dh = q.shape
    band = window // dilation
    n_sub = s // dilation
    nb = -(-n_sub // band)
    lp = nb * band

    def to_sub(t):
        return jnp.moveaxis(t.reshape(b, n_sub, dilation, h, dh), 2, 1)

    qs = jnp.pad(to_sub(q), ((0, 0), (0, 0), (0, lp - n_sub), (0, 0), (0, 0)))
    qs = qs.reshape(b, dilation, nb, band, h, dh)

    def to_blocks(t):
        tp = jnp.pad(to_sub(t), ((0, 0), (0, 0), (band, lp - n_sub), (0, 0), (0, 0)))
        prev = tp[:, :, :lp].reshape(b, dilation, nb, band, h, dh)
        cur = tp[:, :, band:].reshape(b, dilation, nb, band, h, dh)
        return jnp.concatenate([prev, cur], axis=3)

    kb, vb = to_blocks(k), to_blocks(v)
    scores = jnp.einsum('brnqhd,brnkhd->brnhqk', qs, kb, preferred_element_type=jnp.float32) * ATTN_SCALE
    qi = jnp.arange(band)[:, None]
    ku = jnp.arange(2 * band)[None, :]
    rel = qi + band - ku
    jpos = jnp.arange(nb)[:, None, None] * band - band + ku[None]
    valid = (rel >= 0) & (rel <= band) & (jpos >= 0)
    bias = -slopes[:, None, None] * (rel * dilation).astype(jnp.float32)
    scores = jnp.where(valid[:, None], scores + bias, -jnp.inf)
    m = jnp.max(scores, axis=-1, keepdims=True)
    p = jnp.exp(scores - m)
    l = jnp.sum(p, axis=-1, keepdims=True)
    o = jnp.einsum('brnhqk,brnkhd->brnqhd', p.astype(v.dtype), vb, preferred_element_type=jnp.float32)
    o = o / jnp.moveaxis(l, 3, 4)
    lse = jnp.moveaxis(m[..., 0] + jnp.log(l[..., 0]), 3, 4)
    o = jnp.moveaxis(o.reshape(b, dilation, lp, h, dh)[:, :, :n_sub], 1, 2).reshape(b, s, h, dh)
    lse = jnp.moveaxis(lse.reshape(b, dilation, lp, h)[:, :, :n_sub], 1, 2).reshape(b, s, h)
    return o, lse

def dilated_group_sample(q, k_new, v_new, buf, window, dilation, slopes):
    t = q.shape[1]
    wb = buf.shape[1]
    band = window // dilation
    k_all = jnp.concatenate([buf[:, :, 0], k_new], axis=1)
    v_all = jnp.concatenate([buf[:, :, 1], v_new], axis=1)
    steps = jnp.arange(band + 1)
    idx = wb + jnp.arange(t)[:, None] - dilation * steps[None, :]
    valid = idx >= 0
    idx_c = jnp.clip(idx, 0)
    ksel = k_all[:, idx_c]
    vsel = v_all[:, idx_c]
    scores = jnp.einsum('bqhd,bqkhd->bhqk', q, ksel, preferred_element_type=jnp.float32) * ATTN_SCALE
    bias = -slopes[:, None, None] * (dilation * steps).astype(jnp.float32)[None, None, :]
    scores = jnp.where(valid, scores + bias, -jnp.inf)
    m = jnp.max(scores, axis=-1, keepdims=True)
    p = jnp.exp(scores - m)
    l = jnp.sum(p, axis=-1, keepdims=True)
    o = jnp.einsum('bhqk,bqkhd->bqhd', p.astype(v_new.dtype), vsel, preferred_element_type=jnp.float32)
    o = o / jnp.moveaxis(l, 1, 2)
    lse = jnp.moveaxis(m[..., 0] + jnp.log(l[..., 0]), 1, 2)
    new_buf = jnp.stack([k_all[:, -wb:], v_all[:, -wb:]], axis=2)
    return o, lse, new_buf

def combine_dilated(outs, lses):
    o = jnp.stack(outs, axis=0)
    w = jax.nn.softmax(jnp.stack(lses, axis=0), axis=0)
    y = jnp.sum(w[..., None] * o, axis=0)
    return y.reshape(*y.shape[:-2], WIDTH_B_OUT)

def hier_moe(h, w_group, b_group, w_expert, b_expert, w_gate_e, w_up_e, w_down_e):
    n = h.shape[0]
    group_logits = (h @ w_group).astype(jnp.float32) + b_group.astype(jnp.float32)
    group_prob = jax.nn.softmax(group_logits, axis=-1)
    g_sel = jnp.argmax(group_logits, axis=-1)
    p_group = jnp.take_along_axis(group_prob, g_sel[:, None], axis=1)
    expert_logits = ((h @ w_expert).astype(jnp.float32) + b_expert.astype(jnp.float32))
    expert_logits = expert_logits.reshape(n, N_EXPERT_GROUPS, EXPERTS_PER_GROUP)
    in_group = jnp.take_along_axis(expert_logits, g_sel[:, None, None], axis=1)[:, 0]
    top_val, top_idx = lax.top_k(in_group, TOP_K_INNER)
    w_inner = jax.nn.softmax(top_val, axis=-1)
    expert_id = g_sel[:, None] * EXPERTS_PER_GROUP + top_idx
    gates = jnp.sum(jax.nn.one_hot(expert_id, N_EXPERTS, dtype=jnp.float32)
                    * (p_group * w_inner)[..., None], axis=1).astype(h.dtype)
    out = jnp.zeros_like(h)
    for e in range(N_EXPERTS):
        hid = jax.nn.silu(h @ w_gate_e[e]) * (h @ w_up_e[e])
        out = out + gates[:, e:e + 1] * (hid @ w_down_e[e])
    return out

def finish_layer(x, o_a, y_b, gate_a, gate_b, w_br_a, w_br_b, w_o, g_ffn,
                 w_group, b_group, w_expert, b_expert, w_gate_e, w_up_e, w_down_e):
    ya = o_a.reshape(*x.shape[:-1], WIDTH_A).astype(x.dtype) @ w_br_a
    yb = y_b.astype(x.dtype) @ w_br_b
    mixed = jax.nn.sigmoid(gate_a) * ya + jax.nn.sigmoid(gate_b) * yb
    x = x + mixed @ w_o
    h2 = rmsnorm(x, g_ffn).reshape(-1, D_MODEL)
    return x + hier_moe(h2, w_group, b_group, w_expert, b_expert, w_gate_e, w_up_e, w_down_e).reshape(x.shape)

def layer_prompt(x, slopes, g_attn, w_in, b_sb, w_br_a, w_br_b, w_o, g_ffn,
                 w_group, b_group, w_expert, b_expert, w_gate_e, w_up_e, w_down_e):
    s = x.shape[1]
    h = rmsnorm(x, g_attn)
    qa, ka, va, qb, kb, vb, gate_a, gate_b = split_projection(h, w_in)
    o_a = stick_breaking_prompt(qa, ka, va, b_sb)
    outs, lses, bufs = [], [], []
    for g, (window, dil) in enumerate(DILATED_GROUPS):
        o, lse = dilated_group_prompt(qb[:, :, g], kb[:, :, g], vb[:, :, g], window, dil, slopes[g])
        outs.append(o)
        lses.append(lse)
        keep = min(window, s)
        bufs.append(jnp.stack([kb[:, s - keep:, g], vb[:, s - keep:, g]], axis=2))
    y_b = combine_dilated(outs, lses)
    x = finish_layer(x, o_a, y_b, gate_a, gate_b, w_br_a, w_br_b, w_o, g_ffn,
                     w_group, b_group, w_expert, b_expert, w_gate_e, w_up_e, w_down_e)
    return x, ka, va, bufs

def layer_sample(x, cache_k_a, cache_v_a, page_table, bufs_in, slopes, g_attn, w_in, b_sb, w_br_a, w_br_b, w_o,
                 g_ffn, w_group, b_group, w_expert, b_expert, w_gate_e, w_up_e, w_down_e):
    h = rmsnorm(x, g_attn)
    qa, ka, va, qb, kb, vb, gate_a, gate_b = split_projection(h, w_in)
    o_a = stick_breaking_sample(qa, ka, va, cache_k_a, cache_v_a, page_table, b_sb)
    outs, lses, bufs = [], [], []
    for g, (window, dil) in enumerate(DILATED_GROUPS):
        o, lse, nbuf = dilated_group_sample(qb[:, :, g], kb[:, :, g], vb[:, :, g], bufs_in[g], window, dil, slopes[g])
        outs.append(o)
        lses.append(lse)
        bufs.append(nbuf)
    y_b = combine_dilated(outs, lses)
    x = finish_layer(x, o_a, y_b, gate_a, gate_b, w_br_a, w_br_b, w_o, g_ffn,
                     w_group, b_group, w_expert, b_expert, w_gate_e, w_up_e, w_down_e)
    return x, ka, va, bufs

def setup_inputs(seed: int = 0) -> dict:
    key = jax.random.key(seed)
    ks = jax.random.split(key, 24)
    f32 = jnp.float32
    n_pages = PAST_LEN // PAGE_SIZE
    n_used = DEC_BATCH * n_pages
    n_phys = n_used + max(1, n_used // 4)

    def nrm(k, shape, scale=1.0):
        return jax.random.normal(k, shape, f32) * scale

    x_prompt = nrm(ks[0], (BATCH, SEQ, D_MODEL))
    x_sample = nrm(ks[1], (DEC_BATCH, DEC_SEQ, D_MODEL))
    cache_k_a = nrm(ks[2], (DEPTH, n_phys, PAGE_SIZE, N_HEADS_A, HEAD_DIM))
    cache_v_a = nrm(ks[3], (DEPTH, n_phys, PAGE_SIZE, N_HEADS_A, HEAD_DIM))
    page_table = jax.random.permutation(ks[4], n_phys)[:n_used].reshape(DEC_BATCH, n_pages).astype(jnp.int32)
    w0, w1, w2 = (w for w, _ in DILATED_GROUPS)
    cache_kv_b0 = nrm(ks[5], (DEPTH, DEC_BATCH, min(w0, PAST_LEN), 2, HEADS_PER_GROUP_B, HEAD_DIM))
    cache_kv_b1 = nrm(ks[6], (DEPTH, DEC_BATCH, min(w1, PAST_LEN), 2, HEADS_PER_GROUP_B, HEAD_DIM))
    cache_kv_b2 = nrm(ks[7], (DEPTH, DEC_BATCH, min(w2, PAST_LEN), 2, HEADS_PER_GROUP_B, HEAD_DIM))
    g_attn = 1.0 + 0.02 * nrm(ks[8], (DEPTH, D_MODEL))
    w_in = nrm(ks[9], (DEPTH, D_MODEL, IN_WIDTH), D_MODEL ** -0.5)
    b_sb = (jnp.linspace(SB_BIAS_HI, SB_BIAS_LO, N_HEADS_A, dtype=f32)[None, :]
            + 0.1 * nrm(ks[22], (DEPTH, N_HEADS_A)))
    w_br_a = nrm(ks[10], (DEPTH, WIDTH_A, D_MODEL), WIDTH_A ** -0.5)
    w_br_b = nrm(ks[11], (DEPTH, WIDTH_B_OUT, D_MODEL), WIDTH_B_OUT ** -0.5)
    w_o = nrm(ks[12], (DEPTH, D_MODEL, D_MODEL), D_MODEL ** -0.5)
    g_ffn = 1.0 + 0.02 * nrm(ks[13], (DEPTH, D_MODEL))
    w_group = nrm(ks[14], (DEPTH, D_MODEL, N_EXPERT_GROUPS), D_MODEL ** -0.5)
    b_group = nrm(ks[15], (DEPTH, N_EXPERT_GROUPS), 0.01)
    w_expert = nrm(ks[16], (DEPTH, D_MODEL, N_EXPERTS), D_MODEL ** -0.5)
    b_expert = nrm(ks[17], (DEPTH, N_EXPERTS), 0.01)
    w_gate_e = nrm(ks[18], (DEPTH, N_EXPERTS, D_MODEL, D_EXPERT), D_MODEL ** -0.5)
    w_up_e = nrm(ks[19], (DEPTH, N_EXPERTS, D_MODEL, D_EXPERT), D_MODEL ** -0.5)
    w_down_e = nrm(ks[20], (DEPTH, N_EXPERTS, D_EXPERT, D_MODEL), D_EXPERT ** -0.5)
    g_final = 1.0 + 0.02 * nrm(ks[21], (D_MODEL,))
    return {"x_prompt": x_prompt, "x_sample": x_sample, "cache_k_a": cache_k_a, "cache_v_a": cache_v_a,
            "page_table": page_table, "cache_kv_b0": cache_kv_b0, "cache_kv_b1": cache_kv_b1,
            "cache_kv_b2": cache_kv_b2, "g_attn": g_attn, "w_in": w_in, "b_sb": b_sb, "w_br_a": w_br_a,
            "w_br_b": w_br_b, "w_o": w_o, "g_ffn": g_ffn, "w_group": w_group, "b_group": b_group,
            "w_expert": w_expert, "b_expert": b_expert, "w_gate_e": w_gate_e, "w_up_e": w_up_e,
            "w_down_e": w_down_e, "g_final": g_final}

def reference(x_prompt, x_sample, cache_k_a, cache_v_a, page_table, cache_kv_b0, cache_kv_b1, cache_kv_b2,
              g_attn, w_in, b_sb, w_br_a, w_br_b, w_o, g_ffn, w_group, b_group, w_expert, b_expert,
              w_gate_e, w_up_e, w_down_e, g_final):
    slopes = alibi_slopes()
    xp, xs = x_prompt, x_sample
    ka_p, va_p, ka_s, va_s = [], [], [], []
    bp = [[] for _ in range(N_GROUPS_B)]
    bs = [[] for _ in range(N_GROUPS_B)]
    for layer in range(DEPTH):
        lw = (g_attn[layer], w_in[layer], b_sb[layer], w_br_a[layer], w_br_b[layer], w_o[layer], g_ffn[layer],
              w_group[layer], b_group[layer], w_expert[layer], b_expert[layer],
              w_gate_e[layer], w_up_e[layer], w_down_e[layer])
        xp, k_new, v_new, bufs = layer_prompt(xp, slopes, *lw)
        ka_p.append(k_new)
        va_p.append(v_new)
        for g in range(N_GROUPS_B):
            bp[g].append(bufs[g])
        bufs_in = (cache_kv_b0[layer], cache_kv_b1[layer], cache_kv_b2[layer])
        xs, k_new, v_new, bufs = layer_sample(xs, cache_k_a[layer], cache_v_a[layer], page_table, bufs_in, slopes, *lw)
        ka_s.append(k_new)
        va_s.append(v_new)
        for g in range(N_GROUPS_B):
            bs[g].append(bufs[g])
    y_prompt = rmsnorm(xp, g_final)
    y_sample = rmsnorm(xs, g_final)
    return (y_prompt, y_sample,
            jnp.stack(ka_p), jnp.stack(va_p), jnp.stack(ka_s), jnp.stack(va_s),
            jnp.stack(bp[0]), jnp.stack(bp[1]), jnp.stack(bp[2]),
            jnp.stack(bs[0]), jnp.stack(bs[1]), jnp.stack(bs[2]))


_drawn_inputs = setup_inputs


def setup_inputs(seed=0):
    import zlib

    import numpy as np

    out = dict(_drawn_inputs(seed))
    spreads = {}
    factors = {'g_attn': 2.94, 'b_group': 36.88, 'b_expert': 19.503, 'g_final': 7.513, 'g_ffn': 4.002}
    for name, (base, spread) in spreads.items():
        noise = np.random.default_rng([zlib.crc32(name.encode()), seed]).standard_normal(out[name].shape)
        drawn = base * np.exp(spread * noise) if base else spread * noise
        out[name] = __import__('jax').numpy.asarray(drawn.astype(out[name].dtype))
    for name, factor in factors.items():
        out[name] = (out[name] * factor).astype(out[name].dtype)
    return out
```

```python
from contextlib import ExitStack

import numpy as np

import concourse.bass as bass
from concourse import mybir

F32 = mybir.dt.float32
I32 = mybir.dt.int32
U32 = mybir.dt.uint32
ALU = mybir.AluOpType
ACT = mybir.ActivationFunctionType
AX = mybir.AxisListType.X

P = 128
D = 1024
KC = D // P
SEQ = 512
NB = SEQ // P
DEC = 8
TOK = SEQ + DEC
HD = 64
HA = 8
WA = HA * HD
SLOTS_B = 4
GROUPS = ((128, 1), (512, 4), (2048, 16))
NG = len(GROUPS)
HB = NG * SLOTS_B
WB = HB * HD
WBO = SLOTS_B * HD
PAGES = 32
PPG = 4
RING = 4
TILES = (3 * WA + 3 * WB) // P
QK_TILES = 2 * (WA + WB) // P
SCALE = HD ** -0.5
EPS = 1e-6
CLAMP = 30.0
EXPERTS = 32
E_GROUPS = 4
E_PER = EXPERTS // E_GROUPS
FF = 512
SLOT = 64
MORE = 16
ALL_SLOTS = EXPERTS + MORE
NONE = 1 << 20
FAR = 1e30
OPEN = 1
NBLK = NB + 1

SLOPES = [[2.0 ** (-8.0 * (g * SLOTS_B + s + 1) / HB) for s in range(SLOTS_B)] for g in range(NG)]


def constants():
    p = np.arange(P)[:, None]
    f = np.arange(P)[None, :]
    u = np.arange(SEQ)[None, :]
    rel = p - u + (SEQ - P)
    t = np.arange(NBLK)[None, :] * P + p
    parts = {
        "ident": (p == f),
        "later_eq": (p >= f),
        "before": (p < f),
        "ones": np.ones((P, P)),
        "own_head": (np.arange(WA)[None, :] // HD == p),
        "rel": np.concatenate([
            np.where((rel >= 0) & (rel <= w) & (rel % d == 0), rel, FAR) if d > 1 else
            np.where((rel >= 0) & (rel <= w), rel, FAR) for w, d in GROUPS], axis=1),
        "slope": np.broadcast_to(-np.array(SLOPES).reshape(1, HB) / SCALE, (P, HB)),
        "row_bias": np.concatenate([-np.array(SLOPES[g])[None, :] * d * (P - p)
                                    for g, (_, d) in enumerate(GROUPS)], axis=1),
        "own_sample": (p // SLOTS_B == np.arange(DEC)[None, :]),
        "iota": np.broadcast_to(np.arange(SLOT)[None, :], (P, SLOT)),
        "steps": np.broadcast_to(SLOT * (np.arange(TOK // SLOT)[None, :] + 1), (P, TOK // SLOT)),
        "pair0": (2 * t + 1) * (t < TOK),
        "pair1": (2 * t + 2) * (t < TOK),
        "token": (t + 1) * (t < TOK),
        "real": (t < TOK),
        "eps": np.full((P, 1), EPS),
    }
    at, cols, n = {}, [], 0
    for name, a in parts.items():
        a = np.asarray(a, np.float32)
        at[name] = (n, n + a.shape[1])
        n += a.shape[1]
        cols.append(a)
    return at, np.ascontiguousarray(np.concatenate(cols, axis=1))


class Chain:

    def __init__(self, eng, sem):
        self.eng, self.sem, self.base, self.k = eng, sem, 0, 0

    def __call__(self, ins):
        self.k += 1
        ins.then_inc(self.sem, 1)
        self.eng.wait_ge(self.sem, self.base + self.k)

    def enter(self, i, per):
        self.before = self.base + self.k
        self.base, self.k = self.before + i * per, 0

    def leave(self, per, trips):
        assert self.k == per, (self.k, per)
        self.base, self.k = self.before + per * trips, 0


class Kernel:

    def __init__(self, nc, ctx, io, at):
        self.nc, self.ctx, self.io, self.at, self.sems = nc, ctx, io, at, []

    def sb(self, name, shape, dt=F32, ctx=None):
        return (ctx or self.ctx).enter_context(self.nc.sbuf_tensor(name, shape, dt))

    def ps(self, name, shape, ctx):
        return ctx.enter_context(self.nc.psum_tensor(name, shape, F32))

    def sem(self, name, ctx):
        sem = ctx.enter_context(self.nc.semaphore(name))
        self.sems.append(sem)
        return sem

    def pool_sem(self, name):
        return self.ctx.enter_context(self.nc.semaphore(name))

    def clear_semaphores(self):
        with self.nc.Block() as block:

            @block.gpsimd
            def _(pool):
                for sem in self.sems:
                    pool.sem_clear(sem)
        self.sems = []

    def const(self, name, rows=P):
        a, b = self.at[name]
        return self.consts[0:rows, a:b]


def rows_of(blk):
    return P if blk < NB else DEC


def x_rows(k, blk):
    return k.io["x_prompt"][0, blk * P:(blk + 1) * P, :] if blk < NB else k.io["x_sample"][:, 0, :]


def prepare(k):
    nc = k.nc
    with ExitStack() as ctx:
        x = k.sb("prep_x", [P, NBLK, D], ctx=ctx)
        junk = k.sb("prep_junk", [P, D], ctx=ctx)
        ms = k.sb("prep_ms", [P, NBLK], ctx=ctx)
        rms = k.sb("prep_rms", [P, NBLK], ctx=ctx)
        rstd = k.sb("prep_rstd", [P, NBLK], ctx=ctx)
        tr = k.ps("prep_tr", [P, 2, KC, P], ctx)
        consts_in = k.pool_sem("consts_in")
        x_in = [k.sem(f"x_in{b}", ctx) for b in range(NBLK)]
        squares = k.sem("squares", ctx)
        roots = k.sem("roots", ctx)
        scaled = k.sem("scaled", ctx)
        turned = k.sem("turned", ctx)
        placed = k.sem("placed", ctx)
        own = k.sem("prep_dve", ctx)
        with nc.Block() as block:

            @block.sync
            def _(sp):
                for b in range(NBLK):
                    sp.dma_start(x[0:rows_of(b), b, :], x_rows(k, b)).then_inc(x_in[b], 16)

            @block.gpsimd
            def _(pool):
                pool.dma_start(k.consts[:], k.io["consts"]).then_inc(consts_in, 16)
                pool.dma_start(k.g_attn[:], k.io["g_attn"][0].rearrange("(p c) -> p c", c=KC)).then_inc(consts_in, 16)
                pool.dma_start(k.g_ffn[:], k.io["g_ffn"][0].rearrange("(p c) -> p c", c=KC)).then_inc(consts_in, 16)
                pool.dma_start(k.b_sb[:], k.io["b_sb"][0].partition_broadcast(P)).then_inc(consts_in, 16)
                pool.dma_start(k.pages[:], k.io["page_table"].rearrange("b n -> (b n)").unsqueeze(0))\
                    .then_inc(consts_in, 16)
                pool.wait_ge(consts_in, 80)

            @block.scalar
            def _(act):
                for b in range(NBLK):
                    r = rows_of(b)
                    act.wait_ge(x_in[b], 16)
                    act.activation(junk[0:r, :], x[0:r, b, :], ACT.Square,
                                   accum_out=ms[0:r, b:b + 1]).then_inc(squares, 1)
                    act.wait_ge(squares, b + 1)
                act.wait_ge(consts_in, 80)
                for b in range(NBLK):
                    r = rows_of(b)
                    act.activation(rms[0:r, b:b + 1], ms[0:r, b:b + 1], ACT.Sqrt,
                                   bias=k.const("eps", r), scale=1.0 / D).then_inc(roots, 1)

            @block.vector
            def _(dve):
                link = Chain(dve, own)
                for b in range(NBLK):
                    r = rows_of(b)
                    dve.wait_ge(roots, b + 1)
                    link(dve.reciprocal(rstd[0:r, b:b + 1], rms[0:r, b:b + 1]))
                    dve.tensor_scalar(x[0:r, b, :], x[0:r, b, :], rstd[0:r, b:b + 1], None,
                                      ALU.mult).then_inc(scaled, 1)
                dve.wait_ge(consts_in, 80)
                for b in range(NBLK):
                    r = rows_of(b)
                    dve.wait_ge(turned, b + 1)
                    dve.tensor_tensor(k.hT[:, :, b * P:b * P + r], tr[:, b % 2, :, 0:r],
                                      k.g_attn[:].unsqueeze(2).to_broadcast([P, KC, r]),
                                      ALU.mult).then_inc(placed, 1)
                dve.wait_ge(placed, NBLK)

            @block.tensor
            def _(pe):
                pe.wait_ge(consts_in, 80)
                for b in range(NBLK):
                    r = rows_of(b)
                    pe.wait_ge(scaled, b + 1)
                    if b >= 2:
                        pe.wait_ge(placed, b - 1)
                    v = x[0:r, b, :].rearrange("t (p c) -> t c p", c=KC)
                    for c in range(KC):
                        last = pe.transpose(tr[:, b % 2, c, 0:r], v[:, c, :], k.const("ident", r)[:, 0:r])
                    last.then_inc(turned, 1)


def page_loads(k, sp, cache, ring_in, ring_used, fills):
    with sp.Fori(0, DEC) as b:
        for g in range(PAGES // PPG):
            s, n = g % RING, fills + g // RING
            sp.wait_ge(ring_used[s], b * 2 + n + OPEN)
            for j in range(PPG):
                page = sp.value_load(k.pages[0:1, bass.ds(b * PAGES + (g * PPG + j), 1)],
                                     min_val=0, max_val=cache.shape[1] - 1)
                sp.dma_start(k.ring[:, s, PPG - 1 - j, :],
                             cache[0, bass.ds(page, 1)].rearrange("a p h d -> (a p) (h d)"))\
                    .then_inc(ring_in[s], 16)


def project(k):
    nc = k.nc
    with ExitStack() as ctx:
        w = k.sb("w_slot", [P, 2, KC, P], ctx=ctx)
        stage = k.sb("stage", [P, 2, TOK], ctx=ctx)
        krows = k.sb("k_rows", [P, NB, WB], ctx=ctx)
        qrep = k.sb("q_rep", [P, DEC, WA], ctx=ctx)
        prod = k.sb("prod", [P, PPG, WA], ctx=ctx)
        pp = k.ps("proj_ps", [P, 2, 2, 512], ctx)
        tp = k.ps("turn_ps", [P, 2, 512], ctx)
        ts = k.ps("turn_sample_ps", [P, 2, 512], ctx)
        rp = tp[:, 0, :]
        w_in = [k.sem(f"w_in{j}", ctx) for j in range(2)]
        made = [k.sem(f"made{j}", ctx) for j in range(2)]
        staged = [k.sem(f"staged{j}", ctx) for j in range(2)]
        turned = [k.sem(f"q_turned{j}", ctx) for j in range(2)]
        laid = [k.sem(f"laid{j}", ctx) for j in range(2)]
        kept = [k.sem(f"kept{j}", ctx) for j in range(2)]
        k_out = k.sem("k_out", ctx)
        v_out = k.sem("v_out", ctx)
        rep = k.sem("rep", ctx)
        rep_laid = k.sem("rep_laid", ctx)
        ring_in = [k.sem(f"k_ring_in{s}", ctx) for s in range(RING)]
        ring_used = [k.sem(f"k_ring_used{s}", ctx) for s in range(RING)]
        own = k.sem("proj_dve", ctx)
        H = TOK // 2
        io = k.io
        secs = [(0, 4, None, 0), (4, 4, "k", 1), (8, 4, "v", 2), (12, 6, None, 0), (18, 6, "k", 1), (24, 6, "v", 2)]

        def tiles_loop(eng, t0, n, body):
            with eng.Fori(0, n // 2) as i:
                body(i + t0 // 2, i)

        with nc.Block() as block:

            @block.sync
            def _(sp):
                page_loads(k, sp, io["cache_k_a"], ring_in, ring_used, 0)

            @block.scalar
            def _(act):
                for sem in (*staged, *laid,):
                    act.sem_inc(sem, OPEN)
                def load(m, j):
                    act.dma_start(w[:, j], io["w_in"][0].rearrange("(p c) n -> p c n", c=KC)[
                        :, :, bass.ds(m * (2 * P) + j * P, P)]).then_inc(w_in[j], 16)

                for j in range(2):
                    load(0, j)
                for t0, n, what, kind in secs:
                    wide = n * P
                    if what == "k":
                        rows = krows[:, :, 0:wide]
                        if t0 > 4:
                            act.wait_ge(k_out, 16)
                    elif what == "v":
                        rows = k.v_rows[:, :, 0:WA] if wide == WA else k.v_rows[:, :, WA:WA + WB]

                    def body(m, i, last=False):
                        for j in range(2):
                            act.wait_ge(made[j], m + 1)
                            if not last:
                                load(m + 1, j)
                            act.wait_ge(turned[j], m + OPEN)
                            act.wait_ge(kept[j], m + OPEN)
                            act.activation(stage[:, j, :].rearrange("p (a n) -> p a n", a=2), pp[:, j, :, 0:H],
                                           ACT.Copy).then_inc(staged[j], 1)
                        for j in range(2):
                            act.wait_ge(turned[j], m + 1 + OPEN)
                            if what:
                                act.activation(rows[:, :, bass.ds(i * (2 * P) + j * P, P)],
                                               tp[:, j, :].rearrange("p (b n) -> p b n", b=NB),
                                               ACT.Copy).then_inc(laid[j], 1)
                            else:
                                act.sem_inc(laid[j], 1)
                            act.activation(k.samp[0:DEC, bass.ds(m * (2 * P) + j * P, P)],
                                           ts[0:DEC, j, 0:P], ACT.Copy).then_inc(laid[j], 1)

                    final = t0 + n == TILES
                    tiles_loop(act, t0, n - 2 * final, body)
                    if final:
                        body(TILES // 2 - 1, n // 2 - 1, last=True)
                    for j in range(2):
                        act.wait_ge(laid[j], t0 + n + OPEN)
                    if what == "k":
                        if wide == WA:
                            act.dma_start(io["o_ka"].rearrange("(b p) n -> p b n", p=P), rows).then_inc(k_out, 16)
                        else:
                            for g in range(NG):
                                keep = min(GROUPS[g][0], SEQ) // P
                                act.dma_start(io[f"o_kvp{g}"][:, 0:WBO].rearrange("(b p) n -> p b n", p=P),
                                              rows[:, NB - keep:NB, g * WBO:(g + 1) * WBO]).then_inc(k_out, 16)
                    elif what == "v":
                        if wide == WA:
                            act.dma_start(io["o_va"].rearrange("(b p) n -> p b n", p=P), rows).then_inc(v_out, 16)
                        else:
                            for g in range(NG):
                                keep = min(GROUPS[g][0], SEQ) // P
                                act.dma_start(io[f"o_kvp{g}"][:, WBO:2 * WBO].rearrange("(b p) n -> p b n", p=P),
                                              rows[:, NB - keep:NB, g * WBO:(g + 1) * WBO]).then_inc(v_out, 16)
                    if t0 == 0:
                        for b in range(DEC):
                            act.wait_ge(rep, b + 1)
                            act.activation(qrep[:, b, :], rp, ACT.Copy).then_inc(rep_laid, 1)
                act.dma_start(io["o_kas"], k.samp[0:DEC, WA:2 * WA]).then_inc(k_out, 16)
                act.dma_start(io["o_vas"], k.samp[0:DEC, 2 * WA:3 * WA]).then_inc(v_out, 16)
                for g, (wlen, _) in enumerate(GROUPS):
                    for c, s in ((0, k_out), (1, v_out)):
                        at = 3 * WA + (1 + c) * WB + g * WBO
                        act.dma_start(io[f"o_kvs{g}"][:, wlen - 1, c * WBO:(c + 1) * WBO],
                                      k.samp[0:DEC, at:at + WBO]).then_inc(s, 16)
                act.wait_ge(k_out, 16 * (2 + 2 * NG))
                act.wait_ge(v_out, 16 * (2 + 2 * NG))

            @block.gpsimd
            def _(pool):
                for sem in (*kept,):
                    pool.sem_inc(sem, OPEN)
                for g, (wlen, _) in enumerate(GROUPS):
                    pool.dma_start(io[f"o_kvs{g}"][:, 0:wlen - 1, :],
                                   io[f"cache_kv_b{g}"][0].rearrange("b w k h d -> b w (k h d)")[:, 1:wlen, :])\
                        .then_inc(k.shifted, 16)
                at = 0
                for t0, n, what, kind in secs:
                    def body(m, i):
                        for j in range(2):
                            pool.wait_ge(staged[j], m + 1 + OPEN)
                            if what == "v":
                                pool.sem_inc(kept[j], 1)
                            else:
                                pool.tensor_copy(k.qk[:, bass.ds(i * 2 + (at + j), 1), :].rearrange(
                                    "p a n -> p (a n)"), stage[:, j, 0:SEQ]).then_inc(kept[j], 1)
                    tiles_loop(pool, t0, n, body)
                    if what != "v":
                        at += n

            @block.tensor
            def _(pe):
                for sem in (*turned,):
                    pe.sem_inc(sem, OPEN)
                for t0, n, what, kind in secs:
                    def body(m, i):
                        for j in range(2):
                            pe.wait_ge(w_in[j], (m + 1) * 16)
                            pe.wait_ge(staged[j], m + OPEN)
                            for half in range(2):
                                for c in range(KC):
                                    last = pe.matmul(pp[:, j, half, 0:H], w[:, j, c, :],
                                                     k.hT[:, c, half * H:(half + 1) * H],
                                                     start=(c == 0), stop=(c == KC - 1))
                            last.then_inc(made[j], 1)
                        for j in range(2):
                            pe.wait_ge(staged[j], m + 1 + OPEN)
                            pe.wait_ge(laid[j], m * 2 + OPEN)
                            if what:
                                for b in range(NB):
                                    pe.transpose(tp[:, j, b * P:(b + 1) * P], stage[:, j, b * P:(b + 1) * P],
                                                 k.const("ident"))
                            pe.transpose(ts[0:DEC, j, 0:P], stage[:, j, SEQ:TOK],
                                         k.const("ident")).then_inc(turned[j], 1)
                    tiles_loop(pe, t0, n, body)
                    if t0 == 0:
                        for j in range(2):
                            pe.wait_ge(laid[j], n + OPEN)
                        for b in range(DEC):
                            if b:
                                pe.wait_ge(rep_laid, b)
                            pe.matmul(rp, k.const("ident", DEC)[:, b:b + 1].to_broadcast([DEC, P]),
                                      k.samp[0:DEC, 0:WA], start=True, stop=True).then_inc(rep, 1)
                        pe.wait_ge(rep_laid, DEC)

            @block.vector
            def _(dve):
                for sem in (*ring_used,):
                    dve.sem_inc(sem, OPEN)
                link = Chain(dve, own)
                dve.wait_ge(rep_laid, DEC)
                per = PAGES // PPG
                with dve.Fori(0, DEC) as b:
                    link.enter(b, per)
                    for g in range(per):
                        s = g % RING
                        dve.wait_ge(ring_in[s], b * (32 * PPG) + 16 * PPG * (g // RING + 1))
                        link_ready = dve.tensor_tensor(
                            prod[:, :, :], k.ring[:, s, :, :],
                            qrep[:, bass.ds(b, 1), :].to_broadcast([P, PPG, WA]), ALU.mult)
                        link_ready.then_inc(ring_used[s], 1)
                        dve.wait_ge(ring_used[s], b * 2 + (g // RING + 1) + OPEN)
                        at = PAGES - PPG * (g + 1)
                        link(dve.tensor_reduce(
                            k.scores[:, bass.ds(b, 1), :, at:at + PPG].rearrange("p a h j -> p j (a h)"),
                            prod[:, :, :].rearrange("p j (h d) -> p j h d", d=HD), axis=AX, op=ALU.add))
                    link.leave(per, DEC)


def weigh_a(k):
    nc = k.nc
    N = DEC * HA * PAGES
    with ExitStack() as ctx:
        t = k.sb("wa_t", [P, N], ctx=ctx)
        later = k.sb("wa_later", [P, DEC * HA, PAGES], ctx=ctx)
        keep = k.sb("wa_keep", [P, DEC * HA, PAGES], ctx=ctx)
        within = k.ps("wa_within", [P, N], ctx)
        totals = k.ps("wa_totals", [P, N], ctx)
        own = k.sem("wa_dve", ctx)
        clamped = k.sem("wa_clamped", ctx)
        exped = k.sem("wa_exped", ctx)
        logged = k.sem("wa_logged", ctx)
        soft = k.sem("wa_soft", ctx)
        summed = k.sem("wa_summed", ctx)
        arg = k.sem("wa_arg", ctx)
        weighed = k.sem("wa_weighed", ctx)
        z = k.scores[:].rearrange("p b h n -> p (b h n)")
        zv = k.scores[:].rearrange("p b h n -> p b h n")
        with nc.Block() as block:

            @block.vector
            def _(dve):
                link = Chain(dve, own)
                bias = k.b_sb[:].unsqueeze(2).to_broadcast([P, HA, PAGES])
                for b in range(DEC):
                    last = dve.scalar_tensor_tensor(zv[:, b], zv[:, b], SCALE, bias, ALU.mult, ALU.add)
                link(last)
                dve.tensor_scalar(t[:], z, CLAMP, None, ALU.min).then_inc(clamped, 1)
                link(dve.memset(keep[:], 1.0))
                link(dve.memset(keep[:, :, 0:1], 0.0))
                link(dve.memset(later[:, :, 0:1], 0.0))
                dve.wait_ge(logged, 1)
                dve.tensor_tensor(t[:], z, t[:], ALU.max).then_inc(soft, 1)
                dve.wait_ge(summed, 2)
                link(dve.tensor_copy(later[:, :, 1:PAGES],
                                     totals[:].rearrange("p (a n) -> p a n", n=PAGES)[:, :, 0:PAGES - 1]))
                lf = later[:].rearrange("p a n -> p (a n)")
                link(dve.tensor_tensor_scan(lf, keep[:].rearrange("p a n -> p (a n)"), lf, 0.0, ALU.mult, ALU.add))
                link(dve.tensor_tensor(z, z, within[:], ALU.subtract))
                dve.tensor_tensor(z, z, lf, ALU.subtract).then_inc(arg, 1)

            @block.scalar
            def _(act):
                act.wait_ge(clamped, 1)
                act.activation(t[:], t[:], ACT.Exp).then_inc(exped, 1)
                act.wait_ge(exped, 1)
                act.activation(t[:], t[:], ACT.Ln, bias=k.const("ones")[:, 0:1]).then_inc(logged, 1)
                act.wait_ge(arg, 1)
                act.activation(z, z, ACT.Exp).then_inc(weighed, 1)
                act.wait_ge(weighed, 1)

            @block.tensor
            def _(pe):
                pe.wait_ge(soft, 1)
                for out, table in ((within, "later_eq"), (totals, "ones")):
                    for c in range(N // 512):
                        last = pe.matmul(out[:, c * 512:(c + 1) * 512], k.const(table), t[:, c * 512:(c + 1) * 512],
                                         start=True, stop=True)
                    last.then_inc(summed, 1)


def attend_a(k):
    nc = k.nc
    OFF = {0: 0, 1: SEQ, 3: SEQ + 3 * P, 2: 2 * SEQ}
    W = 2 * SEQ + 2 * P
    GPS = PAGES // PPG
    with ExitStack() as ctx:
        qs = k.sb("aa_q", [HD, 2, SEQ], ctx=ctx)
        ks = k.sb("aa_k", [HD, 2, SEQ], ctx=ctx)
        vs = k.sb("aa_v", [P, 2, NB, HD], ctx=ctx)
        z = k.sb("aa_z", [P, 2, W], ctx=ctx)
        sp_ = k.sb("aa_soft", [P, 2, W], ctx=ctx)
        a = k.sb("aa_a", [P, 2, W], ctx=ctx)
        w_cur = k.sb("aa_w", [P, 2, PAGES, HA], ctx=ctx)
        om = k.sb("aa_own", [HA, WA], ctx=ctx)
        zp = k.ps("aa_zp", [P, 2, 3 * SEQ], ctx)
        op = k.ps("aa_op", [P, SEQ], ctx)
        vp = k.ps("aa_vp", [P, WA], ctx)
        s = {n: k.sem("aa_" + n, ctx) for n in (
            "staged", "scored", "z_kept", "clamped", "exped", "logged", "soft", "masked", "summed", "arg_done",
            "exp_a", "a_masked", "o_made", "o_kept", "w_laid", "own_kept", "col_made", "col_kept")}
        own = k.sem("aa_pool", ctx)
        ring_in = [k.sem(f"v_ring_in{n}", ctx) for n in range(RING)]
        ring_used = [k.sem(f"v_ring_used{n}", ctx) for n in range(RING)]
        TRIPS = HA // 2
        with nc.Block() as block:

            @block.sync
            def _(sp):
                page_loads(k, sp, k.io["cache_v_a"], ring_in, ring_used, 0)

            @block.gpsimd
            def _(pool):
                link = Chain(pool, own)

                def stage(i, j, n):
                    if n is not None:
                        pool.wait_ge(s["o_made"], n + OPEN)
                    rows = slice(j * HD, (j + 1) * HD)
                    link(pool.tensor_copy(qs[:, j, :], k.qk[rows, bass.ds(i, 1), :].rearrange("p a n -> p (a n)")))
                    link(pool.tensor_copy(ks[:, j, :], k.qk[rows, bass.ds(i + HA // 2, 1), :].rearrange(
                        "p a n -> p (a n)")))
                    link(pool.tensor_copy(vs[:, j], k.v_rows[:, :, bass.ds(i * P + j * HD, HD)]))
                    pool.sem_inc(s["staged"], 1)

                stage(0, 0, None)
                with pool.Fori(0, TRIPS) as i:
                    link.enter(i, 6)
                    for j in range(2):
                        h = i * 2 + j
                        stage(i + j, 1 - j, h)
                        pool.wait_ge(s["soft"], h + 1)
                        for kb in range(NB):
                            d = sp_[:, j, OFF[kb]:OFF[kb] + P]
                            last = pool.tensor_tensor(d, d, k.const("before"), ALU.mult)
                        last.then_inc(s["masked"], 1)
                        pool.wait_ge(s["exp_a"], h + 1)
                        for kb in range(NB):
                            d = a[:, j, OFF[kb]:OFF[kb] + P]
                            last = pool.tensor_tensor(d, d, k.const("before"), ALU.mult)
                        last.then_inc(s["a_masked"], 1)
                        pool.wait_ge(s["a_masked"], h + 1)
                    link.leave(6, TRIPS)

            @block.vector
            def _(dve):
                for sem in (s["arg_done"], s["own_kept"],):
                    dve.sem_inc(sem, OPEN)
                with dve.Fori(0, TRIPS) as i:
                    for j in range(2):
                        h = i * 2 + j
                        dve.wait_ge(s["scored"], h + 1)
                        dve.tensor_scalar(z[:, j], zp[:, j, 0:W], SCALE, k.b_sb[:, bass.ds(h, 1)],
                                          ALU.mult, ALU.add).then_inc(s["z_kept"], 1)
                        dve.wait_ge(s["z_kept"], h + 1)
                        dve.tensor_scalar(sp_[:, j], z[:, j], CLAMP, None, ALU.min).then_inc(s["clamped"], 1)
                        dve.wait_ge(s["logged"], h + 1)
                        dve.tensor_tensor(sp_[:, j], z[:, j], sp_[:, j], ALU.max).then_inc(s["soft"], 1)
                        dve.wait_ge(s["summed"], h + 1)
                        dve.wait_ge(s["o_made"], i * 2 + OPEN)
                        dve.tensor_tensor(a[:, j], z[:, j], zp[:, j, 0:W], ALU.subtract).then_inc(s["arg_done"], 1)
                        dve.wait_ge(ring_used[(GPS - 1) % RING], h * 2 + 2 + OPEN)
                        dve.wait_ge(s["col_made"], h + OPEN)
                        dve.tensor_tensor(om[:], vp[0:HA, :], k.const("own_head", HA), ALU.mult)\
                            .then_inc(s["own_kept"], 1)

            @block.scalar
            def _(act):
                for sem in (s["col_kept"],):
                    act.sem_inc(sem, OPEN)
                with act.Fori(0, TRIPS) as i:
                    for j in range(2):
                        h = i * 2 + j
                        act.activation(w_cur[:, j].rearrange("p n h -> p h n"),
                                       k.scores[:, bass.ds(h, 1)].rearrange("p a h n -> p (a h) n"),
                                       ACT.Copy).then_inc(s["w_laid"], 1)
                        act.wait_ge(s["clamped"], h + 1)
                        act.activation(sp_[:, j], sp_[:, j], ACT.Exp).then_inc(s["exped"], 1)
                        act.wait_ge(s["exped"], h + 1)
                        act.activation(sp_[:, j], sp_[:, j], ACT.Ln, bias=k.const("ones")[:, 0:1])\
                            .then_inc(s["logged"], 1)
                        act.wait_ge(s["arg_done"], h + 1 + OPEN)
                        act.activation(a[:, j], a[:, j], ACT.Exp).then_inc(s["exp_a"], 1)
                        act.wait_ge(s["o_made"], h + 1 + OPEN)
                        rows = slice(j * HD, (j + 1) * HD)
                        act.activation(k.oT[rows, bass.ds(i, 1), 0:SEQ].rearrange("p a n -> p (a n)"), op[rows, :],
                                       ACT.Copy).then_inc(s["o_kept"], 1)
                        act.wait_ge(s["col_made"], h + 1 + OPEN)
                        act.activation(k.oT[:, 0:WA // P, bass.ds(h + SEQ, 1)].rearrange("p c a -> p (c a)"),
                                       op[:, 0:WA // P], ACT.Copy).then_inc(s["col_kept"], 1)
                act.wait_ge(s["col_kept"], HA + OPEN)

            @block.tensor
            def _(pe):
                for sem in (*ring_used, s["o_made"], s["col_made"],):
                    pe.sem_inc(sem, OPEN)
                with pe.Fori(0, TRIPS) as i:
                    for j in range(2):
                        h = i * 2 + j

                        def values(groups):
                            for g in groups:
                                pe.wait_ge(ring_in[g % RING], h * (32 * PPG) + 16 * PPG * (g // RING + 1))
                                for n in range(PPG):
                                    page = PAGES - PPG * (g + 1) + n
                                    last = pe.matmul(vp[0:HA, :], w_cur[:, j, page, :], k.ring[:, g % RING, n, :],
                                                     start=(g == 0 and n == 0), stop=(g == GPS - 1 and n == PPG - 1))
                                last.then_inc(ring_used[g % RING], 1)

                        pe.wait_ge(s["staged"], h + 1)
                        pe.wait_ge(s["arg_done"], (h if j == 0 else h - 1) + OPEN)
                        for kb in range(NB):
                            n = SEQ - kb * P
                            last = pe.matmul(zp[:, j, OFF[kb]:OFF[kb] + n], ks[:, j, kb * P:(kb + 1) * P],
                                             qs[:, j, kb * P:SEQ], start=True, stop=True)
                        last.then_inc(s["scored"], 1)
                        pe.wait_ge(s["w_laid"], h + 1)
                        pe.wait_ge(s["own_kept"], h + OPEN)
                        values(range(GPS // 2))
                        pe.wait_ge(s["masked"], h + 1)
                        for kb in range(NB):
                            for kb2 in range(kb, NB):
                                n, at = SEQ - kb2 * P, OFF[kb] + (kb2 - kb) * P
                                last = pe.matmul(zp[:, j, at:at + n], k.const("later_eq" if kb2 == kb else "ones"),
                                                 sp_[:, j, OFF[kb2]:OFF[kb2] + n], start=(kb2 == kb),
                                                 stop=(kb2 == NB - 1), skip_group_check=True)
                        last.then_inc(s["summed"], 1)
                        values(range(GPS // 2, GPS - 1))
                        pe.wait_ge(s["a_masked"], h + 1)
                        pe.wait_ge(s["col_kept"], h + OPEN)
                        for kb in range(NB):
                            last = pe.matmul(op[j * HD:(j + 1) * HD, kb * P:SEQ], vs[:, j, kb, :],
                                             a[:, j, OFF[kb]:OFF[kb] + SEQ - kb * P], start=(kb == 0),
                                             stop=(kb == NB - 1), skip_group_check=True)
                        last.then_inc(s["o_made"], 1)
                        values(range(GPS - 1, GPS))
                        pe.wait_ge(s["own_kept"], h + 1 + OPEN)
                        pe.wait_ge(s["o_kept"], h + 1)
                        for c in range(WA // P):
                            last = pe.matmul(op[:, c:c + 1], om[:, c * P:(c + 1) * P], k.const("ones", HA)[:, 0:1],
                                             start=True, stop=True)
                        last.then_inc(s["col_made"], 1)


def attend_b(k):
    nc = k.nc
    FIRST = [lambda qb: max(qb - 1, 0), lambda qb: 0, lambda qb: 0]
    WMAX = (2 + 2 * NB) * P
    with ExitStack() as ctx:
        qs = k.sb("ab_q", [HD, 2, NG, SEQ], ctx=ctx)
        ks = k.sb("ab_k", [HD, 2, NG, SEQ], ctx=ctx)
        sc = k.sb("ab_sc", [P, 2, WMAX], ctx=ctx)
        pt = k.sb("ab_pt", [P, WMAX], ctx=ctx)
        y = k.sb("ab_y", [P, NB, WBO], ctx=ctx)
        mx = k.sb("ab_mx", [P, 4], ctx=ctx)
        nm = k.sb("ab_nm", [P, 2], ctx=ctx)
        den = k.sb("ab_den", [P, 2], ctx=ctx)
        rd = k.sb("ab_rd", [P, 4], ctx=ctx)
        sps = k.ps("ab_sp", [P, 2, NG, 512], ctx)
        tps = k.ps("ab_tp", [P, 2, 512], ctx)
        s = {n: k.sem("ab_" + n, ctx) for n in (
            "staged", "scored", "biased", "shifted", "exped", "turned", "laid", "mixed", "y_kept", "y_turned", "y_laid")}
        own = k.sem("ab_dve", ctx)
        moved = k.sem("ab_pool", ctx)
        rel = k.const("rel").rearrange("p (g n) -> p g n", g=NG)
        units = [(j, qb) for j in range(2) for qb in range(NB)]
        U = len(units)

        def pieces(qb):
            out, at = [], 0
            for g in range(NG):
                lo = FIRST[g](qb)
                out.append((g, lo, at, (qb + 1 - lo) * P))
                at += out[-1][3]
            return out, at

        def blocks_of(qb):
            return [(g, lo + n) for g, lo, _, w in pieces(qb)[0] for n in range(w // P)]

        def lots(qb):
            n = len(blocks_of(qb))
            return [range(a, min(a + 4, n)) for a in range(0, n, 4)]

        first_lot, n_lots = [], 0
        for _, qb in units:
            first_lot.append(n_lots)
            n_lots += len(lots(qb))
        assert n_lots % 2 == 0
        TRIPS = SLOTS_B // 2
        with nc.Block() as block:

            @block.gpsimd
            def _(pool):
                link = Chain(pool, moved)
                with pool.Fori(0, TRIPS) as i:
                    link.enter(i, 4 * NG)
                    for j in range(2):
                        pool.wait_ge(s["y_kept"], i * U + OPEN)
                        rows = slice(j * HD, (j + 1) * HD)
                        for g in range(NG):
                            for dst, t0 in ((qs, 2 * WA // P), (ks, (2 * WA + WB) // P)):
                                link(pool.tensor_copy(dst[:, j, g, :], k.qk[
                                    rows, bass.ds(i + (t0 + 2 * g), 1), :].rearrange("p a n -> p (a n)")))
                        pool.sem_inc(s["staged"], 1)
                    link.leave(4 * NG, TRIPS)

            @block.vector
            def _(dve):
                for sem in (s["y_kept"],):
                    dve.sem_inc(sem, OPEN)
                link = Chain(dve, own)
                per = 3 * U

                def keep(i, u):
                    j, qb = units[u]
                    dve.wait_ge(s["exped"], i * U + (u + 1))
                    link(dve.reciprocal(rd[:, u % 2:u % 2 + 1], den[:, u % 2:u % 2 + 1]))
                    dve.wait_ge(s["mixed"], i * U + (u + 1) + OPEN)
                    dve.tensor_scalar(y[:, qb, bass.ds(i * P + j * HD, HD)], sps[:, u % 2, 0, 256:256 + HD],
                                      rd[:, u % 2:u % 2 + 1], None, ALU.mult).then_inc(s["y_kept"], 1)

                with dve.Fori(0, TRIPS) as i:
                    link.enter(i, per)
                    for u, (j, qb) in enumerate(units):
                        dve.wait_ge(s["scored"], i * U + (u + 1))
                        ps_, W = pieces(qb)
                        for g, lo, at, w in ps_:
                            last = dve.scalar_tensor_tensor(
                                sc[:, u % 2, at:at + w], rel[:, g, SEQ - w:SEQ],
                                k.const("slope")[:, bass.ds(i * 2 + (j + g * SLOTS_B), 1)],
                                sps[:, u % 2, g, 0:w], ALU.mult, ALU.add)
                        link(last)
                        link(dve.reduce_max(mx[:, u % 2:u % 2 + 1], sc[:, u % 2, 0:W], axis=AX))
                        dve.tensor_scalar(nm[:, u % 2:u % 2 + 1], mx[:, u % 2:u % 2 + 1], -SCALE, None,
                                          ALU.mult).then_inc(s["shifted"], 1)
                        if u:
                            keep(i, u - 1)
                    keep(i, U - 1)
                    link.leave(per, TRIPS)

            @block.scalar
            def _(act):
                for sem in (s["laid"],):
                    act.sem_inc(sem, OPEN)
                with act.Fori(0, TRIPS) as i:
                    def exp(u):
                        j, qb = units[u]
                        W = pieces(qb)[1]
                        act.wait_ge(s["shifted"], i * U + (u + 1))
                        act.activation(sc[:, u % 2, 0:W], sc[:, u % 2, 0:W], ACT.Exp, bias=nm[:, u % 2:u % 2 + 1],
                                       scale=SCALE, accum_out=den[:, u % 2:u % 2 + 1]).then_inc(s["exped"], 1)

                    exp(0)
                    for u, (j, qb) in enumerate(units):
                        act.wait_ge(s["mixed"], i * U + u + OPEN)
                        for n, lot in enumerate(lots(qb)):
                            m = first_lot[u] + n
                            act.wait_ge(s["turned"], i * n_lots + (m + 1))
                            act.activation(pt[:, lot[0] * P:(lot[-1] + 1) * P], tps[:, m % 2, 0:len(lot) * P],
                                           ACT.Copy).then_inc(s["laid"], 1)
                            if n == 0 and u + 1 < U:
                                exp(u + 1)
                for n in range(NB):
                    act.wait_ge(s["y_turned"], n + 1)
                    act.activation(k.oT[:, WA // P:(WA + WBO) // P, n * P:(n + 1) * P],
                                   tps[:, n % 2, 0:WBO].rearrange("p (c n) -> p c n", c=WBO // P),
                                   ACT.Copy).then_inc(s["y_laid"], 1)
                act.wait_ge(s["y_laid"], NB)

            @block.tensor
            def _(pe):
                for sem in (s["mixed"],):
                    pe.sem_inc(sem, OPEN)
                with pe.Fori(0, TRIPS) as i:
                    def score(u):
                        j, qb = units[u]
                        if qb == 0:
                            pe.wait_ge(s["staged"], i * 2 + (j + 1))
                        if u >= 2:
                            pe.wait_ge(s["y_kept"], i * U + (u - 1) + OPEN)
                        else:
                            pe.wait_ge(s["y_kept"], i * U + OPEN)
                        for g, lo, at, w in pieces(qb)[0]:
                            last = pe.matmul(sps[:, u % 2, g, 0:w], qs[:, j, g, qb * P:(qb + 1) * P],
                                             ks[:, j, g, lo * P:lo * P + w], start=True, stop=True)
                        last.then_inc(s["scored"], 1)

                    score(0)
                    for u, (j, qb) in enumerate(units):
                        if u + 1 < U:
                            score(u + 1)
                        pe.wait_ge(s["exped"], i * U + (u + 1))
                        for n, lot in enumerate(lots(qb)):
                            m = first_lot[u] + n
                            if m >= 2:
                                pe.wait_ge(s["laid"], i * n_lots + (m - 1) + OPEN)
                            else:
                                pe.wait_ge(s["laid"], i * n_lots + OPEN)
                            for c, blk in enumerate(lot):
                                last = pe.transpose(tps[:, m % 2, c * P:(c + 1) * P],
                                                    sc[:, u % 2, blk * P:(blk + 1) * P], k.const("ident"))
                            last.then_inc(s["turned"], 1)
                        pe.wait_ge(s["laid"], i * n_lots + (first_lot[u] + len(lots(qb))) + OPEN)
                        bl = blocks_of(qb)
                        for n, (g, kb) in enumerate(bl):
                            last = pe.matmul(sps[:, u % 2, 0, 256:256 + HD], pt[:, n * P:(n + 1) * P],
                                             k.v_rows[:, kb, bass.ds(i * P + (WA + j * HD + g * WBO), HD)],
                                             start=(n == 0), stop=(n == len(bl) - 1))
                        last.then_inc(s["mixed"], 1)
                pe.wait_ge(s["y_kept"], U * TRIPS + OPEN)
                for n in range(NB):
                    if n >= 2:
                        pe.wait_ge(s["y_laid"], n - 1)
                    for c in range(WBO // P):
                        last = pe.transpose(tps[:, n % 2, c * P:(c + 1) * P], y[:, n, c * P:(c + 1) * P],
                                            k.const("ident"))
                    last.then_inc(s["y_turned"], 1)


def decode_b(k):
    nc = k.nc
    BS = DEC * SLOTS_B
    Q0, K0, V0 = 3 * WA, 3 * WA + WB, 3 * WA + 2 * WB
    with ExitStack() as ctx:
        kv = k.sb("db_kv", [P, DEC, NG, 2 * WBO], ctx=ctx)
        prod = k.sb("db_prod", [P, WB], ctx=ctx)
        sc = k.sb("db_sc", [P, NG, DEC, SLOTS_B], ctx=ctx)
        sn = k.sb("db_sn", [DEC, NG, SLOTS_B], ctx=ctx)
        dn = k.sb("db_dn", [DEC, NG, DEC, SLOTS_B], ctx=ctx)
        pr = k.sb("db_pr", [BS, NG, P + 1], ctx=ctx)
        pt = k.sb("db_pt", [P, NG, BS], ctx=ctx)
        xs = k.sb("db_xs", [BS, NG, DEC], ctx=ctx)
        pn = k.sb("db_pn", [DEC, NG, BS], ctx=ctx)
        om = k.sb("db_om", [SLOTS_B, WBO], ctx=ctx)
        mx = k.sb("db_mx", [BS, 4], ctx=ctx)
        rep = k.ps("db_rep", [P, 2, 2, 512], ctx)
        row = k.ps("db_row", [P, 512], ctx)
        new = k.ps("db_new", [P, 512], ctx)
        vp = k.ps("db_vp", [P, 512], ctx)
        cp = k.ps("db_cp", [P, 512], ctx)
        kv_in = [k.sem(f"db_kv_in{b}", ctx) for b in range(DEC)]
        s = {n: k.sem("db_" + n, ctx) for n in (
            "rep", "rep_used", "scores", "rows", "exped", "probs", "turned", "laid", "new_turned", "new_laid",
            "mixed", "own_kept", "cols", "cols_kept")}
        own = k.sem("db_dve", ctx)
        HW = WB // 2
        with nc.Block() as block:

            @block.sync
            def _(sp):
                for b in range(DEC):
                    for g, (_, d) in enumerate(GROUPS):
                        sp.dma_start(kv[:, b, g, :], k.io[f"cache_kv_b{g}"][0, b].rearrange(
                            "(n d) k h e -> n d (k h e)", d=d)[:, 0, :]).then_inc(kv_in[b], 16)

            @block.tensor
            def _(pe):
                for b in range(DEC):
                    if b >= 2:
                        pe.wait_ge(s["rep_used"], b - 1)
                    for c in range(2):
                        last = pe.matmul(rep[:, b % 2, c, 0:HW], k.const("ident", DEC)[:, b:b + 1].to_broadcast([DEC, P]),
                                         k.samp[0:DEC, Q0 + c * HW:Q0 + (c + 1) * HW], start=True, stop=True)
                    last.then_inc(s["rep"], 1)
                pe.wait_ge(s["scores"], 1)
                for g in range(NG):
                    pe.transpose(row[0:BS, g * P:(g + 1) * P], sc[:, g].rearrange("p b s -> p (b s)"), k.const("ident"))
                for g in range(NG):
                    last = pe.matmul(new[0:BS, g:g + 1], dn[:, g].rearrange("p b s -> p (b s)"),
                                     k.const("ones", DEC)[:, 0:1], start=True, stop=True)
                last.then_inc(s["rows"], 1)
                pe.wait_ge(s["probs"], 1)
                for g in range(NG):
                    pe.transpose(row[:, g * BS:(g + 1) * BS], pr[:, g, 0:P], k.const("ident", BS)[:, 0:BS])
                for g in range(NG):
                    last = pe.matmul(new[0:DEC, g * BS:(g + 1) * BS], xs[:, g], k.const("ident", BS)[:, 0:BS],
                                     start=True, stop=True)
                last.then_inc(s["turned"], 1)
                pe.wait_ge(s["laid"], 1)
                for b in range(DEC):
                    if b:
                        pe.wait_ge(s["own_kept"], b)
                    mine = slice(b * SLOTS_B, (b + 1) * SLOTS_B)
                    for g in range(NG):
                        pe.matmul(vp[0:SLOTS_B, 0:WBO], pt[:, g, mine], kv[:, b, g, WBO:], start=(g == 0), stop=False)
                        last = pe.matmul(vp[0:SLOTS_B, 0:WBO], pn[:, g, mine],
                                         k.samp[0:DEC, V0 + g * WBO:V0 + (g + 1) * WBO], start=False,
                                         stop=(g == NG - 1))
                    last.then_inc(s["mixed"], 1)
                    pe.wait_ge(s["own_kept"], b + 1)
                    for c in range(WBO // P):
                        last = pe.matmul(cp[:, c * DEC + b:c * DEC + b + 1], om[:, c * P:(c + 1) * P],
                                         k.const("ones", SLOTS_B)[:, 0:1], start=True, stop=True)
                    last.then_inc(s["cols"], 1)

            @block.scalar
            def _(act):
                act.wait_ge(s["scores"], 2)
                act.activation(pr[:].rearrange("p g n -> p (g n)"), pr[:].rearrange("p g n -> p (g n)"), ACT.Exp,
                               bias=mx[:, 1:2], accum_out=mx[:, 2:3]).then_inc(s["exped"], 1)
                act.wait_ge(s["cols"], DEC)
                act.activation(k.oT[:, WA // P:(WA + WBO) // P, SEQ:TOK],
                               cp[:, 0:WBO // P * DEC].rearrange("p (c b) -> p c b", b=DEC),
                               ACT.Copy).then_inc(s["cols_kept"], 1)
                act.wait_ge(s["cols_kept"], 1)

            @block.vector
            def _(dve):
                link = Chain(dve, own)
                link(dve.tensor_tensor(prod[0:DEC, :], k.samp[0:DEC, Q0:Q0 + WB], k.samp[0:DEC, K0:K0 + WB], ALU.mult))
                link(dve.tensor_reduce(sn[:].rearrange("p g s -> p (g s)"),
                                       prod[0:DEC, :].rearrange("p (n d) -> p n d", d=HD), axis=AX, op=ALU.add))
                for g in range(NG):
                    link(dve.tensor_tensor(dn[:, g], sn[:, g].unsqueeze(1).to_broadcast([DEC, DEC, SLOTS_B]),
                                           k.const("ident", DEC)[:, 0:DEC].unsqueeze(2).to_broadcast(
                                               [DEC, DEC, SLOTS_B]), ALU.mult))
                for b in range(DEC):
                    dve.wait_ge(s["rep"], b + 1)
                    dve.wait_ge(kv_in[b], 16 * NG)
                    for g in range(NG):
                        for c in range(2):
                            lo, hi = max(g * WBO, c * HW), min((g + 1) * WBO, (c + 1) * HW)
                            if lo < hi:
                                last = dve.tensor_tensor(prod[:, lo:hi], kv[:, b, g, lo - g * WBO:hi - g * WBO],
                                                         rep[:, b % 2, c, lo - c * HW:hi - c * HW], ALU.mult)
                    last.then_inc(s["rep_used"], 1)
                    dve.wait_ge(s["rep_used"], b + 1)
                    link(dve.tensor_reduce(sc[:, :, b, :], prod[:].rearrange("p (g s d) -> p g s d", g=NG, s=SLOTS_B),
                                           axis=AX, op=ALU.add))
                for g in range(NG):
                    last = dve.scalar_tensor_tensor(
                        sc[:, g], sc[:, g], SCALE,
                        k.const("row_bias")[:, g * SLOTS_B:(g + 1) * SLOTS_B].unsqueeze(1).to_broadcast(
                            [P, DEC, SLOTS_B]), ALU.mult, ALU.add)
                last.then_inc(s["scores"], 1)
                dve.wait_ge(s["rows"], 1)
                link(dve.tensor_copy(pr[:, :, 0:P], row[0:BS, 0:NG * P].rearrange("p (g n) -> p g n", g=NG)))
                link(dve.tensor_scalar(pr[:, :, P:P + 1], new[0:BS, 0:NG].unsqueeze(2), SCALE, None, ALU.mult))
                link(dve.reduce_max(mx[:, 0:1], pr[:].rearrange("p g n -> p (g n)"), axis=AX))
                dve.tensor_scalar(mx[:, 1:2], mx[:, 0:1], -1.0, None, ALU.mult).then_inc(s["scores"], 1)
                dve.wait_ge(s["exped"], 1)
                link(dve.reciprocal(mx[:, 3:4], mx[:, 2:3]))
                flat = pr[:].rearrange("p g n -> p (g n)")
                link(dve.tensor_scalar(flat, flat, mx[:, 3:4], None, ALU.mult))
                dve.tensor_tensor(xs[:], pr[:, :, P:P + 1].to_broadcast([BS, NG, DEC]),
                                  k.const("own_sample", BS).unsqueeze(1).to_broadcast([BS, NG, DEC]),
                                  ALU.mult).then_inc(s["probs"], 1)
                dve.wait_ge(s["turned"], 1)
                link(dve.tensor_copy(pt[:].rearrange("p g n -> p (g n)"), row[:, 0:NG * BS]))
                dve.tensor_copy(pn[:].rearrange("p g n -> p (g n)"), new[0:DEC, 0:NG * BS]).then_inc(s["laid"], 1)
                for b in range(DEC):
                    dve.wait_ge(s["mixed"], b + 1)
                    if b:
                        dve.wait_ge(s["cols"], b)
                    dve.tensor_tensor(om[:], vp[0:SLOTS_B, 0:WBO], k.const("own_head", SLOTS_B)[:, 0:WBO],
                                      ALU.mult).then_inc(s["own_kept"], 1)


def merge(k):
    nc = k.nc
    CA, CB = WA // P, WBO // P
    H = TOK // 2
    GATE0 = 3 * WA + 3 * WB
    with ExitStack() as ctx:
        wg = k.sb("mg_wg", [P, 2, 2, KC, P], ctx=ctx)
        wb = k.sb("mg_wb", [P, 2, CA + CB, P], ctx=ctx)
        wo = k.sb("mg_wo", [P, KC, D], ctx=ctx)
        sg = k.sb("mg_sg", [P, 2, 2, H], ctx=ctx)
        mixT = k.sb("mg_mix", [P, KC, TOK], ctx=ctx)
        ps = k.ps("mg_ps", [P, 8, 512], ctx)
        w_in = [k.sem(f"mg_w_in{j}", ctx) for j in range(2)]
        s = {n: k.sem("mg_" + n, ctx) for n in (
            "gate_a", "gate_b", "ya", "yb", "sig_a", "sig_b", "part_a", "part_b", "mixed", "proj", "kept")}
        x_in = k.pool_sem("mg_x_in")
        wo_in = k.pool_sem("mg_wo_in")
        TRIPS = KC // 2
        halves = lambda t: t.rearrange("p (a n) -> p a n", a=2)
        with nc.Block() as block:

            @block.sync
            def _(sp):
                with sp.Fori(0, TRIPS) as i:
                    for j in range(2):
                        sp.wait_ge(s["yb"], i * 2 + OPEN)
                        at = i * (2 * P) + j * P
                        for n in range(2):
                            sp.dma_start(wg[:, j, n], k.io["w_in"][0].rearrange("(p c) n -> p c n", c=KC)[
                                :, :, bass.ds(at + (GATE0 + n * D), P)]).then_inc(w_in[j], 16)
                        sp.dma_start(wb[:, j, 0:CA], k.io["w_br_a"][0].rearrange("(c p) n -> p c n", p=P)[
                            :, :, bass.ds(at, P)]).then_inc(w_in[j], 16)
                        sp.dma_start(wb[:, j, CA:CA + CB], k.io["w_br_b"][0].rearrange("(c p) n -> p c n", p=P)[
                            :, :, bass.ds(at, P)]).then_inc(w_in[j], 16)

            @block.gpsimd
            def _(pool):
                pool.dma_start(wo[:], k.io["w_o"][0].rearrange("(c p) n -> p c n", p=P)).then_inc(wo_in, 16)
                pool.dma_start(k.x1[:, 0:NB, :], k.io["x_prompt"][0].rearrange("(b p) n -> p b n", p=P))\
                    .then_inc(x_in, 16)
                pool.dma_start(k.x1[0:DEC, NB, :], x_rows(k, NB)).then_inc(x_in, 16)

            @block.scalar
            def _(act):
                for sem in (s["sig_a"], s["sig_b"],):
                    act.sem_inc(sem, OPEN)
                with act.Fori(0, TRIPS) as i:
                    for j in range(2):
                        t = i * 2 + j
                        act.wait_ge(s["part_a"], t + OPEN)
                        act.wait_ge(s["gate_a"], t + 1)
                        act.activation(sg[:, 0], ps[:, 0:2, 0:H], ACT.Sigmoid).then_inc(s["sig_a"], 1)
                        act.wait_ge(s["mixed"], t + OPEN)
                        act.wait_ge(s["gate_b"], t + 1)
                        act.activation(sg[:, 1], ps[:, 2:4, 0:H], ACT.Sigmoid).then_inc(s["sig_b"], 1)

            @block.vector
            def _(dve):
                for sem in (s["part_a"], s["part_b"], s["mixed"],):
                    dve.sem_inc(sem, OPEN)
                with dve.Fori(0, TRIPS) as i:
                    for j in range(2):
                        t = i * 2 + j
                        mix = mixT[:, bass.ds(t, 1), :].rearrange("p a (h n) -> p (a h) n", h=2)
                        dve.wait_ge(s["sig_a"], t + 1 + OPEN)
                        dve.wait_ge(s["ya"], t + 1)
                        dve.tensor_tensor(mix, sg[:, 0], ps[:, 4:6, 0:H], ALU.mult).then_inc(s["part_a"], 1)
                        dve.wait_ge(s["sig_b"], t + 1 + OPEN)
                        dve.wait_ge(s["yb"], t + 1 + OPEN)
                        dve.tensor_tensor(sg[:, 1], sg[:, 1], ps[:, 6:8, 0:H], ALU.mult).then_inc(s["part_b"], 1)
                        dve.wait_ge(s["part_b"], t + 1 + OPEN)
                        dve.tensor_tensor(mix, mix, sg[:, 1], ALU.add).then_inc(s["mixed"], 1)
                        dve.wait_ge(s["mixed"], t + 1 + OPEN)
                dve.wait_ge(x_in, 32)
                for b in range(NBLK):
                    r = rows_of(b)
                    for h in range(2):
                        n = 2 * b + h
                        dve.wait_ge(s["proj"], n + 1)
                        x = k.x1[0:r, b, h * 512:(h + 1) * 512]
                        dve.tensor_tensor(x, x, ps[0:r, n % 8, :], ALU.add).then_inc(s["kept"], 1)
                dve.wait_ge(s["kept"], 2 * NBLK)

            @block.tensor
            def _(pe):
                for sem in (s["yb"],):
                    pe.sem_inc(sem, OPEN)
                def tile(dst, w, src, pieces):
                    for h in range(2):
                        for c in range(pieces):
                            last = pe.matmul(ps[:, dst + h, 0:H], w[:, c, :], src[:, c, h * H:(h + 1) * H],
                                             start=(c == 0), stop=(c == pieces - 1))
                    return last

                with pe.Fori(0, TRIPS) as i:
                    for j in range(2):
                        t = i * 2 + j
                        pe.wait_ge(w_in[j], i * 64 + 64)
                        pe.wait_ge(s["sig_a"], t + OPEN)
                        tile(0, wg[:, j, 0], k.hT, KC).then_inc(s["gate_a"], 1)
                        pe.wait_ge(s["sig_b"], t + OPEN)
                        tile(2, wg[:, j, 1], k.hT, KC).then_inc(s["gate_b"], 1)
                        pe.wait_ge(s["part_a"], t + OPEN)
                        tile(4, wb[:, j, 0:CA], k.oT[:, 0:CA], CA).then_inc(s["ya"], 1)
                        pe.wait_ge(s["part_b"], t + OPEN)
                        tile(6, wb[:, j, CA:CA + CB], k.oT[:, CA:CA + CB], CB).then_inc(s["yb"], 1)
                pe.wait_ge(wo_in, 16)
                pe.wait_ge(s["mixed"], KC + OPEN)
                for b in range(NBLK):
                    r = rows_of(b)
                    for h in range(2):
                        n = 2 * b + h
                        if n >= 8:
                            pe.wait_ge(s["kept"], n - 7)
                        for c in range(KC):
                            last = pe.matmul(ps[0:r, n % 8, :], mixT[:, c, b * P:b * P + r],
                                             wo[:, c, h * 512:(h + 1) * 512], start=(c == 0), stop=(c == KC - 1))
                        last.then_inc(s["proj"], 1)


def route(k):
    nc = k.nc
    NR = E_GROUPS + EXPERTS
    MUL = TOK // SLOT
    BIG = 64.0
    with ExitStack() as ctx:
        hn = k.sb("rt_hn", [P, NBLK, D], ctx=ctx)
        ms = k.sb("rt_ms", [P, NBLK], ctx=ctx)
        rms = k.sb("rt_rms", [P, NBLK], ctx=ctx)
        rstd = k.sb("rt_rstd", [P, NBLK], ctx=ctx)
        wr = k.sb("rt_wr", [P, KC, NR], ctx=ctx)
        bias = k.sb("rt_bias", [P, NR], ctx=ctx)
        small = lambda name, *shape: k.sb("rt_" + name, [P, NBLK, *shape], ctx=ctx)
        lg = small("lg", NR)
        pick = small("pick", 8)
        mx = [small(f"mx{n}", 1) for n in range(3)]
        low = small("low", 1)
        oh_g = small("oh_g", E_GROUPS)
        oh_k = [small(f"oh{n}", E_PER) for n in range(2)]
        shifted = small("shifted", E_GROUPS)
        eg = small("eg", E_GROUPS)
        pg = small("pg", 1)
        e2 = small("e2", 1)
        by_g = small("by_g", E_GROUPS, E_PER)
        ing = small("ing", E_PER)
        ing2 = small("ing2", E_PER)
        one = [small(f"one{n}", E_GROUPS, E_PER) for n in range(2)]
        both = small("both", EXPERTS)
        rank = small("rank", EXPERTS)
        tmp = small("tmp", EXPERTS)
        col = {n: small("col_" + n, 1) for n in ("rank", "full", "pos", "eid", "base", "slot", "some")}
        at_pos = [small(f"at_pos{n}", SLOT) for n in range(2)]
        at_slot = [small(f"at_slot{n}", 2 * ALL_SLOTS) for n in range(2)]
        cmp_ = k.sb("rt_cmp", [P, EXPERTS, MUL], ctx=ctx)
        more = k.sb("rt_more", [P, EXPERTS], ctx=ctx)
        upto = k.sb("rt_upto", [P, EXPERTS], ctx=ctx)
        base = k.sb("rt_base", [P, EXPERTS], ctx=ctx)
        which = k.sb("rt_which", [1, MORE, EXPERTS], ctx=ctx)
        eid = k.sb("rt_eid", [1, MORE], ctx=ctx)
        empty = k.sb("rt_empty", [SLOT, 2 * ALL_SLOTS], ctx=ctx)
        tr = k.ps("rt_tr", [P, 2, KC, P], ctx)
        lp = k.ps("rt_lp", [P, 512], ctx)
        rp = k.ps("rt_rp", [P, 512], ctx)
        cp = k.ps("rt_cp", [P, 512], ctx)
        tp = k.ps("rt_tp", [P, 512], ctx)
        s = {n: k.sem("rt_" + n, ctx) for n in (
            "in", "squares", "roots", "scaled", "turned", "placed", "h2_out", "logits", "chosen", "exped", "ranks",
            "tables", "slots")}
        own = k.sem("rt_dve", ctx)
        with nc.Block() as block:

            @block.sync
            def _(sp):
                v = lambda name: k.io[name][0].rearrange("(p c) n -> p c n", c=KC)
                sp.dma_start(wr[:, :, 0:E_GROUPS], v("w_group")).then_inc(s["in"], 16)
                sp.dma_start(wr[:, :, E_GROUPS:NR], v("w_expert")).then_inc(s["in"], 16)
                sp.dma_start(bias[:, 0:E_GROUPS], k.io["b_group"][0].partition_broadcast(P)).then_inc(s["in"], 16)
                sp.dma_start(bias[:, E_GROUPS:NR], k.io["b_expert"][0].partition_broadcast(P)).then_inc(s["in"], 16)
                for b in range(NBLK):
                    r = rows_of(b)
                    sp.wait_ge(s["scaled"], b + 1)
                    sp.dma_start(k.io["h2"][b * P:b * P + r, :], hn[0:r, b, :]).then_inc(s["h2_out"], 16)
                sp.wait_ge(s["h2_out"], 16 * NBLK)

            @block.scalar
            def _(act):
                for b in range(NBLK):
                    r = rows_of(b)
                    act.activation(hn[0:r, b, :], k.x1[0:r, b, :], ACT.Square,
                                   accum_out=ms[0:r, b:b + 1]).then_inc(s["squares"], 1)
                act.wait_ge(s["squares"], NBLK)
                for b in range(NBLK):
                    r = rows_of(b)
                    act.activation(rms[0:r, b:b + 1], ms[0:r, b:b + 1], ACT.Sqrt, bias=k.const("eps", r),
                                   scale=1.0 / D).then_inc(s["roots"], 1)
                act.wait_ge(s["chosen"], 1)
                act.activation(eg[:], shifted[:], ACT.Exp).then_inc(s["exped"], 1)
                act.wait_ge(s["chosen"], 2)
                act.activation(e2[:], e2[:], ACT.Exp).then_inc(s["exped"], 1)

            @block.tensor
            def _(pe):
                for b in range(NBLK):
                    r = rows_of(b)
                    pe.wait_ge(s["scaled"], b + 1)
                    if b >= 2:
                        pe.wait_ge(s["placed"], b - 1)
                    v = hn[0:r, b, :].rearrange("t (p c) -> t c p", c=KC)
                    for c in range(KC):
                        last = pe.transpose(tr[:, b % 2, c, 0:r], v[:, c, :], k.const("ident", r)[:, 0:r])
                    last.then_inc(s["turned"], 1)
                pe.wait_ge(s["in"], 64)
                pe.wait_ge(s["placed"], NBLK)
                for b in range(NBLK):
                    r = rows_of(b)
                    for c in range(KC):
                        last = pe.matmul(lp[0:r, b * NR:(b + 1) * NR], k.hT[:, c, b * P:b * P + r], wr[:, c, :],
                                         start=(c == 0), stop=(c == KC - 1))
                last.then_inc(s["logits"], 1)
                pe.wait_ge(s["chosen"], 3)
                for b in range(NBLK):
                    for b2 in range(b + 1):
                        pe.matmul(rp[:, b * EXPERTS:(b + 1) * EXPERTS], k.const("before" if b2 == b else "ones"),
                                  both[:, b2, :], start=(b2 == 0), stop=(b2 == b))
                for b in range(NBLK):
                    last = pe.matmul(cp[:, 0:EXPERTS], k.const("ones"), both[:, b, :], start=(b == 0),
                                     stop=(b == NBLK - 1))
                last.then_inc(s["ranks"], 1)
                pe.wait_ge(s["slots"], 1)
                n = 0
                for q in range(2):
                    for b in range(NBLK):
                        last = pe.matmul(tp[0:SLOT, 0:2 * ALL_SLOTS], at_pos[q][:, b, :], at_slot[q][:, b, :],
                                         start=(n == 0), stop=(n == 2 * NBLK - 1))
                        n += 1
                last.then_inc(s["tables"], 1)

            @block.vector
            def _(dve):
                link = Chain(dve, own)
                tt = lambda o, a, b, op: link(dve.tensor_tensor(o, a, b, op))
                wide = lambda ap, n: ap.to_broadcast([P, NBLK, n])
                real = k.const("real").unsqueeze(2)
                iota = lambda n: k.const("iota")[:, 0:n].unsqueeze(1).to_broadcast([P, NBLK, n])
                link(dve.memset(lg[:], 0.0))
                for b in range(NBLK):
                    r = rows_of(b)
                    dve.wait_ge(s["roots"], b + 1)
                    link(dve.reciprocal(rstd[0:r, b:b + 1], rms[0:r, b:b + 1]))
                    dve.tensor_scalar(hn[0:r, b, :], k.x1[0:r, b, :], rstd[0:r, b:b + 1], None,
                                      ALU.mult).then_inc(s["scaled"], 1)
                for b in range(NBLK):
                    r = rows_of(b)
                    dve.wait_ge(s["turned"], b + 1)
                    dve.tensor_tensor(k.hT[:, :, b * P:b * P + r], tr[:, b % 2, :, 0:r],
                                      k.g_ffn[:].unsqueeze(2).to_broadcast([P, KC, r]),
                                      ALU.mult).then_inc(s["placed"], 1)
                dve.wait_ge(s["logits"], 1)
                dve.wait_ge(s["in"], 64)
                for b in range(NBLK):
                    r = rows_of(b)
                    last = dve.tensor_tensor(lg[0:r, b, :], lp[0:r, b * NR:(b + 1) * NR], bias[0:r, :], ALU.add)
                link(last)

                def first_largest(vals, n, most, onehot):
                    link(dve.tensor_reduce(most[:], vals, axis=AX, op=ALU.max))
                    tt(pick[:, :, 0:n], vals, wide(most[:], n), ALU.is_equal)
                    link(dve.scalar_tensor_tensor(pick[:, :, 0:n], pick[:, :, 0:n], -BIG, iota(n), ALU.mult, ALU.add))
                    link(dve.tensor_reduce(low[:], pick[:, :, 0:n], axis=AX, op=ALU.min))
                    tt(onehot[:], pick[:, :, 0:n], wide(low[:], n), ALU.is_equal)

                first_largest(lg[:, :, 0:E_GROUPS], E_GROUPS, mx[0], oh_g)
                dve.tensor_tensor(shifted[:], lg[:, :, 0:E_GROUPS], wide(mx[0][:], E_GROUPS), ALU.subtract)\
                    .then_inc(s["chosen"], 1)
                flat = [P, NBLK, E_GROUPS, E_PER]
                tt(by_g[:], lg[:, :, E_GROUPS:NR].rearrange("p b (g e) -> p b g e", g=E_GROUPS),
                   oh_g[:].unsqueeze(3).to_broadcast(flat), ALU.mult)
                link(dve.tensor_reduce(ing[:], by_g[:].rearrange("p b g e -> p b e g"), axis=AX, op=ALU.add))
                first_largest(ing[:], E_PER, mx[1], oh_k[0])
                link(dve.scalar_tensor_tensor(ing2[:], oh_k[0][:], -FAR, ing[:], ALU.mult, ALU.add))
                first_largest(ing2[:], E_PER, mx[2], oh_k[1])
                dve.tensor_tensor(e2[:], mx[2][:], mx[1][:], ALU.subtract).then_inc(s["chosen"], 1)
                for q in range(2):
                    tt(one[q][:], oh_g[:].unsqueeze(3).to_broadcast(flat),
                       oh_k[q][:].unsqueeze(2).to_broadcast(flat), ALU.mult)
                    f = one[q][:].rearrange("p b g e -> p b (g e)")
                    tt(f, f, wide(real, EXPERTS), ALU.mult)
                oh = [o[:].rearrange("p b g e -> p b (g e)") for o in one]
                dve.tensor_tensor(both[:], oh[0], oh[1], ALU.add).then_inc(s["chosen"], 1)
                dve.wait_ge(s["exped"], 2)
                link(dve.tensor_reduce(pg[:], eg[:], axis=AX, op=ALU.add))
                link(dve.reciprocal(pg[:], pg[:]))
                link(dve.tensor_scalar(col["some"][:], e2[:], 1.0, None, ALU.add))
                link(dve.reciprocal(col["some"][:], col["some"][:]))
                tt(k.gate[:, :, 0:1], pg[:], col["some"][:], ALU.mult)
                tt(k.gate[:, :, 1:2], k.gate[:, :, 0:1], e2[:], ALU.mult)
                dve.wait_ge(s["ranks"], 1)
                steps = k.const("steps")
                link(dve.tensor_copy(rank[:].rearrange("p b e -> p (b e)"), rp[:, 0:NBLK * EXPERTS]))
                tt(cmp_[:], cp[:, 0:EXPERTS].unsqueeze(2).to_broadcast([P, EXPERTS, MUL]),
                   steps.unsqueeze(1).to_broadcast([P, EXPERTS, MUL]), ALU.is_gt)
                link(dve.tensor_reduce(more[:], cmp_[:], axis=AX, op=ALU.add))
                link(dve.tensor_tensor_scan(upto[:], k.const("ones")[:, 0:EXPERTS], more[:], 0.0, ALU.mult, ALU.add))
                tt(base[:], upto[:], more[:], ALU.subtract)
                tt(which[:], upto[0:1, :].unsqueeze(1).to_broadcast([1, MORE, EXPERTS]),
                   k.const("iota", 1)[:, 0:MORE].unsqueeze(2).to_broadcast([1, MORE, EXPERTS]), ALU.is_le)
                link(dve.tensor_reduce(eid[:], which[:], axis=AX, op=ALU.add))
                link(dve.tensor_scalar(k.owner[:], eid[:], float(EXPERTS - 1), None, ALU.min))
                link(dve.tensor_copy(k.n_more[:], upto[0:1, EXPERTS - 1:EXPERTS]))
                for q in range(2):
                    def total(out, table):
                        tt(tmp[:], oh[q], table, ALU.mult)
                        link(dve.tensor_reduce(out[:], tmp[:], axis=AX, op=ALU.add))

                    c = col
                    total(c["rank"], rank[:])
                    total(c["eid"], iota(EXPERTS))
                    total(c["base"], base[:].unsqueeze(1).to_broadcast([P, NBLK, EXPERTS]))
                    tt(pick[:], wide(c["rank"][:], MUL), steps.unsqueeze(1).to_broadcast([P, NBLK, MUL]), ALU.is_ge)
                    link(dve.tensor_reduce(c["full"][:], pick[:], axis=AX, op=ALU.add))
                    link(dve.scalar_tensor_tensor(c["pos"][:], c["full"][:], -float(SLOT), c["rank"][:],
                                                  ALU.mult, ALU.add))
                    link(dve.tensor_scalar(c["some"][:], c["full"][:], 0.5, None, ALU.is_ge))
                    tt(c["slot"][:], c["base"][:], c["full"][:], ALU.add)
                    tt(c["slot"][:], c["slot"][:], c["eid"][:], ALU.subtract)
                    link(dve.tensor_scalar(c["slot"][:], c["slot"][:], float(EXPERTS - 1), None, ALU.add))
                    tt(c["slot"][:], c["slot"][:], c["some"][:], ALU.mult)
                    tt(c["slot"][:], c["slot"][:], c["eid"][:], ALU.add)
                    tt(at_pos[q][:], iota(SLOT), wide(c["pos"][:], SLOT), ALU.is_equal)
                    sl = at_slot[q][:, :, 0:ALL_SLOTS]
                    sl2 = at_slot[q][:, :, ALL_SLOTS:2 * ALL_SLOTS]
                    tt(sl, iota(ALL_SLOTS), wide(c["slot"][:], ALL_SLOTS), ALU.is_equal)
                    tt(sl2, sl, wide(k.const("token").unsqueeze(2), ALL_SLOTS), ALU.mult)
                    tt(sl, sl, wide(k.const(f"pair{q}").unsqueeze(2), ALL_SLOTS), ALU.mult)
                dve.sem_inc(s["slots"], 1)
                dve.wait_ge(s["tables"], 1)
                v = tp[0:SLOT, 0:2 * ALL_SLOTS]
                link(dve.memset(k.index[:], NONE))
                link(dve.tensor_scalar(empty[:], v, 0.0, float(NONE), ALU.is_equal, ALU.mult))
                for n in range(2):
                    part = slice(n * ALL_SLOTS, (n + 1) * ALL_SLOTS)
                    link(dve.scalar_tensor_tensor(k.index[:, n, 0:ALL_SLOTS], v[:, part], -1.0, empty[:, part],
                                                  ALU.add, ALU.add))


def experts(k):
    nc = k.nc
    FC = FF // P
    with ExitStack() as ctx:
        wgu = k.sb("ex_wgu", [P, 2, 2, KC, FF], ctx=ctx)
        wd = k.sb("ex_wd", [P, 2, FC, D], ctx=ctx)
        xg = k.sb("ex_xg", [SLOT, 2, D], ctx=ctx)
        xT = k.sb("ex_xT", [P, 2, KC, SLOT], ctx=ctx)
        sg = k.sb("ex_sg", [SLOT, 2, FF], ctx=ctx)
        hm = k.sb("ex_hm", [SLOT, 2, FF], ctx=ctx)
        hmT = k.sb("ex_hmT", [P, 2, FC, SLOT], ctx=ctx)
        yg = k.sb("ex_yg", [SLOT, 2, D], ctx=ctx)
        from_row = k.sb("ex_from", [SLOT, 2, 1], U32, ctx=ctx)
        to_row = k.sb("ex_to", [SLOT, 2, 1], U32, ctx=ctx)
        xp = k.ps("ex_xp", [P, KC, SLOT], ctx)
        gp = k.ps("ex_gp", [SLOT, 2, 2, FF], ctx)
        hp = k.ps("ex_hp", [P, 512], ctx)
        yp = k.ps("ex_yp", [SLOT, 2, 512], ctx)
        pair = lambda n: [k.sem(f"ex_{n}{j}", ctx) for j in range(2)]
        gu_in, d_in = pair("gu_in"), pair("d_in")
        x_in = [k.pool_sem(f"ex_x_in{j}") for j in range(2)]
        y_out = [k.pool_sem(f"ex_y_out{j}") for j in range(2)]
        y_left = pair("y_left")
        from_laid, to_laid = pair("from_laid"), pair("to_laid")
        turned, x_kept = pair("turned"), pair("x_kept")
        gu_made, silu_made, h_made, h_turned, h_kept = (pair("gu_made"), pair("silu"), pair("h_made"),
                                                        pair("h_turned"), pair("h_kept"))
        y_made, y_lo, y_hi = pair("y_made"), pair("y_lo"), pair("y_hi")
        cleared = k.sem("ex_cleared", ctx)
        go_pe, go_pool = k.sem("ex_go_pe", ctx), k.sem("ex_go_pool", ctx)
        TRIPS, ALL = EXPERTS // 2, ALL_SLOTS // 2

        def passes(eng, body, end=lambda trips: None):
            with eng.Fori(0, TRIPS) as i:
                body(i, False)
            end(TRIPS)
            n = eng.value_load(k.n_more[0:1, 0:1], min_val=0, max_val=MORE)
            with eng.If(n > 0):
                with eng.Fori(TRIPS, ALL) as i:
                    body(i, True)
                end(ALL)

        with nc.Block() as block:

            @block.sync
            def _(sp):
                def body(i, further):
                    for j in range(2):
                        if further:
                            e = sp.value_load(k.owner[0:1, bass.ds(i * 2 + (j - EXPERTS), 1)], min_val=0,
                                              max_val=EXPERTS - 1)
                        else:
                            e = i * 2 + j
                        w = lambda name, c: k.io[name][0, bass.ds(e, 1)].rearrange("a (p c) n -> p (a c) n", c=c)
                        sp.wait_ge(gu_made[j], i + OPEN)
                        sp.dma_start(wgu[:, j, 0], w("w_gate_e", KC)).then_inc(gu_in[j], 16)
                        sp.dma_start(wgu[:, j, 1], w("w_up_e", KC)).then_inc(gu_in[j], 16)
                        sp.wait_ge(y_made[j], i + OPEN)
                        sp.dma_start(wd[:, j], w("w_down_e", FC)).then_inc(d_in[j], 16)
                passes(sp, body)

            @block.gpsimd
            def _(pool):
                for sem in (*y_left,):
                    pool.sem_inc(sem, OPEN)
                def gather(j):
                    pool.indirect_dma_start(xg[:, j, :], None, k.io["h2"], bass.IndirectOffsetOnAxis(
                        ap=from_row[:, j, :], axis=0), bounds_check=TOK - 1, oob_is_err=False).then_inc(x_in[j], 16)

                def body(i, further):
                    for j in range(2):
                        pool.wait_ge(from_laid[j], i + 2)
                        pool.wait_ge(turned[j], i + 1)
                        pool.sem_inc(go_pool, 1)
                        gather(j)
                    for j in range(2):
                        pool.wait_ge(to_laid[j], i + 1)
                        pool.wait_ge(y_lo[j], i + 1 + OPEN)
                        pool.wait_ge(y_hi[j], i + 1 + OPEN)
                        pool.sem_inc(go_pool, 1)
                        pool.indirect_dma_start(k.io["pairs"], bass.IndirectOffsetOnAxis(ap=to_row[:, j, :], axis=0),
                                                yg[:, j, :], None, bounds_check=2 * TOK - 1,
                                                oob_is_err=False).then_inc(y_out[j], 16)
                    for j in range(2):
                        pool.wait_ge(y_out[j], i * 16 + 16)
                        pool.sem_inc(y_left[j], 1)

                def end(trips):
                    for j in range(2):
                        pool.wait_ge(y_out[j], 16 * trips)
                        pool.wait_ge(x_in[j], 16 * (trips + 1))

                pool.wait_ge(cleared, 1)
                for j in range(2):
                    pool.wait_ge(from_laid[j], 1)
                    gather(j)
                passes(pool, body, end)

            @block.scalar
            def _(act):
                for sem in (*h_kept, *y_lo,):
                    act.sem_inc(sem, OPEN)
                def body(i, further):
                    for j in range(2):
                        act.wait_ge(gu_made[j], i + 1 + OPEN)
                        act.activation(sg[:, j], gp[:, j, 0], ACT.Silu).then_inc(silu_made[j], 1)
                    for j in range(2):
                        act.wait_ge(h_turned[j], i + 1 + OPEN)
                        act.activation(hmT[:, j].rearrange("p c n -> p (c n)"), hp[:, 0:FC * SLOT],
                                       ACT.Copy).then_inc(h_kept[j], 1)
                        act.wait_ge(y_made[j], i + 1 + OPEN)
                        act.wait_ge(y_left[j], i + OPEN)
                        act.activation(yg[:, j, 0:512], yp[:, 0], ACT.Copy).then_inc(y_lo[j], 1)
                passes(act, body)

            @block.vector
            def _(dve):
                for sem in (*x_kept, *h_made, *y_hi,):
                    dve.sem_inc(sem, OPEN)
                def lay(dst, n, i, j, sem):
                    dve.tensor_copy(dst[:, j, :], k.index[:, n, bass.ds(i * 2 + j, 1)]).then_inc(sem[j], 1)

                def x_up(i, j):
                    dve.wait_ge(turned[j], i + 1)
                    dve.wait_ge(gu_made[j], i + OPEN)
                    dve.tensor_tensor(xT[:, j], xp[:], k.g_ffn[:].unsqueeze(2).to_broadcast([P, KC, SLOT]),
                                      ALU.mult).then_inc(x_kept[j], 1)

                def body(i, further):
                    for j in range(2):
                        dve.wait_ge(x_in[j], i * 16 + 16)
                        lay(from_row, 1, i + 1, j, from_laid)
                        dve.wait_ge(y_left[j], i + OPEN)
                        lay(to_row, 0, i, j, to_laid)
                    for j in range(2):
                        dve.wait_ge(silu_made[j], i + 1)
                        dve.wait_ge(h_turned[j], i + OPEN)
                        dve.tensor_tensor(hm[:, j], sg[:, j], gp[:, j, 1], ALU.mult).then_inc(h_made[j], 1)
                    for j in range(2):
                        x_up(i + 1, j)
                    for j in range(2):
                        dve.wait_ge(y_made[j], i + 1 + OPEN)
                        dve.wait_ge(y_left[j], i + OPEN)
                        dve.tensor_copy(yg[:, j, 512:D], yp[:, 1]).then_inc(y_hi[j], 1)

                dve.memset(xg[:], 0.0).then_inc(cleared, 1)
                for j in range(2):
                    lay(from_row, 1, 0, j, from_laid)
                for j in range(2):
                    x_up(0, j)
                passes(dve, body)

            @block.tensor
            def _(pe):
                for sem in (*gu_made, *y_made, *h_turned,):
                    pe.sem_inc(sem, OPEN)
                def turn(i, j):
                    pe.wait_ge(x_in[j], i * 16 + 16)
                    if j:
                        pe.wait_ge(x_kept[0], i + 1 + OPEN)
                    else:
                        pe.wait_ge(x_kept[1], i + OPEN)
                    pe.sem_inc(go_pe, 1)
                    v = xg[:, j, :].rearrange("t (p c) -> t c p", c=KC)
                    for c in range(KC):
                        last = pe.transpose(xp[:, c, :], v[:, c, :], k.const("ident", SLOT)[:, 0:SLOT])
                    last.then_inc(turned[j], 1)

                def body(i, further):
                    for j in range(2):
                        pe.wait_ge(x_kept[j], i + 1 + OPEN)
                        pe.wait_ge(gu_in[j], i * 32 + 32)
                        pe.wait_ge(h_made[j], i + OPEN)
                        for n in range(2):
                            for c in range(KC):
                                last = pe.matmul(gp[:, j, n], xT[:, j, c, :], wgu[:, j, n, c, :], start=(c == 0),
                                                 stop=(c == KC - 1))
                        last.then_inc(gu_made[j], 1)
                    for j in range(2):
                        turn(i + 1, j)
                    for j in range(2):
                        pe.wait_ge(h_made[j], i + 1 + OPEN)
                        pe.wait_ge(h_kept[1 - j], i + j + OPEN)
                        pe.sem_inc(go_pe, 1)
                        v = hm[:, j, :].rearrange("t (p c) -> t c p", c=FC)
                        for c in range(FC):
                            last = pe.transpose(hp[:, c * SLOT:(c + 1) * SLOT], v[:, c, :],
                                                k.const("ident", SLOT)[:, 0:SLOT])
                        last.then_inc(h_turned[j], 1)
                        pe.wait_ge(h_kept[j], i + 1 + OPEN)
                        pe.wait_ge(d_in[j], i * 16 + 16)
                        pe.wait_ge(y_lo[1 - j], i + j + OPEN)
                        pe.wait_ge(y_hi[1 - j], i + j + OPEN)
                        for h in range(2):
                            for c in range(FC):
                                last = pe.matmul(yp[:, h], hmT[:, j, c, :], wd[:, j, c, h * 512:(h + 1) * 512],
                                                 start=(c == 0), stop=(c == FC - 1))
                        last.then_inc(y_made[j], 1)

                for j in range(2):
                    turn(0, j)
                passes(pe, body)


def finish(k):
    nc = k.nc
    with ExitStack() as ctx:
        two = k.sb("fn_two", [P, NBLK, 2, D], ctx=ctx)
        gf = k.sb("fn_gf", [P, D], ctx=ctx)
        junk = k.sb("fn_junk", [P, D], ctx=ctx)
        ms = k.sb("fn_ms", [P, NBLK], ctx=ctx)
        rms = k.sb("fn_rms", [P, NBLK], ctx=ctx)
        rstd = k.sb("fn_rstd", [P, NBLK], ctx=ctx)
        two_in = [k.sem(f"fn_in{b}", ctx) for b in range(NBLK)]
        s = {n: k.sem("fn_" + n, ctx) for n in ("added", "squares", "roots", "scaled", "out")}
        own = k.sem("fn_dve", ctx)
        gf_in = k.pool_sem("fn_gf_in")
        with nc.Block() as block:

            @block.sync
            def _(sp):
                for b in range(NBLK):
                    r = rows_of(b)
                    sp.dma_start(two[0:r, b], k.io["pairs"].rearrange("(t k) n -> t k n", k=2)[b * P:b * P + r])\
                        .then_inc(two_in[b], 16)
                for b in range(NBLK):
                    r = rows_of(b)
                    out = k.io["o_y"][b * P:(b + 1) * P, :] if b < NB else k.io["o_ys"]
                    sp.wait_ge(s["scaled"], b + 1)
                    sp.dma_start(out, k.x1[0:r, b, :]).then_inc(s["out"], 16)
                sp.wait_ge(s["out"], 16 * NBLK)

            @block.gpsimd
            def _(pool):
                pool.dma_start(gf[:], k.io["g_final"].partition_broadcast(P)).then_inc(gf_in, 16)

            @block.vector
            def _(dve):
                link = Chain(dve, own)
                for b in range(NBLK):
                    r = rows_of(b)
                    x = k.x1[0:r, b, :]
                    dve.wait_ge(two_in[b], 16)
                    link(dve.scalar_tensor_tensor(x, two[0:r, b, 0, :], k.gate[0:r, b, 0:1], x, ALU.mult, ALU.add))
                    dve.scalar_tensor_tensor(x, two[0:r, b, 1, :], k.gate[0:r, b, 1:2], x, ALU.mult,
                                             ALU.add).then_inc(s["added"], 1)
                dve.wait_ge(gf_in, 16)
                for b in range(NBLK):
                    r = rows_of(b)
                    x = k.x1[0:r, b, :]
                    dve.wait_ge(s["roots"], b + 1)
                    link(dve.reciprocal(rstd[0:r, b:b + 1], rms[0:r, b:b + 1]))
                    dve.scalar_tensor_tensor(x, x, rstd[0:r, b:b + 1], gf[0:r, :], ALU.mult,
                                             ALU.mult).then_inc(s["scaled"], 1)

            @block.scalar
            def _(act):
                for b in range(NBLK):
                    r = rows_of(b)
                    act.wait_ge(s["added"], b + 1)
                    act.activation(junk[0:r, :], k.x1[0:r, b, :], ACT.Square,
                                   accum_out=ms[0:r, b:b + 1]).then_inc(s["squares"], 1)
                    act.wait_ge(s["squares"], b + 1)
                for b in range(NBLK):
                    r = rows_of(b)
                    act.activation(rms[0:r, b:b + 1], ms[0:r, b:b + 1], ACT.Sqrt, bias=k.const("eps", r),
                                   scale=1.0 / D).then_inc(s["roots"], 1)


STEPS = [prepare, project, weigh_a, attend_a, attend_b, decode_b, merge, route, experts, finish]


INPUTS = ["x_prompt", "x_sample", "cache_k_a", "cache_v_a", "page_table", "cache_kv_b0", "cache_kv_b1", "cache_kv_b2",
          "g_attn", "w_in", "b_sb", "w_br_a", "w_br_b", "w_o", "g_ffn", "w_group", "b_group", "w_expert", "b_expert",
          "w_gate_e", "w_up_e", "w_down_e", "g_final"]


def outputs():
    out = [("o_y", (SEQ, D)), ("o_ys", (DEC, D)), ("o_ka", (SEQ, WA)), ("o_va", (SEQ, WA)),
           ("o_kas", (DEC, WA)), ("o_vas", (DEC, WA))]
    out += [(f"o_kvp{g}", (min(w, SEQ), 2 * WBO)) for g, (w, _) in enumerate(GROUPS)]
    out += [(f"o_kvs{g}", (DEC, w, 2 * WBO)) for g, (w, _) in enumerate(GROUPS)]
    return out


def build(nc, io, at, stop=99):
    with ExitStack() as ctx:
        k = Kernel(nc, ctx, io, at)
        k.consts = k.sb("consts_sb", [P, io["consts"].shape[1]])
        k.g_attn = k.sb("g_attn_sb", [P, KC])
        k.g_ffn = k.sb("g_ffn_sb", [P, KC])
        k.b_sb = k.sb("b_sb_sb", [P, HA])
        k.pages = k.sb("pages_sb", [1, DEC * PAGES], I32)
        k.hT = k.sb("hT", [P, KC, TOK])
        k.shifted = ctx.enter_context(nc.semaphore("shifted"))
        steps = STEPS[:stop]
        k.oT = k.sb("oT", [P, (WA + WBO) // P, TOK])
        with ExitStack() as inner:
            k.qk = k.sb("qk", [P, QK_TILES, SEQ], ctx=inner)
            k.v_rows = k.sb("v_rows", [P, NB, WA + WB], ctx=inner)
            k.samp = k.sb("samp", [DEC, TILES * P], ctx=inner)
            k.scores = k.sb("scores", [P, DEC, HA, PAGES], ctx=inner)
            with ExitStack() as ringed:
                k.ring = k.sb("ring", [P, RING, PPG, WA], ctx=ringed)
                for f in steps[:4]:
                    f(k)
            for f in steps[4:6]:
                f(k)
        k.x1 = k.sb("x1", [P, NBLK, D])
        k.gate = k.sb("gate", [P, NBLK, 2])
        k.index = k.sb("index", [SLOT, 2, ALL_SLOTS + 2], U32)
        k.owner = k.sb("owner", [1, MORE], I32)
        k.n_more = k.sb("n_more", [1, 1], I32)
        for f in steps[6:8]:
            f(k)
        k.clear_semaphores()
        for f in steps[8:]:
            f(k)
        if stop > 1:
            with nc.Block() as block:
                @block.sync
                def _(sp):
                    sp.wait_ge(k.shifted, 16 * NG)


def kernel(**inputs):
    import concourse.bacc as bacc
    from concourse.bass_utils import run_bass_kernel_spmd

    nc = bacc.Bacc("TRN2", target_bir_lowering=False, num_devices=1)
    at, consts = constants()
    arrays = {"in_consts": consts}
    io = {"consts": nc.dram_tensor("in_consts", consts.shape, F32, kind="ExternalInput").ap()}
    for name in INPUTS:
        a = np.ascontiguousarray(inputs[name])
        arrays[f"in_{name}"] = a
        io[name] = nc.dram_tensor(f"in_{name}", a.shape, mybir.dt.from_np(a.dtype), kind="ExternalInput").ap()
    for name, shape in outputs():
        io[name] = nc.dram_tensor(name, shape, F32, kind="ExternalOutput").ap()
    io["h2"] = nc.dram_tensor("h2_rows", (TOK, D), F32).ap()
    io["pairs"] = nc.dram_tensor("pair_rows", (2 * TOK, D), F32).ap()
    build(nc, io, at)
    got = run_bass_kernel_spmd(nc, [arrays], core_ids=[0]).results[0]
    g = [got[name] for name, _ in outputs()]
    kv = (2, SLOTS_B, HD)
    return (g[0].reshape(1, SEQ, D), g[1].reshape(DEC, 1, D),
            g[2].reshape(1, 1, SEQ, HA, HD), g[3].reshape(1, 1, SEQ, HA, HD),
            g[4].reshape(1, DEC, 1, HA, HD), g[5].reshape(1, DEC, 1, HA, HD),
            *(g[6 + n].reshape(1, 1, min(w, SEQ), *kv) for n, (w, _) in enumerate(GROUPS)),
            *(g[9 + n].reshape(1, DEC, w, *kv) for n, (w, _) in enumerate(GROUPS)))
```

```python
from contextlib import ExitStack

import numpy as np

import concourse.bass as bass
from concourse import mybir

F32 = mybir.dt.float32
F32R = mybir.dt.float32r
I32 = mybir.dt.int32
U32 = mybir.dt.uint32
ALU = mybir.AluOpType
ACT = mybir.ActivationFunctionType
AX = mybir.AxisListType.X

P = 128
D = 1024
KC = D // P
SEQ = 512
NB = SEQ // P
DEC = 8
TOK = SEQ + DEC
HD = 64
HA = 8
WA = HA * HD
SLOTS_B = 4
GROUPS = ((128, 1), (512, 4), (2048, 16))
NG = len(GROUPS)
HB = NG * SLOTS_B
WB = HB * HD
WBO = SLOTS_B * HD
PAGES = 32
PPG = 4
PPV = 2
RING = 4
RAW = 8
TILES = (3 * WA + 3 * WB) // P
GATE_TILES = 2 * D // P
QK_TILES = 2 * (WA + WB) // P
SCALE = HD ** -0.5
EPS = 1e-6
CLAMP = 30.0
EXPERTS = 32
E_GROUPS = 4
E_PER = EXPERTS // E_GROUPS
FF = 512
FC = FF // P
SLOT = 64
MORE = 16
ALL_SLOTS = EXPERTS + MORE
HALVES = 6
HALF = KC // 2 * FF
SPLITS = 4
NONE = 1 << 20
FAR = 1e30
OPEN = 1
NBLK = NB + 1

SLOPES = [[2.0 ** (-8.0 * (g * SLOTS_B + s + 1) / HB) for s in range(SLOTS_B)] for g in range(NG)]


def constants():
    p = np.arange(P)[:, None]
    f = np.arange(P)[None, :]
    u = np.arange(SEQ)[None, :]
    rel = p - u + (SEQ - P)
    t = np.arange(NBLK)[None, :] * P + p
    parts = {
        "ident": (p == f),
        "later_eq": (p >= f),
        "before": (p < f),
        "ones": np.ones((P, P)),
        "own_head": (np.arange(WA)[None, :] // HD == p % HA),
        "rel": np.concatenate([
            np.where((rel >= 0) & (rel <= w) & (rel % d == 0), rel, FAR) if d > 1 else
            np.where((rel >= 0) & (rel <= w), rel, FAR) for w, d in GROUPS], axis=1),
        "slope": np.broadcast_to(-np.array(SLOPES).reshape(1, HB) / SCALE, (P, HB)),
        "row_bias": np.concatenate([-np.array(SLOPES[g])[None, :] * d * (P - p)
                                    for g, (_, d) in enumerate(GROUPS)], axis=1),
        "own_sample": (p // SLOTS_B == np.arange(DEC)[None, :]),
        "iota": np.broadcast_to(np.arange(SLOT)[None, :], (P, SLOT)),
        "steps": np.broadcast_to(SLOT * (np.arange(TOK // SLOT)[None, :] + 1), (P, TOK // SLOT)),
        "pair0": (2 * t + 1) * (t < TOK),
        "pair1": (2 * t + 2) * (t < TOK),
        "token": (t + 1) * (t < TOK),
        "real": (t < TOK),
        "eps": np.full((P, 1), EPS),
    }
    at, cols, n = {}, [], 0
    for name, a in parts.items():
        a = np.asarray(a, np.float32)
        at[name] = (n, n + a.shape[1])
        n += a.shape[1]
        cols.append(a)
    return at, np.ascontiguousarray(np.concatenate(cols, axis=1))


class Chain:

    def __init__(self, eng, sem):
        self.eng, self.sem, self.base, self.k = eng, sem, 0, 0

    def __call__(self, ins):
        self.k += 1
        ins.then_inc(self.sem, 1)
        self.eng.wait_ge(self.sem, self.base + self.k)

    def enter(self, i, per):
        self.before = self.base + self.k
        self.base, self.k = self.before + i * per, 0

    def leave(self, per, trips):
        assert self.k == per, (self.k, per)
        self.base, self.k = self.before + per * trips, 0


class Kernel:

    def __init__(self, nc, ctx, io, at):
        self.nc, self.ctx, self.io, self.at, self.sems = nc, ctx, io, at, []

    def sb(self, name, shape, dt=F32, ctx=None):
        return (ctx or self.ctx).enter_context(self.nc.sbuf_tensor(name, shape, dt))

    def ps(self, name, shape, ctx):
        return ctx.enter_context(self.nc.psum_tensor(name, shape, F32))

    def sem(self, name, ctx):
        sem = ctx.enter_context(self.nc.semaphore(name))
        self.sems.append(sem)
        return sem

    def pool_sem(self, name):
        return self.ctx.enter_context(self.nc.semaphore(name))

    def clear_semaphores(self):
        with self.nc.Block() as block:

            @block.gpsimd
            def _(pool):
                for sem in self.sems:
                    pool.sem_clear(sem)
        self.sems = []

    def const(self, name, rows=P):
        a, b = self.at[name]
        return self.consts[0:rows, a:b]


def rows_of(blk):
    return P if blk < NB else DEC


def x_rows(k, blk):
    return k.io["x_prompt"][0, blk * P:(blk + 1) * P, :] if blk < NB else k.io["x_sample"][:, 0, :]


def prepare(k):
    nc = k.nc
    with ExitStack() as ctx:
        x = k.sb("prep_x", [P, NBLK, D], ctx=ctx)
        junk = k.sb("prep_junk", [P, D], ctx=ctx)
        ms = k.sb("prep_ms", [P, NBLK], ctx=ctx)
        rms = k.sb("prep_rms", [P, NBLK], ctx=ctx)
        rstd = k.sb("prep_rstd", [P, NBLK], ctx=ctx)
        tr = k.ps("prep_tr", [P, 2, KC, P], ctx)
        consts_in = k.pool_sem("consts_in")
        x_in = [k.sem(f"x_in{b}", ctx) for b in range(NBLK)]
        squares = k.sem("squares", ctx)
        roots = k.sem("roots", ctx)
        scaled = k.sem("scaled", ctx)
        turned = k.sem("turned", ctx)
        placed = k.sem("placed", ctx)
        own = k.sem("prep_dve", ctx)
        with nc.Block() as block:

            @block.sync
            def _(sp):
                for b in range(NBLK):
                    sp.dma_start(x[0:rows_of(b), b, :], x_rows(k, b)).then_inc(x_in[b], 16)

            @block.gpsimd
            def _(pool):
                pool.dma_start(k.consts[:], k.io["consts"]).then_inc(consts_in, 16)
                pool.dma_start(k.g_attn[:], k.io["g_attn"][0].rearrange("(p c) -> p c", c=KC)).then_inc(consts_in, 16)
                pool.dma_start(k.b_sb[:], k.io["b_sb"][0].partition_broadcast(P)).then_inc(consts_in, 16)
                pool.dma_start(k.pages[:], k.io["page_table"].rearrange("b n -> (b n)").unsqueeze(0))\
                    .then_inc(consts_in, 16)
                pool.wait_ge(consts_in, 64)

            @block.scalar
            def _(act):
                for b in range(NBLK):
                    r = rows_of(b)
                    act.wait_ge(x_in[b], 16)
                    act.activation(junk[0:r, :], x[0:r, b, :], ACT.Square,
                                   accum_out=ms[0:r, b:b + 1]).then_inc(squares, 1)
                    act.wait_ge(squares, b + 1)
                act.wait_ge(consts_in, 64)
                for b in range(NBLK):
                    r = rows_of(b)
                    act.activation(rms[0:r, b:b + 1], ms[0:r, b:b + 1], ACT.Sqrt,
                                   bias=k.const("eps", r), scale=1.0 / D).then_inc(roots, 1)

            @block.vector
            def _(dve):
                link = Chain(dve, own)
                for b in range(NBLK):
                    r = rows_of(b)
                    dve.wait_ge(roots, b + 1)
                    link(dve.reciprocal(rstd[0:r, b:b + 1], rms[0:r, b:b + 1]))
                    dve.tensor_scalar(x[0:r, b, :], x[0:r, b, :], rstd[0:r, b:b + 1], None,
                                      ALU.mult).then_inc(scaled, 1)
                dve.wait_ge(consts_in, 64)
                for b in range(NBLK):
                    r = rows_of(b)
                    dve.wait_ge(turned, b + 1)
                    dve.tensor_tensor(k.hT[:, :, b * P:b * P + r], tr[:, b % 2, :, 0:r],
                                      k.g_attn[:].unsqueeze(2).to_broadcast([P, KC, r]),
                                      ALU.mult).then_inc(placed, 1)
                dve.wait_ge(placed, NBLK)

            @block.tensor
            def _(pe):
                pe.wait_ge(consts_in, 64)
                for b in range(NBLK):
                    r = rows_of(b)
                    pe.wait_ge(scaled, b + 1)
                    if b >= 2:
                        pe.wait_ge(placed, b - 1)
                    v = x[0:r, b, :].rearrange("t (p c) -> t c p", c=KC)
                    for c in range(KC):
                        last = pe.transpose(tr[:, b % 2, c, 0:r], v[:, c, :], k.const("ident", r)[:, 0:r])
                    last.then_inc(turned, 1)


def load_pages(k, eng, b, g, cache, ring, ring_in):
    per = ring.shape[2]
    s = g % ring.shape[1]
    for j in range(per):
        page = eng.value_load(k.pages[0:1, bass.ds(b * PAGES + (g * per + j), 1)],
                              min_val=0, max_val=cache.shape[1] - 1)
        eng.dma_start(ring[:, s, per - 1 - j, :], cache[0, bass.ds(page, 1)].rearrange("a p h d -> (a p) (h d)"))\
            .then_inc(ring_in[s], 16)


def project(k):
    nc = k.nc
    with ExitStack() as ctx:
        ring = k.sb("k_ring", [P, RING, PPG, WA], ctx=ctx)
        w = k.sb("w_slot", [P, 2, KC, P], ctx=ctx)
        stage = k.sb("stage", [P, 2, TOK], ctx=ctx)
        krows = k.sb("k_rows", [P, NB, WB], ctx=ctx)
        qrep = k.sb("q_rep", [P, DEC, WA], ctx=ctx)
        prod = k.sb("prod", [P, PPG, WA], ctx=ctx)
        pp = k.ps("proj_ps", [P, 2, 2, 512], ctx)
        tp = k.ps("turn_ps", [P, 2, 512], ctx)
        ts = k.ps("turn_sample_ps", [P, 2, 512], ctx)
        rp = tp[:, 0, :]
        w_in = [k.sem(f"w_in{j}", ctx) for j in range(2)]
        made = [k.sem(f"made{j}", ctx) for j in range(2)]
        staged = [k.sem(f"staged{j}", ctx) for j in range(2)]
        turned = [k.sem(f"q_turned{j}", ctx) for j in range(2)]
        laid = [k.sem(f"laid{j}", ctx) for j in range(2)]
        kept = [k.sem(f"kept{j}", ctx) for j in range(2)]
        k_out = k.sem("k_out", ctx)
        v_out = k.sem("v_out", ctx)
        gate_out = [k.sem(f"gate_out{j}", ctx) for j in range(2)]
        rep = k.sem("rep", ctx)
        rep_laid = k.sem("rep_laid", ctx)
        ring_in = [k.sem(f"k_ring_in{s}", ctx) for s in range(RING)]
        ring_used = [k.sem(f"k_ring_used{s}", ctx) for s in range(RING)]
        own = k.sem("proj_dve", ctx)
        H = TOK // 2
        io = k.io
        secs = [(0, 4, None, 0), (4, 4, "k", 1), (8, 4, "v", 2), (12, 6, None, 0), (18, 6, "k", 1), (24, 6, "v", 2)]

        def tiles_loop(eng, t0, n, body):
            with eng.Fori(0, n // 2) as i:
                body(i + t0 // 2, i)

        with nc.Block() as block:

            @block.sync
            def _(sp):
                with sp.Fori(0, DEC) as b:
                    for g in range(PAGES // PPG):
                        sp.wait_ge(ring_used[g % RING], b * (PAGES // PPG // RING) + g // RING + OPEN)
                        load_pages(k, sp, b, g, io["cache_k_a"], ring, ring_in)

            @block.scalar
            def _(act):
                for sem in (*staged, *laid, *gate_out):
                    act.sem_inc(sem, OPEN)
                def load(m, j):
                    act.dma_start(w[:, j], io["w_in"][0].rearrange("(p c) n -> p c n", c=KC)[
                        :, :, bass.ds(m * (2 * P) + j * P, P)]).then_inc(w_in[j], 16)

                for j in range(2):
                    load(0, j)
                for t0, n, what, kind in secs:
                    wide = n * P
                    if what == "k":
                        rows = krows[:, :, 0:wide]
                        if t0 > 4:
                            act.wait_ge(k_out, 16)
                    elif what == "v":
                        rows = k.v_rows[:, :, 0:WA] if wide == WA else k.v_rows[:, :, WA:WA + WB]

                    def body(m, i):
                        for j in range(2):
                            act.wait_ge(made[j], m + 1)
                            load(m + 1, j)
                            act.wait_ge(turned[j], m + OPEN)
                            act.wait_ge(kept[j], m + OPEN)
                            act.activation(stage[:, j, :].rearrange("p (a n) -> p a n", a=2), pp[:, j, :, 0:H],
                                           ACT.Copy).then_inc(staged[j], 1)
                        for j in range(2):
                            act.wait_ge(turned[j], m + 1 + OPEN)
                            if what:
                                act.activation(rows[:, :, bass.ds(i * (2 * P) + j * P, P)],
                                               tp[:, j, :].rearrange("p (b n) -> p b n", b=NB),
                                               ACT.Copy).then_inc(laid[j], 1)
                            else:
                                act.sem_inc(laid[j], 1)
                            act.activation(k.samp[0:DEC, bass.ds(m * (2 * P) + j * P, P)],
                                           ts[0:DEC, j, 0:P], ACT.Copy).then_inc(laid[j], 1)

                    tiles_loop(act, t0, n, body)
                    for j in range(2):
                        act.wait_ge(laid[j], t0 + n + OPEN)
                    if what == "k":
                        if wide == WA:
                            act.dma_start(io["o_ka"].rearrange("(b p) n -> p b n", p=P), rows).then_inc(k_out, 16)
                        else:
                            for g in range(NG):
                                keep = min(GROUPS[g][0], SEQ) // P
                                act.dma_start(io[f"o_kvp{g}"][:, 0:WBO].rearrange("(b p) n -> p b n", p=P),
                                              rows[:, NB - keep:NB, g * WBO:(g + 1) * WBO]).then_inc(k_out, 16)
                    elif what == "v":
                        if wide == WA:
                            act.dma_start(io["o_va"].rearrange("(b p) n -> p b n", p=P), rows).then_inc(v_out, 16)
                        else:
                            for g in range(NG):
                                keep = min(GROUPS[g][0], SEQ) // P
                                act.dma_start(io[f"o_kvp{g}"][:, WBO:2 * WBO].rearrange("(b p) n -> p b n", p=P),
                                              rows[:, NB - keep:NB, g * WBO:(g + 1) * WBO]).then_inc(v_out, 16)
                    if t0 == 0:
                        for b in range(DEC):
                            act.wait_ge(rep, b + 1)
                            act.activation(qrep[:, b, :], rp, ACT.Copy).then_inc(rep_laid, 1)
                act.dma_start(io["o_kas"], k.samp[0:DEC, WA:2 * WA]).then_inc(k_out, 16)
                act.dma_start(io["o_vas"], k.samp[0:DEC, 2 * WA:3 * WA]).then_inc(v_out, 16)
                for g, (wlen, _) in enumerate(GROUPS):
                    for c, s in ((0, k_out), (1, v_out)):
                        at = 3 * WA + (1 + c) * WB + g * WBO
                        act.dma_start(io[f"o_kvs{g}"][:, wlen - 1, c * WBO:(c + 1) * WBO],
                                      k.samp[0:DEC, at:at + WBO]).then_inc(s, 16)

                def gate(i, last=False):
                    m = i + TILES // 2
                    for j in range(2):
                        act.wait_ge(made[j], m + 1)
                        if not last:
                            load(m + 1, j)
                        act.wait_ge(gate_out[j], i * 16 + OPEN)
                        act.activation(stage[:, j, :].rearrange("p (a n) -> p a n", a=2), pp[:, j, :, 0:H],
                                       ACT.Sigmoid).then_inc(staged[j], 1)
                    for j in range(2):
                        act.wait_ge(staged[j], m + 1 + OPEN)
                        act.dma_start(io["gates"][:, bass.ds(i * 2 + j, 1), :].rearrange("p a n -> p (a n)"),
                                      stage[:, j, :]).then_inc(gate_out[j], 16)

                with act.Fori(0, GATE_TILES // 2 - 1) as i:
                    gate(i)
                gate(GATE_TILES // 2 - 1, last=True)
                for j in range(2):
                    act.wait_ge(gate_out[j], 16 * (GATE_TILES // 2) + OPEN)
                act.wait_ge(k_out, 16 * (2 + 2 * NG))
                act.wait_ge(v_out, 16 * (2 + 2 * NG))

            @block.gpsimd
            def _(pool):
                for sem in (*kept,):
                    pool.sem_inc(sem, OPEN)
                at = 0
                for t0, n, what, kind in secs:
                    def body(m, i):
                        for j in range(2):
                            pool.wait_ge(staged[j], m + 1 + OPEN)
                            if what == "v":
                                pool.sem_inc(kept[j], 1)
                            else:
                                pool.tensor_copy(k.qk[:, bass.ds(i * 2 + (at + j), 1), :].rearrange(
                                    "p a n -> p (a n)"), stage[:, j, 0:SEQ]).then_inc(kept[j], 1)
                    tiles_loop(pool, t0, n, body)
                    if what != "v":
                        at += n

            @block.tensor
            def _(pe):
                for sem in (*turned,):
                    pe.sem_inc(sem, OPEN)

                def make(m):
                    for j in range(2):
                        pe.wait_ge(w_in[j], (m + 1) * 16)
                        pe.wait_ge(staged[j], m + OPEN)
                        for half in range(2):
                            for c in range(KC):
                                last = pe.matmul(pp[:, j, half, 0:H], w[:, j, c, :],
                                                 k.hT[:, c, half * H:(half + 1) * H],
                                                 start=(c == 0), stop=(c == KC - 1))
                        last.then_inc(made[j], 1)

                for t0, n, what, kind in secs:
                    def body(m, i):
                        make(m)
                        for j in range(2):
                            pe.wait_ge(staged[j], m + 1 + OPEN)
                            pe.wait_ge(laid[j], m * 2 + OPEN)
                            if what:
                                for b in range(NB):
                                    pe.transpose(tp[:, j, b * P:(b + 1) * P], stage[:, j, b * P:(b + 1) * P],
                                                 k.const("ident"))
                            pe.transpose(ts[0:DEC, j, 0:P], stage[:, j, SEQ:TOK],
                                         k.const("ident")).then_inc(turned[j], 1)
                    tiles_loop(pe, t0, n, body)
                    if t0 == 0:
                        for j in range(2):
                            pe.wait_ge(laid[j], n + OPEN)
                        for b in range(DEC):
                            if b:
                                pe.wait_ge(rep_laid, b)
                            pe.matmul(rp, k.const("ident", DEC)[:, b:b + 1].to_broadcast([DEC, P]),
                                      k.samp[0:DEC, 0:WA], start=True, stop=True).then_inc(rep, 1)
                        pe.wait_ge(rep_laid, DEC)
                with pe.Fori(TILES // 2, (TILES + GATE_TILES) // 2) as m:
                    make(m)

            @block.vector
            def _(dve):
                for sem in (*ring_used,):
                    dve.sem_inc(sem, OPEN)
                link = Chain(dve, own)
                dve.wait_ge(rep_laid, DEC)
                per = PAGES // PPG
                with dve.Fori(0, DEC) as b:
                    link.enter(b, per)
                    for g in range(per):
                        s = g % RING
                        dve.wait_ge(ring_in[s], b * (32 * PPG) + 16 * PPG * (g // RING + 1))
                        link_ready = dve.tensor_tensor(
                            prod[:, :, :], ring[:, s, :, :],
                            qrep[:, bass.ds(b, 1), :].to_broadcast([P, PPG, WA]), ALU.mult)
                        link_ready.then_inc(ring_used[s], 1)
                        dve.wait_ge(ring_used[s], b * 2 + (g // RING + 1) + OPEN)
                        at = PAGES - PPG * (g + 1)
                        link(dve.tensor_reduce(
                            k.scores[:, bass.ds(b, 1), :, at:at + PPG].rearrange("p a h j -> p j (a h)"),
                            prod[:, :, :].rearrange("p j (h d) -> p j h d", d=HD), axis=AX, op=ALU.add))
                    link.leave(per, DEC)


def weigh_a(k):
    nc = k.nc
    N = DEC * HA * PAGES
    with ExitStack() as ctx:
        t = k.sb("wa_t", [P, N], ctx=ctx)
        later = k.sb("wa_later", [P, DEC * HA, PAGES], ctx=ctx)
        keep = k.sb("wa_keep", [P, DEC * HA, PAGES], ctx=ctx)
        within = k.ps("wa_within", [P, N], ctx)
        totals = k.ps("wa_totals", [P, N], ctx)
        own = k.sem("wa_dve", ctx)
        clamped = k.sem("wa_clamped", ctx)
        exped = k.sem("wa_exped", ctx)
        logged = k.sem("wa_logged", ctx)
        soft = k.sem("wa_soft", ctx)
        summed = k.sem("wa_summed", ctx)
        arg = k.sem("wa_arg", ctx)
        weighed = k.sem("wa_weighed", ctx)
        z = k.scores[:].rearrange("p b h n -> p (b h n)")
        zv = k.scores[:].rearrange("p b h n -> p b h n")
        with nc.Block() as block:

            @block.vector
            def _(dve):
                link = Chain(dve, own)
                bias = k.b_sb[:].unsqueeze(2).to_broadcast([P, HA, PAGES])
                for b in range(DEC):
                    last = dve.scalar_tensor_tensor(zv[:, b], zv[:, b], SCALE, bias, ALU.mult, ALU.add)
                link(last)
                dve.tensor_scalar(t[:], z, CLAMP, None, ALU.min).then_inc(clamped, 1)
                link(dve.memset(keep[:], 1.0))
                link(dve.memset(keep[:, :, 0:1], 0.0))
                link(dve.memset(later[:, :, 0:1], 0.0))
                dve.wait_ge(logged, 1)
                dve.tensor_tensor(t[:], z, t[:], ALU.max).then_inc(soft, 1)
                dve.wait_ge(summed, 2)
                link(dve.tensor_copy(later[:, :, 1:PAGES],
                                     totals[:].rearrange("p (a n) -> p a n", n=PAGES)[:, :, 0:PAGES - 1]))
                lf = later[:].rearrange("p a n -> p (a n)")
                link(dve.tensor_tensor_scan(lf, keep[:].rearrange("p a n -> p (a n)"), lf, 0.0, ALU.mult, ALU.add))
                link(dve.tensor_tensor(z, z, within[:], ALU.subtract))
                dve.tensor_tensor(z, z, lf, ALU.subtract).then_inc(arg, 1)

            @block.scalar
            def _(act):
                act.wait_ge(clamped, 1)
                act.activation(t[:], t[:], ACT.Exp).then_inc(exped, 1)
                act.wait_ge(exped, 1)
                act.activation(t[:], t[:], ACT.Ln, bias=k.const("ones")[:, 0:1]).then_inc(logged, 1)
                act.wait_ge(arg, 1)
                act.activation(z, z, ACT.Exp).then_inc(weighed, 1)
                act.wait_ge(weighed, 1)

            @block.tensor
            def _(pe):
                pe.wait_ge(soft, 1)
                for out, table in ((within, "later_eq"), (totals, "ones")):
                    for c in range(N // 512):
                        last = pe.matmul(out[:, c * 512:(c + 1) * 512], k.const(table), t[:, c * 512:(c + 1) * 512],
                                         start=True, stop=True)
                    last.then_inc(summed, 1)


def attend_a(k):
    nc = k.nc
    OFF = {0: 0, 1: SEQ, 3: SEQ + 3 * P, 2: 2 * SEQ}
    W = 2 * SEQ + 2 * P
    UNITS = PAGES // PPV
    EARLY, MID, LATE = range(0, 5), range(5, 10), range(10, UNITS)
    with ExitStack() as ctx:
        qs = k.sb("aa_q", [HD, 2, SEQ], ctx=ctx)
        ks = k.sb("aa_k", [HD, 2, SEQ], ctx=ctx)
        vs = k.sb("aa_v", [P, 2, NB, HD], ctx=ctx)
        z = k.sb("aa_z", [P, 2, W], ctx=ctx)
        sp_ = k.sb("aa_soft", [P, 2, W], ctx=ctx)
        w_cur = k.sb("aa_w", [P, 2, PAGES, 2, HA], F32R, ctx=ctx)
        om = k.sb("aa_own", [2 * HA, WA], ctx=ctx)
        raw = k.sb("aa_raw", [P, RAW, PPV, WA], ctx=ctx)
        hi = k.sb("aa_hi", [P, RING, PPV, WA], F32R, ctx=ctx)
        lo = k.sb("aa_lo", [P, RING, PPV, WA], F32R, ctx=ctx)
        zp = k.ps("aa_zp", [P, 2, 3 * SEQ], ctx)
        op = k.ps("aa_op", [P, SEQ], ctx)
        vp = k.ps("aa_vp", [P, WA], ctx)
        s = {n: k.sem("aa_" + n, ctx) for n in (
            "staged", "scored", "z_kept", "clamped", "exped", "logged", "soft", "masked", "summed", "arg_done",
            "exp_a", "a_masked", "o_made", "o_kept", "w_hi", "w_laid", "own_kept", "col_made", "col_kept")}
        own = k.sem("aa_pool", ctx)
        ring_in = [k.sem(f"v_ring_in{n}", ctx) for n in range(RAW)]
        hi_made = [k.sem(f"v_hi_made{n}", ctx) for n in range(RING)]
        lo_made = [k.sem(f"v_lo_made{n}", ctx) for n in range(RING)]
        split_used = [k.sem(f"v_split_used{n}", ctx) for n in range(RING)]
        FILLS = UNITS // RING
        TRIPS = HA // 2
        AHEAD = 7
        LO_OPEN = RAW // RING
        BY_ACT = range(RAW - 1, UNITS, RAW)

        def load(eng, b, u):
            eng.wait_ge(lo_made[u % RING], b * FILLS + u // RING + 1 - RAW // RING + LO_OPEN)
            load_pages(k, eng, b, u, k.io["cache_v_a"], raw, ring_in)

        with nc.Block() as block:

            @block.sync
            def _(sp):
                with sp.Fori(0, DEC) as b:
                    for u in range(UNITS):
                        if u not in BY_ACT:
                            load(sp, b, u)

            @block.gpsimd
            def _(pool):
                link = Chain(pool, own)

                def stage(i, j, n):
                    if n is not None:
                        pool.wait_ge(s["o_made"], n + OPEN)
                    rows = slice(j * HD, (j + 1) * HD)
                    link(pool.tensor_copy(qs[:, j, :], k.qk[rows, bass.ds(i, 1), :].rearrange("p a n -> p (a n)")))
                    link(pool.tensor_copy(ks[:, j, :], k.qk[rows, bass.ds(i + HA // 2, 1), :].rearrange(
                        "p a n -> p (a n)")))
                    link(pool.tensor_copy(vs[:, j], k.v_rows[:, :, bass.ds(i * P + j * HD, HD)]))
                    pool.sem_inc(s["staged"], 1)

                stage(0, 0, None)
                with pool.Fori(0, TRIPS) as i:
                    link.enter(i, 6)
                    for j in range(2):
                        h = i * 2 + j
                        stage(i + j, 1 - j, h)
                        pool.wait_ge(s["soft"], h + 1)
                        for kb in range(NB):
                            d = sp_[:, j, OFF[kb]:OFF[kb] + P]
                            last = pool.tensor_tensor(d, d, k.const("before"), ALU.mult)
                        last.then_inc(s["masked"], 1)
                        pool.wait_ge(s["exp_a"], h + 1)
                        for kb in range(NB):
                            d = z[:, j, OFF[kb]:OFF[kb] + P]
                            last = pool.tensor_tensor(d, d, k.const("before"), ALU.mult)
                        last.then_inc(s["a_masked"], 1)
                        pool.wait_ge(s["a_masked"], h + 1)
                    link.leave(6, TRIPS)

            @block.vector
            def _(dve):
                for sem in (s["arg_done"], s["own_kept"]):
                    dve.sem_inc(sem, OPEN)
                for sem in lo_made:
                    dve.sem_inc(sem, LO_OPEN)

                def low(h, units):
                    for u in units:
                        n = u % RING
                        dve.wait_ge(hi_made[n], h * FILLS + (u // RING + 1))
                        dve.tensor_tensor(lo[:, n], raw[:, u % RAW], hi[:, n], ALU.subtract).then_inc(lo_made[n], 1)

                with dve.Fori(0, TRIPS) as i:
                    for j in range(2):
                        h = i * 2 + j
                        dve.wait_ge(s["w_hi"], h + 1)
                        dve.tensor_tensor(w_cur[:, j, :, 1, :].rearrange("p n h -> p h n"),
                                          k.scores[:, bass.ds(h, 1)].rearrange("p a h n -> p (a h) n"),
                                          w_cur[:, j, :, 0, :].rearrange("p n h -> p h n"),
                                          ALU.subtract).then_inc(s["w_laid"], 1)
                        low(h, range(0, 1))
                        dve.wait_ge(s["scored"], h + 1)
                        dve.wait_ge(s["o_made"], i * 2 + OPEN)
                        dve.tensor_scalar(z[:, j], zp[:, j, 0:W], SCALE, k.b_sb[:, bass.ds(h, 1)],
                                          ALU.mult, ALU.add).then_inc(s["z_kept"], 1)
                        dve.wait_ge(s["z_kept"], h + 1)
                        dve.tensor_scalar(sp_[:, j], z[:, j], CLAMP, None, ALU.min).then_inc(s["clamped"], 1)
                        low(h, range(1, 4))
                        dve.wait_ge(s["logged"], h + 1)
                        dve.tensor_tensor(sp_[:, j], z[:, j], sp_[:, j], ALU.max).then_inc(s["soft"], 1)
                        low(h, range(4, 9))
                        dve.wait_ge(s["summed"], h + 1)
                        dve.tensor_tensor(z[:, j], z[:, j], zp[:, j, 0:W], ALU.subtract).then_inc(s["arg_done"], 1)
                        low(h, range(9, UNITS))
                        dve.wait_ge(split_used[RING - 1], h * FILLS + FILLS + OPEN)
                        dve.wait_ge(s["col_made"], h + OPEN)
                        dve.tensor_tensor(om[:], vp[0:2 * HA, :], k.const("own_head", 2 * HA), ALU.mult)\
                            .then_inc(s["own_kept"], 1)

            @block.scalar
            def _(act):
                for sem in (s["col_kept"],):
                    act.sem_inc(sem, OPEN)

                def high(h, units):
                    for u in units:
                        n = u % RING
                        act.wait_ge(ring_in[u % RAW], (h * (UNITS // RAW) + (u // RAW + 1)) * (16 * PPV))
                        act.wait_ge(split_used[n], h * FILLS + u // RING + OPEN)
                        act.activation(hi[:, n], raw[:, u % RAW], ACT.Copy).then_inc(hi_made[n], 1)
                        if u + AHEAD in BY_ACT:
                            load(act, h, u + AHEAD)

                with act.Fori(0, TRIPS) as i:
                    for j in range(2):
                        h = i * 2 + j
                        act.activation(w_cur[:, j, :, 0, :].rearrange("p n h -> p h n"),
                                       k.scores[:, bass.ds(h, 1)].rearrange("p a h n -> p (a h) n"),
                                       ACT.Copy).then_inc(s["w_hi"], 1)
                        high(h, range(0, 4))
                        act.wait_ge(s["clamped"], h + 1)
                        act.activation(sp_[:, j], sp_[:, j], ACT.Exp).then_inc(s["exped"], 1)
                        act.wait_ge(s["exped"], h + 1)
                        act.activation(sp_[:, j], sp_[:, j], ACT.Ln, bias=k.const("ones")[:, 0:1])\
                            .then_inc(s["logged"], 1)
                        high(h, range(4, 9))
                        act.wait_ge(s["arg_done"], h + 1 + OPEN)
                        act.activation(z[:, j], z[:, j], ACT.Exp).then_inc(s["exp_a"], 1)
                        high(h, range(9, UNITS))
                        act.wait_ge(s["o_made"], h + 1 + OPEN)
                        rows = slice(j * HD, (j + 1) * HD)
                        act.activation(k.oT[rows, bass.ds(i, 1), 0:SEQ].rearrange("p a n -> p (a n)"), op[rows, :],
                                       ACT.Copy).then_inc(s["o_kept"], 1)
                        act.wait_ge(s["col_made"], h + 1 + OPEN)
                        act.activation(k.oT[:, 0:WA // P, bass.ds(h + SEQ, 1)].rearrange("p c a -> p (c a)"),
                                       op[:, 0:WA // P], ACT.Copy).then_inc(s["col_kept"], 1)
                act.wait_ge(s["col_kept"], HA + OPEN)

            @block.tensor
            def _(pe):
                for sem in (*split_used, s["o_made"], s["col_made"],):
                    pe.sem_inc(sem, OPEN)
                with pe.Fori(0, TRIPS) as i:
                    for j in range(2):
                        h = i * 2 + j

                        def values(units):
                            for u in units:
                                n = u % RING
                                pe.wait_ge(lo_made[n], h * FILLS + (u // RING + 1) + LO_OPEN)
                                for m in range(PPV):
                                    page = PAGES - PPV * (u + 1) + m
                                    for part in (hi, lo):
                                        last = pe.matmul(
                                            vp[0:2 * HA, :], w_cur[:, j, page].rearrange("p a h -> p (a h)"),
                                            part[:, n, m, :], start=(u == m == 0 and part is hi),
                                            stop=(u == UNITS - 1 and m == PPV - 1 and part is lo))
                                last.then_inc(split_used[n], 1)

                        pe.wait_ge(s["staged"], h + 1)
                        pe.wait_ge(s["arg_done"], (h if j == 0 else h - 1) + OPEN)
                        for kb in range(NB):
                            n = SEQ - kb * P
                            last = pe.matmul(zp[:, j, OFF[kb]:OFF[kb] + n], ks[:, j, kb * P:(kb + 1) * P],
                                             qs[:, j, kb * P:SEQ], start=True, stop=True)
                        last.then_inc(s["scored"], 1)
                        pe.wait_ge(s["w_laid"], h + 1)
                        pe.wait_ge(s["own_kept"], h + OPEN)
                        values(EARLY)
                        pe.wait_ge(s["masked"], h + 1)
                        for kb in range(NB):
                            for kb2 in range(kb, NB):
                                n, at = SEQ - kb2 * P, OFF[kb] + (kb2 - kb) * P
                                last = pe.matmul(zp[:, j, at:at + n], k.const("later_eq" if kb2 == kb else "ones"),
                                                 sp_[:, j, OFF[kb2]:OFF[kb2] + n], start=(kb2 == kb),
                                                 stop=(kb2 == NB - 1), skip_group_check=True)
                        last.then_inc(s["summed"], 1)
                        values(MID)
                        pe.wait_ge(s["a_masked"], h + 1)
                        pe.wait_ge(s["col_kept"], h + OPEN)
                        for kb in range(NB):
                            last = pe.matmul(op[j * HD:(j + 1) * HD, kb * P:SEQ], vs[:, j, kb, :],
                                             z[:, j, OFF[kb]:OFF[kb] + SEQ - kb * P], start=(kb == 0),
                                             stop=(kb == NB - 1), skip_group_check=True)
                        last.then_inc(s["o_made"], 1)
                        values(LATE)
                        pe.wait_ge(s["own_kept"], h + 1 + OPEN)
                        pe.wait_ge(s["o_kept"], h + 1)
                        for c in range(WA // P):
                            last = pe.matmul(op[:, c:c + 1], om[:, c * P:(c + 1) * P], k.const("ones", 2 * HA)[:, 0:1],
                                             start=True, stop=True)
                        last.then_inc(s["col_made"], 1)


def attend_b(k):
    nc = k.nc
    FIRST = [lambda qb: max(qb - 1, 0), lambda qb: 0, lambda qb: 0]
    WMAX = (2 + 2 * NB) * P
    with ExitStack() as ctx:
        qs = k.sb("ab_q", [HD, 2, NG, SEQ], ctx=ctx)
        ks = k.sb("ab_k", [HD, 2, NG, SEQ], ctx=ctx)
        sc = k.sb("ab_sc", [P, 2, WMAX], ctx=ctx)
        pt = k.sb("ab_pt", [P, WMAX], ctx=ctx)
        y = k.sb("ab_y", [P, NB, WBO], ctx=ctx)
        mx = k.sb("ab_mx", [P, 4], ctx=ctx)
        nm = k.sb("ab_nm", [P, 2], ctx=ctx)
        den = k.sb("ab_den", [P, 2], ctx=ctx)
        rd = k.sb("ab_rd", [P, 4], ctx=ctx)
        sps = k.ps("ab_sp", [P, 2, NG, 512], ctx)
        tps = k.ps("ab_tp", [P, 2, 512], ctx)
        s = {n: k.sem("ab_" + n, ctx) for n in (
            "staged", "scored", "biased", "shifted", "exped", "turned", "laid", "mixed", "y_kept", "y_turned", "y_laid")}
        own = k.sem("ab_dve", ctx)
        moved = k.sem("ab_pool", ctx)
        rel = k.const("rel").rearrange("p (g n) -> p g n", g=NG)
        units = [(j, qb) for j in range(2) for qb in range(NB)]
        U = len(units)

        def pieces(qb):
            out, at = [], 0
            for g in range(NG):
                lo = FIRST[g](qb)
                out.append((g, lo, at, (qb + 1 - lo) * P))
                at += out[-1][3]
            return out, at

        def blocks_of(qb):
            return [(g, lo + n) for g, lo, _, w in pieces(qb)[0] for n in range(w // P)]

        def lots(qb):
            n = len(blocks_of(qb))
            return [range(a, min(a + 4, n)) for a in range(0, n, 4)]

        first_lot, n_lots = [], 0
        for _, qb in units:
            first_lot.append(n_lots)
            n_lots += len(lots(qb))
        assert n_lots % 2 == 0
        TRIPS = SLOTS_B // 2
        with nc.Block() as block:

            @block.sync
            def _(sp):
                for b in range(DEC):
                    for g, (_, d) in enumerate(GROUPS):
                        sp.dma_start(k.kv[:, b, g, :], k.io[f"cache_kv_b{g}"][0, b].rearrange(
                            "(n d) k h e -> n d (k h e)", d=d)[:, 0, :]).then_inc(k.kv_in[b], 16)
                for g, (wlen, _) in enumerate(GROUPS):
                    sp.dma_start(k.io[f"o_kvs{g}"][:, 0:wlen - 1, :],
                                 k.io[f"cache_kv_b{g}"][0].rearrange("b w k h d -> b w (k h d)")[:, 1:wlen, :])\
                        .then_inc(k.shifted, 16)

            @block.gpsimd
            def _(pool):
                link = Chain(pool, moved)
                with pool.Fori(0, TRIPS) as i:
                    link.enter(i, 4 * NG)
                    for j in range(2):
                        pool.wait_ge(s["y_kept"], i * U + OPEN)
                        rows = slice(j * HD, (j + 1) * HD)
                        for g in range(NG):
                            for dst, t0 in ((qs, 2 * WA // P), (ks, (2 * WA + WB) // P)):
                                link(pool.tensor_copy(dst[:, j, g, :], k.qk[
                                    rows, bass.ds(i + (t0 + 2 * g), 1), :].rearrange("p a n -> p (a n)")))
                        pool.sem_inc(s["staged"], 1)
                    link.leave(4 * NG, TRIPS)

            @block.vector
            def _(dve):
                for sem in (s["y_kept"],):
                    dve.sem_inc(sem, OPEN)
                link = Chain(dve, own)
                per = 3 * U

                def keep(i, u):
                    j, qb = units[u]
                    dve.wait_ge(s["exped"], i * U + (u + 1))
                    link(dve.reciprocal(rd[:, u % 2:u % 2 + 1], den[:, u % 2:u % 2 + 1]))
                    dve.wait_ge(s["mixed"], i * U + (u + 1) + OPEN)
                    dve.tensor_scalar(y[:, qb, bass.ds(i * P + j * HD, HD)], sps[:, u % 2, 0, 256:256 + HD],
                                      rd[:, u % 2:u % 2 + 1], None, ALU.mult).then_inc(s["y_kept"], 1)

                with dve.Fori(0, TRIPS) as i:
                    link.enter(i, per)
                    for u, (j, qb) in enumerate(units):
                        dve.wait_ge(s["scored"], i * U + (u + 1))
                        ps_, W = pieces(qb)
                        for g, lo, at, w in ps_:
                            last = dve.scalar_tensor_tensor(
                                sc[:, u % 2, at:at + w], rel[:, g, SEQ - w:SEQ],
                                k.const("slope")[:, bass.ds(i * 2 + (j + g * SLOTS_B), 1)],
                                sps[:, u % 2, g, 0:w], ALU.mult, ALU.add)
                        link(last)
                        link(dve.reduce_max(mx[:, u % 2:u % 2 + 1], sc[:, u % 2, 0:W], axis=AX))
                        dve.tensor_scalar(nm[:, u % 2:u % 2 + 1], mx[:, u % 2:u % 2 + 1], -SCALE, None,
                                          ALU.mult).then_inc(s["shifted"], 1)
                        if u:
                            keep(i, u - 1)
                    keep(i, U - 1)
                    link.leave(per, TRIPS)

            @block.scalar
            def _(act):
                for sem in (s["laid"],):
                    act.sem_inc(sem, OPEN)
                with act.Fori(0, TRIPS) as i:
                    def exp(u):
                        j, qb = units[u]
                        W = pieces(qb)[1]
                        act.wait_ge(s["shifted"], i * U + (u + 1))
                        act.activation(sc[:, u % 2, 0:W], sc[:, u % 2, 0:W], ACT.Exp, bias=nm[:, u % 2:u % 2 + 1],
                                       scale=SCALE, accum_out=den[:, u % 2:u % 2 + 1]).then_inc(s["exped"], 1)

                    exp(0)
                    for u, (j, qb) in enumerate(units):
                        act.wait_ge(s["mixed"], i * U + u + OPEN)
                        for n, lot in enumerate(lots(qb)):
                            m = first_lot[u] + n
                            act.wait_ge(s["turned"], i * n_lots + (m + 1))
                            act.activation(pt[:, lot[0] * P:(lot[-1] + 1) * P], tps[:, m % 2, 0:len(lot) * P],
                                           ACT.Copy).then_inc(s["laid"], 1)
                            if n == 0 and u + 1 < U:
                                exp(u + 1)
                for n in range(NB):
                    act.wait_ge(s["y_turned"], n + 1)
                    act.activation(k.oT[:, WA // P:(WA + WBO) // P, n * P:(n + 1) * P],
                                   tps[:, n % 2, 0:WBO].rearrange("p (c n) -> p c n", c=WBO // P),
                                   ACT.Copy).then_inc(s["y_laid"], 1)
                act.wait_ge(s["y_laid"], NB)

            @block.tensor
            def _(pe):
                for sem in (s["mixed"],):
                    pe.sem_inc(sem, OPEN)
                with pe.Fori(0, TRIPS) as i:
                    def score(u):
                        j, qb = units[u]
                        if qb == 0:
                            pe.wait_ge(s["staged"], i * 2 + (j + 1))
                        if u >= 2:
                            pe.wait_ge(s["y_kept"], i * U + (u - 1) + OPEN)
                        else:
                            pe.wait_ge(s["y_kept"], i * U + OPEN)
                        for g, lo, at, w in pieces(qb)[0]:
                            last = pe.matmul(sps[:, u % 2, g, 0:w], qs[:, j, g, qb * P:(qb + 1) * P],
                                             ks[:, j, g, lo * P:lo * P + w], start=True, stop=True)
                        last.then_inc(s["scored"], 1)

                    score(0)
                    for u, (j, qb) in enumerate(units):
                        if u + 1 < U:
                            score(u + 1)
                        pe.wait_ge(s["exped"], i * U + (u + 1))
                        for n, lot in enumerate(lots(qb)):
                            m = first_lot[u] + n
                            if m >= 2:
                                pe.wait_ge(s["laid"], i * n_lots + (m - 1) + OPEN)
                            else:
                                pe.wait_ge(s["laid"], i * n_lots + OPEN)
                            for c, blk in enumerate(lot):
                                last = pe.transpose(tps[:, m % 2, c * P:(c + 1) * P],
                                                    sc[:, u % 2, blk * P:(blk + 1) * P], k.const("ident"))
                            last.then_inc(s["turned"], 1)
                        pe.wait_ge(s["laid"], i * n_lots + (first_lot[u] + len(lots(qb))) + OPEN)
                        bl = blocks_of(qb)
                        for n, (g, kb) in enumerate(bl):
                            last = pe.matmul(sps[:, u % 2, 0, 256:256 + HD], pt[:, n * P:(n + 1) * P],
                                             k.v_rows[:, kb, bass.ds(i * P + (WA + j * HD + g * WBO), HD)],
                                             start=(n == 0), stop=(n == len(bl) - 1))
                        last.then_inc(s["mixed"], 1)
                pe.wait_ge(s["y_kept"], U * TRIPS + OPEN)
                for n in range(NB):
                    if n >= 2:
                        pe.wait_ge(s["y_laid"], n - 1)
                    for c in range(WBO // P):
                        last = pe.transpose(tps[:, n % 2, c * P:(c + 1) * P], y[:, n, c * P:(c + 1) * P],
                                            k.const("ident"))
                    last.then_inc(s["y_turned"], 1)


def decode_b(k):
    nc = k.nc
    BS = DEC * SLOTS_B
    Q0, K0, V0 = 3 * WA, 3 * WA + WB, 3 * WA + 2 * WB
    with ExitStack() as ctx:
        kv = k.kv
        prod = k.sb("db_prod", [P, WB], ctx=ctx)
        sc = k.sb("db_sc", [P, NG, DEC, SLOTS_B], ctx=ctx)
        sn = k.sb("db_sn", [DEC, NG, SLOTS_B], ctx=ctx)
        dn = k.sb("db_dn", [DEC, NG, DEC, SLOTS_B], ctx=ctx)
        pr = k.sb("db_pr", [BS, NG, P + 1], ctx=ctx)
        pt = k.sb("db_pt", [P, NG, BS], ctx=ctx)
        xs = k.sb("db_xs", [BS, NG, DEC], ctx=ctx)
        pn = k.sb("db_pn", [DEC, NG, BS], ctx=ctx)
        om = k.sb("db_om", [SLOTS_B, WBO], ctx=ctx)
        mx = k.sb("db_mx", [BS, 4], ctx=ctx)
        rep = k.ps("db_rep", [P, 2, 2, 512], ctx)
        row = k.ps("db_row", [P, 512], ctx)
        new = k.ps("db_new", [P, 512], ctx)
        vp = k.ps("db_vp", [P, 512], ctx)
        cp = k.ps("db_cp", [P, 512], ctx)
        kv_in = k.kv_in
        s = {n: k.sem("db_" + n, ctx) for n in (
            "rep", "rep_used", "scores", "rows", "exped", "probs", "turned", "laid", "new_turned", "new_laid",
            "mixed", "own_kept", "cols", "cols_kept")}
        own = k.sem("db_dve", ctx)
        HW = WB // 2
        with nc.Block() as block:

            @block.tensor
            def _(pe):
                for b in range(DEC):
                    if b >= 2:
                        pe.wait_ge(s["rep_used"], b - 1)
                    for c in range(2):
                        last = pe.matmul(rep[:, b % 2, c, 0:HW], k.const("ident", DEC)[:, b:b + 1].to_broadcast([DEC, P]),
                                         k.samp[0:DEC, Q0 + c * HW:Q0 + (c + 1) * HW], start=True, stop=True)
                    last.then_inc(s["rep"], 1)
                pe.wait_ge(s["scores"], 1)
                for g in range(NG):
                    pe.transpose(row[0:BS, g * P:(g + 1) * P], sc[:, g].rearrange("p b s -> p (b s)"), k.const("ident"))
                for g in range(NG):
                    last = pe.matmul(new[0:BS, g:g + 1], dn[:, g].rearrange("p b s -> p (b s)"),
                                     k.const("ones", DEC)[:, 0:1], start=True, stop=True)
                last.then_inc(s["rows"], 1)
                pe.wait_ge(s["probs"], 1)
                for g in range(NG):
                    pe.transpose(row[:, g * BS:(g + 1) * BS], pr[:, g, 0:P], k.const("ident", BS)[:, 0:BS])
                for g in range(NG):
                    last = pe.matmul(new[0:DEC, g * BS:(g + 1) * BS], xs[:, g], k.const("ident", BS)[:, 0:BS],
                                     start=True, stop=True)
                last.then_inc(s["turned"], 1)
                pe.wait_ge(s["laid"], 1)
                for b in range(DEC):
                    if b:
                        pe.wait_ge(s["own_kept"], b)
                    mine = slice(b * SLOTS_B, (b + 1) * SLOTS_B)
                    for g in range(NG):
                        pe.matmul(vp[0:SLOTS_B, 0:WBO], pt[:, g, mine], kv[:, b, g, WBO:], start=(g == 0), stop=False)
                        last = pe.matmul(vp[0:SLOTS_B, 0:WBO], pn[:, g, mine],
                                         k.samp[0:DEC, V0 + g * WBO:V0 + (g + 1) * WBO], start=False,
                                         stop=(g == NG - 1))
                    last.then_inc(s["mixed"], 1)
                    pe.wait_ge(s["own_kept"], b + 1)
                    for c in range(WBO // P):
                        last = pe.matmul(cp[:, c * DEC + b:c * DEC + b + 1], om[:, c * P:(c + 1) * P],
                                         k.const("ones", SLOTS_B)[:, 0:1], start=True, stop=True)
                    last.then_inc(s["cols"], 1)

            @block.scalar
            def _(act):
                act.wait_ge(s["scores"], 2)
                act.activation(pr[:].rearrange("p g n -> p (g n)"), pr[:].rearrange("p g n -> p (g n)"), ACT.Exp,
                               bias=mx[:, 1:2], accum_out=mx[:, 2:3]).then_inc(s["exped"], 1)
                act.wait_ge(s["cols"], DEC)
                act.activation(k.oT[:, WA // P:(WA + WBO) // P, SEQ:TOK],
                               cp[:, 0:WBO // P * DEC].rearrange("p (c b) -> p c b", b=DEC),
                               ACT.Copy).then_inc(s["cols_kept"], 1)
                act.wait_ge(s["cols_kept"], 1)

            @block.vector
            def _(dve):
                link = Chain(dve, own)
                link(dve.tensor_tensor(prod[0:DEC, :], k.samp[0:DEC, Q0:Q0 + WB], k.samp[0:DEC, K0:K0 + WB], ALU.mult))
                link(dve.tensor_reduce(sn[:].rearrange("p g s -> p (g s)"),
                                       prod[0:DEC, :].rearrange("p (n d) -> p n d", d=HD), axis=AX, op=ALU.add))
                for g in range(NG):
                    link(dve.tensor_tensor(dn[:, g], sn[:, g].unsqueeze(1).to_broadcast([DEC, DEC, SLOTS_B]),
                                           k.const("ident", DEC)[:, 0:DEC].unsqueeze(2).to_broadcast(
                                               [DEC, DEC, SLOTS_B]), ALU.mult))
                for b in range(DEC):
                    dve.wait_ge(s["rep"], b + 1)
                    dve.wait_ge(kv_in[b], 16 * NG)
                    for g in range(NG):
                        for c in range(2):
                            lo, hi = max(g * WBO, c * HW), min((g + 1) * WBO, (c + 1) * HW)
                            if lo < hi:
                                last = dve.tensor_tensor(prod[:, lo:hi], kv[:, b, g, lo - g * WBO:hi - g * WBO],
                                                         rep[:, b % 2, c, lo - c * HW:hi - c * HW], ALU.mult)
                    last.then_inc(s["rep_used"], 1)
                    dve.wait_ge(s["rep_used"], b + 1)
                    link(dve.tensor_reduce(sc[:, :, b, :], prod[:].rearrange("p (g s d) -> p g s d", g=NG, s=SLOTS_B),
                                           axis=AX, op=ALU.add))
                for g in range(NG):
                    last = dve.scalar_tensor_tensor(
                        sc[:, g], sc[:, g], SCALE,
                        k.const("row_bias")[:, g * SLOTS_B:(g + 1) * SLOTS_B].unsqueeze(1).to_broadcast(
                            [P, DEC, SLOTS_B]), ALU.mult, ALU.add)
                last.then_inc(s["scores"], 1)
                dve.wait_ge(s["rows"], 1)
                link(dve.tensor_copy(pr[:, :, 0:P], row[0:BS, 0:NG * P].rearrange("p (g n) -> p g n", g=NG)))
                link(dve.tensor_scalar(pr[:, :, P:P + 1], new[0:BS, 0:NG].unsqueeze(2), SCALE, None, ALU.mult))
                link(dve.reduce_max(mx[:, 0:1], pr[:].rearrange("p g n -> p (g n)"), axis=AX))
                dve.tensor_scalar(mx[:, 1:2], mx[:, 0:1], -1.0, None, ALU.mult).then_inc(s["scores"], 1)
                dve.wait_ge(s["exped"], 1)
                link(dve.reciprocal(mx[:, 3:4], mx[:, 2:3]))
                flat = pr[:].rearrange("p g n -> p (g n)")
                link(dve.tensor_scalar(flat, flat, mx[:, 3:4], None, ALU.mult))
                dve.tensor_tensor(xs[:], pr[:, :, P:P + 1].to_broadcast([BS, NG, DEC]),
                                  k.const("own_sample", BS).unsqueeze(1).to_broadcast([BS, NG, DEC]),
                                  ALU.mult).then_inc(s["probs"], 1)
                dve.wait_ge(s["turned"], 1)
                link(dve.tensor_copy(pt[:].rearrange("p g n -> p (g n)"), row[:, 0:NG * BS]))
                dve.tensor_copy(pn[:].rearrange("p g n -> p (g n)"), new[0:DEC, 0:NG * BS]).then_inc(s["laid"], 1)
                for b in range(DEC):
                    dve.wait_ge(s["mixed"], b + 1)
                    if b:
                        dve.wait_ge(s["cols"], b)
                    dve.tensor_tensor(om[:], vp[0:SLOTS_B, 0:WBO], k.const("own_head", SLOTS_B)[:, 0:WBO],
                                      ALU.mult).then_inc(s["own_kept"], 1)


def merge(k):
    nc = k.nc
    CA, CB = WA // P, WBO // P
    H = TOK // 2
    with ExitStack() as ctx:
        wb = k.sb("mg_wb", [P, 2, CA + CB, P], ctx=ctx)
        wo = k.sb("mg_wo", [P, KC, D], ctx=ctx)
        gate = k.sb("mg_gate", [P, 2, KC, TOK], ctx=ctx)
        part = k.sb("mg_part", [P, 2, H], ctx=ctx)
        mixT = k.sb("mg_mix", [P, KC, TOK], ctx=ctx)
        ps = k.ps("mg_ps", [P, 8, 512], ctx)
        w_in = [k.sem(f"mg_w_in{j}", ctx) for j in range(2)]
        s = {n: k.sem("mg_" + n, ctx) for n in (
            "ya", "yb", "part_a", "part_b", "mixed", "proj", "kept", "gates_in")}
        x_in = k.pool_sem("mg_x_in")
        wo_in = k.pool_sem("mg_wo_in")
        TRIPS = KC // 2
        with nc.Block() as block:

            @block.sync
            def _(sp):
                sp.dma_start(gate[:].rearrange("p k c n -> p (k c n)"),
                             k.io["gates"].rearrange("p t n -> p (t n)")).then_inc(s["gates_in"], 16)
                with sp.Fori(0, TRIPS) as i:
                    for j in range(2):
                        sp.wait_ge(s["yb"], i * 2 + OPEN)
                        at = i * (2 * P) + j * P
                        sp.dma_start(wb[:, j, 0:CA], k.io["w_br_a"][0].rearrange("(c p) n -> p c n", p=P)[
                            :, :, bass.ds(at, P)]).then_inc(w_in[j], 16)
                        sp.dma_start(wb[:, j, CA:CA + CB], k.io["w_br_b"][0].rearrange("(c p) n -> p c n", p=P)[
                            :, :, bass.ds(at, P)]).then_inc(w_in[j], 16)

            @block.gpsimd
            def _(pool):
                pool.dma_start(wo[:], k.io["w_o"][0].rearrange("(c p) n -> p c n", p=P)).then_inc(wo_in, 16)
                pool.dma_start(k.x1[:, 0:NB, :], k.io["x_prompt"][0].rearrange("(b p) n -> p b n", p=P))\
                    .then_inc(x_in, 16)
                pool.dma_start(k.x1[0:DEC, NB, :], x_rows(k, NB)).then_inc(x_in, 16)

            @block.vector
            def _(dve):
                for sem in (s["part_a"], s["part_b"], s["mixed"],):
                    dve.sem_inc(sem, OPEN)
                dve.wait_ge(s["gates_in"], 16)
                with dve.Fori(0, TRIPS) as i:
                    for j in range(2):
                        t = i * 2 + j
                        g = lambda n: gate[:, n, bass.ds(t, 1), :].rearrange("p a (h n) -> p (a h) n", h=2)
                        mix = mixT[:, bass.ds(t, 1), :].rearrange("p a (h n) -> p (a h) n", h=2)
                        dve.wait_ge(s["ya"], t + 1)
                        dve.tensor_tensor(mix, g(0), ps[:, 4 * j:4 * j + 2, 0:H], ALU.mult).then_inc(s["part_a"], 1)
                        dve.wait_ge(s["yb"], t + 1 + OPEN)
                        dve.tensor_tensor(part[:], g(1), ps[:, 4 * j + 2:4 * j + 4, 0:H], ALU.mult)\
                            .then_inc(s["part_b"], 1)
                        dve.wait_ge(s["part_b"], t + 1 + OPEN)
                        dve.tensor_tensor(mix, mix, part[:], ALU.add).then_inc(s["mixed"], 1)
                        dve.wait_ge(s["mixed"], t + 1 + OPEN)
                dve.wait_ge(x_in, 32)
                for b in range(NBLK):
                    r = rows_of(b)
                    for h in range(2):
                        n = 2 * b + h
                        dve.wait_ge(s["proj"], n + 1)
                        x = k.x1[0:r, b, h * 512:(h + 1) * 512]
                        dve.tensor_tensor(x, x, ps[0:r, n % 8, :], ALU.add).then_inc(s["kept"], 1)
                dve.wait_ge(s["kept"], 2 * NBLK)

            @block.tensor
            def _(pe):
                for sem in (s["yb"],):
                    pe.sem_inc(sem, OPEN)
                def tile(dst, w, src, pieces):
                    for h in range(2):
                        for c in range(pieces):
                            last = pe.matmul(ps[:, dst + h, 0:H], w[:, c, :], src[:, c, h * H:(h + 1) * H],
                                             start=(c == 0), stop=(c == pieces - 1))
                    return last

                with pe.Fori(0, TRIPS) as i:
                    for j in range(2):
                        t = i * 2 + j
                        pe.wait_ge(w_in[j], i * 32 + 32)
                        pe.wait_ge(s["part_b"], (t if j == 0 else t - 1) + OPEN)
                        tile(4 * j, wb[:, j, 0:CA], k.oT[:, 0:CA], CA).then_inc(s["ya"], 1)
                        tile(4 * j + 2, wb[:, j, CA:CA + CB], k.oT[:, CA:CA + CB], CB).then_inc(s["yb"], 1)
                pe.wait_ge(wo_in, 16)
                pe.wait_ge(s["mixed"], KC + OPEN)
                for b in range(NBLK):
                    r = rows_of(b)
                    for h in range(2):
                        n = 2 * b + h
                        if n >= 8:
                            pe.wait_ge(s["kept"], n - 7)
                        for c in range(KC):
                            last = pe.matmul(ps[0:r, n % 8, :], mixT[:, c, b * P:b * P + r],
                                             wo[:, c, h * 512:(h + 1) * 512], start=(c == 0), stop=(c == KC - 1))
                        last.then_inc(s["proj"], 1)


def route(k):
    nc = k.nc
    NR = E_GROUPS + EXPERTS
    MUL = TOK // SLOT
    BIG = 64.0
    with ExitStack() as ctx:
        hn = k.sb("rt_hn", [P, NBLK, D], ctx=ctx)
        hT = k.sb("rt_hT", [P, KC, TOK], ctx=ctx)
        ms = k.sb("rt_ms", [P, NBLK], ctx=ctx)
        rms = k.sb("rt_rms", [P, NBLK], ctx=ctx)
        g_row = k.sb("rt_g_row", [P, D], ctx=ctx)
        rstd = k.sb("rt_rstd", [P, NBLK], ctx=ctx)
        wr = k.sb("rt_wr", [P, KC, NR], ctx=ctx)
        bias = k.sb("rt_bias", [P, NR], ctx=ctx)
        small = lambda name, *shape: k.sb("rt_" + name, [P, NBLK, *shape], ctx=ctx)
        lg = small("lg", NR)
        pick = small("pick", 8)
        mx = [small(f"mx{n}", 1) for n in range(3)]
        low = small("low", 1)
        oh_g = small("oh_g", E_GROUPS)
        oh_k = [small(f"oh{n}", E_PER) for n in range(2)]
        shifted = small("shifted", E_GROUPS)
        eg = small("eg", E_GROUPS)
        pg = small("pg", 1)
        e2 = small("e2", 1)
        by_g = small("by_g", E_GROUPS, E_PER)
        ing = small("ing", E_PER)
        ing2 = small("ing2", E_PER)
        one = [small(f"one{n}", E_GROUPS, E_PER) for n in range(2)]
        both = small("both", EXPERTS)
        rank = small("rank", EXPERTS)
        tmp = small("tmp", EXPERTS)
        col = {n: small("col_" + n, 1) for n in ("rank", "full", "pos", "eid", "base", "slot", "some")}
        at_pos = [small(f"at_pos{n}", SLOT) for n in range(2)]
        at_slot = [small(f"at_slot{n}", 2 * ALL_SLOTS) for n in range(2)]
        cmp_ = k.sb("rt_cmp", [P, EXPERTS, MUL], ctx=ctx)
        more = k.sb("rt_more", [P, EXPERTS], ctx=ctx)
        upto = k.sb("rt_upto", [P, EXPERTS], ctx=ctx)
        base = k.sb("rt_base", [P, EXPERTS], ctx=ctx)
        which = k.sb("rt_which", [1, MORE, EXPERTS], ctx=ctx)
        eid = k.sb("rt_eid", [1, MORE], ctx=ctx)
        empty = k.sb("rt_empty", [SLOT, 2 * ALL_SLOTS], ctx=ctx)
        tr = k.ps("rt_tr", [P, 2, KC, P], ctx)
        lp = k.ps("rt_lp", [P, 512], ctx)
        rp = k.ps("rt_rp", [P, 512], ctx)
        cp = k.ps("rt_cp", [P, 512], ctx)
        tp = k.ps("rt_tp", [P, 512], ctx)
        s = {n: k.sem("rt_" + n, ctx) for n in (
            "in", "g_in", "squares", "roots", "scaled", "turned", "placed", "h2_out", "logits", "chosen", "exped", "ranks",
            "tables", "slots")}
        own = k.sem("rt_dve", ctx)
        with nc.Block() as block:

            @block.sync
            def _(sp):
                v = lambda name: k.io[name][0].rearrange("(p c) n -> p c n", c=KC)
                sp.dma_start(g_row[:], k.io["g_ffn"][0].partition_broadcast(P)).then_inc(s["g_in"], 16)
                sp.dma_start(wr[:, :, 0:E_GROUPS], v("w_group")).then_inc(s["in"], 16)
                sp.dma_start(wr[:, :, E_GROUPS:NR], v("w_expert")).then_inc(s["in"], 16)
                sp.dma_start(bias[:, 0:E_GROUPS], k.io["b_group"][0].partition_broadcast(P)).then_inc(s["in"], 16)
                sp.dma_start(bias[:, E_GROUPS:NR], k.io["b_expert"][0].partition_broadcast(P)).then_inc(s["in"], 16)
                for q in range(HALVES):
                    load_half(k, sp, q, 0)
                for b in range(NBLK):
                    r = rows_of(b)
                    sp.wait_ge(s["scaled"], b + 1)
                    sp.dma_start(k.io["h2"][b * P:b * P + r, :], hn[0:r, b, :]).then_inc(s["h2_out"], 16)
                sp.wait_ge(s["h2_out"], 16 * NBLK)

            @block.scalar
            def _(act):
                for b in range(NBLK):
                    r = rows_of(b)
                    act.activation(hn[0:r, b, :], k.x1[0:r, b, :], ACT.Square,
                                   accum_out=ms[0:r, b:b + 1]).then_inc(s["squares"], 1)
                act.wait_ge(s["squares"], NBLK)
                for b in range(NBLK):
                    r = rows_of(b)
                    act.activation(rms[0:r, b:b + 1], ms[0:r, b:b + 1], ACT.Sqrt, bias=k.const("eps", r),
                                   scale=1.0 / D).then_inc(s["roots"], 1)
                act.wait_ge(s["chosen"], 1)
                act.activation(eg[:], shifted[:], ACT.Exp).then_inc(s["exped"], 1)
                act.wait_ge(s["chosen"], 2)
                act.activation(e2[:], e2[:], ACT.Exp).then_inc(s["exped"], 1)

            @block.tensor
            def _(pe):
                for b in range(NBLK):
                    r = rows_of(b)
                    pe.wait_ge(s["scaled"], b + 1)
                    if b >= 2:
                        pe.wait_ge(s["placed"], b - 1)
                    v = hn[0:r, b, :].rearrange("t (p c) -> t c p", c=KC)
                    for c in range(KC):
                        last = pe.transpose(tr[:, b % 2, c, 0:r], v[:, c, :], k.const("ident", r)[:, 0:r])
                    last.then_inc(s["turned"], 1)
                pe.wait_ge(s["in"], 64)
                pe.wait_ge(s["placed"], NBLK)
                for b in range(NBLK):
                    r = rows_of(b)
                    for c in range(KC):
                        last = pe.matmul(lp[0:r, b * NR:(b + 1) * NR], hT[:, c, b * P:b * P + r], wr[:, c, :],
                                         start=(c == 0), stop=(c == KC - 1))
                last.then_inc(s["logits"], 1)
                pe.wait_ge(s["chosen"], 3)
                for b in range(NBLK):
                    for b2 in range(b + 1):
                        pe.matmul(rp[:, b * EXPERTS:(b + 1) * EXPERTS], k.const("before" if b2 == b else "ones"),
                                  both[:, b2, :], start=(b2 == 0), stop=(b2 == b))
                for b in range(NBLK):
                    last = pe.matmul(cp[:, 0:EXPERTS], k.const("ones"), both[:, b, :], start=(b == 0),
                                     stop=(b == NBLK - 1))
                last.then_inc(s["ranks"], 1)
                pe.wait_ge(s["slots"], 1)
                n = 0
                for q in range(2):
                    for b in range(NBLK):
                        last = pe.matmul(tp[0:SLOT, 0:2 * ALL_SLOTS], at_pos[q][:, b, :], at_slot[q][:, b, :],
                                         start=(n == 0), stop=(n == 2 * NBLK - 1))
                        n += 1
                last.then_inc(s["tables"], 1)

            @block.vector
            def _(dve):
                link = Chain(dve, own)
                tt = lambda o, a, b, op: link(dve.tensor_tensor(o, a, b, op))
                wide = lambda ap, n: ap.to_broadcast([P, NBLK, n])
                real = k.const("real").unsqueeze(2)
                iota = lambda n: k.const("iota")[:, 0:n].unsqueeze(1).to_broadcast([P, NBLK, n])
                link(dve.memset(lg[:], 0.0))
                dve.wait_ge(s["g_in"], 16)
                for b in range(NBLK):
                    r = rows_of(b)
                    dve.wait_ge(s["roots"], b + 1)
                    link(dve.reciprocal(rstd[0:r, b:b + 1], rms[0:r, b:b + 1]))
                    dve.scalar_tensor_tensor(hn[0:r, b, :], k.x1[0:r, b, :], rstd[0:r, b:b + 1], g_row[0:r, :],
                                             ALU.mult, ALU.mult).then_inc(s["scaled"], 1)
                for b in range(NBLK):
                    r = rows_of(b)
                    dve.wait_ge(s["turned"], b + 1)
                    dve.tensor_copy(hT[:, :, b * P:b * P + r], tr[:, b % 2, :, 0:r]).then_inc(s["placed"], 1)
                dve.wait_ge(s["logits"], 1)
                dve.wait_ge(s["in"], 64)
                for b in range(NBLK):
                    r = rows_of(b)
                    last = dve.tensor_tensor(lg[0:r, b, :], lp[0:r, b * NR:(b + 1) * NR], bias[0:r, :], ALU.add)
                link(last)

                def first_largest(vals, n, most, onehot):
                    link(dve.tensor_reduce(most[:], vals, axis=AX, op=ALU.max))
                    tt(pick[:, :, 0:n], vals, wide(most[:], n), ALU.is_equal)
                    link(dve.scalar_tensor_tensor(pick[:, :, 0:n], pick[:, :, 0:n], -BIG, iota(n), ALU.mult, ALU.add))
                    link(dve.tensor_reduce(low[:], pick[:, :, 0:n], axis=AX, op=ALU.min))
                    tt(onehot[:], pick[:, :, 0:n], wide(low[:], n), ALU.is_equal)

                first_largest(lg[:, :, 0:E_GROUPS], E_GROUPS, mx[0], oh_g)
                dve.tensor_tensor(shifted[:], lg[:, :, 0:E_GROUPS], wide(mx[0][:], E_GROUPS), ALU.subtract)\
                    .then_inc(s["chosen"], 1)
                flat = [P, NBLK, E_GROUPS, E_PER]
                tt(by_g[:], lg[:, :, E_GROUPS:NR].rearrange("p b (g e) -> p b g e", g=E_GROUPS),
                   oh_g[:].unsqueeze(3).to_broadcast(flat), ALU.mult)
                link(dve.tensor_reduce(ing[:], by_g[:].rearrange("p b g e -> p b e g"), axis=AX, op=ALU.add))
                first_largest(ing[:], E_PER, mx[1], oh_k[0])
                link(dve.scalar_tensor_tensor(ing2[:], oh_k[0][:], -FAR, ing[:], ALU.mult, ALU.add))
                first_largest(ing2[:], E_PER, mx[2], oh_k[1])
                dve.tensor_tensor(e2[:], mx[2][:], mx[1][:], ALU.subtract).then_inc(s["chosen"], 1)
                for q in range(2):
                    tt(one[q][:], oh_g[:].unsqueeze(3).to_broadcast(flat),
                       oh_k[q][:].unsqueeze(2).to_broadcast(flat), ALU.mult)
                    f = one[q][:].rearrange("p b g e -> p b (g e)")
                    tt(f, f, wide(real, EXPERTS), ALU.mult)
                oh = [o[:].rearrange("p b g e -> p b (g e)") for o in one]
                dve.tensor_tensor(both[:], oh[0], oh[1], ALU.add).then_inc(s["chosen"], 1)
                dve.wait_ge(s["exped"], 2)
                link(dve.tensor_reduce(pg[:], eg[:], axis=AX, op=ALU.add))
                link(dve.reciprocal(pg[:], pg[:]))
                link(dve.tensor_scalar(col["some"][:], e2[:], 1.0, None, ALU.add))
                link(dve.reciprocal(col["some"][:], col["some"][:]))
                tt(k.gate[:, :, 0:1], pg[:], col["some"][:], ALU.mult)
                tt(k.gate[:, :, 1:2], k.gate[:, :, 0:1], e2[:], ALU.mult)
                dve.wait_ge(s["ranks"], 1)
                steps = k.const("steps")
                link(dve.tensor_copy(rank[:].rearrange("p b e -> p (b e)"), rp[:, 0:NBLK * EXPERTS]))
                tt(cmp_[:], cp[:, 0:EXPERTS].unsqueeze(2).to_broadcast([P, EXPERTS, MUL]),
                   steps.unsqueeze(1).to_broadcast([P, EXPERTS, MUL]), ALU.is_gt)
                link(dve.tensor_reduce(more[:], cmp_[:], axis=AX, op=ALU.add))
                link(dve.tensor_tensor_scan(upto[:], k.const("ones")[:, 0:EXPERTS], more[:], 0.0, ALU.mult, ALU.add))
                tt(base[:], upto[:], more[:], ALU.subtract)
                tt(which[:], upto[0:1, :].unsqueeze(1).to_broadcast([1, MORE, EXPERTS]),
                   k.const("iota", 1)[:, 0:MORE].unsqueeze(2).to_broadcast([1, MORE, EXPERTS]), ALU.is_le)
                link(dve.tensor_reduce(eid[:], which[:], axis=AX, op=ALU.add))
                link(dve.tensor_scalar(k.owner[:], eid[:], float(EXPERTS - 1), None, ALU.min))
                link(dve.tensor_copy(k.n_more[:], upto[0:1, EXPERTS - 1:EXPERTS]))
                for q in range(2):
                    def total(out, table):
                        tt(tmp[:], oh[q], table, ALU.mult)
                        link(dve.tensor_reduce(out[:], tmp[:], axis=AX, op=ALU.add))

                    c = col
                    total(c["rank"], rank[:])
                    total(c["eid"], iota(EXPERTS))
                    total(c["base"], base[:].unsqueeze(1).to_broadcast([P, NBLK, EXPERTS]))
                    tt(pick[:], wide(c["rank"][:], MUL), steps.unsqueeze(1).to_broadcast([P, NBLK, MUL]), ALU.is_ge)
                    link(dve.tensor_reduce(c["full"][:], pick[:], axis=AX, op=ALU.add))
                    link(dve.scalar_tensor_tensor(c["pos"][:], c["full"][:], -float(SLOT), c["rank"][:],
                                                  ALU.mult, ALU.add))
                    link(dve.tensor_scalar(c["some"][:], c["full"][:], 0.5, None, ALU.is_ge))
                    tt(c["slot"][:], c["base"][:], c["full"][:], ALU.add)
                    tt(c["slot"][:], c["slot"][:], c["eid"][:], ALU.subtract)
                    link(dve.tensor_scalar(c["slot"][:], c["slot"][:], float(EXPERTS - 1), None, ALU.add))
                    tt(c["slot"][:], c["slot"][:], c["some"][:], ALU.mult)
                    tt(c["slot"][:], c["slot"][:], c["eid"][:], ALU.add)
                    tt(at_pos[q][:], iota(SLOT), wide(c["pos"][:], SLOT), ALU.is_equal)
                    sl = at_slot[q][:, :, 0:ALL_SLOTS]
                    sl2 = at_slot[q][:, :, ALL_SLOTS:2 * ALL_SLOTS]
                    tt(sl, iota(ALL_SLOTS), wide(c["slot"][:], ALL_SLOTS), ALU.is_equal)
                    tt(sl2, sl, wide(k.const("token").unsqueeze(2), ALL_SLOTS), ALU.mult)
                    tt(sl, sl, wide(k.const(f"pair{q}").unsqueeze(2), ALL_SLOTS), ALU.mult)
                dve.sem_inc(s["slots"], 1)
                dve.wait_ge(s["tables"], 1)
                v = tp[0:SLOT, 0:2 * ALL_SLOTS]
                link(dve.memset(k.index[:], NONE))
                link(dve.tensor_scalar(empty[:], v, 0.0, float(NONE), ALU.is_equal, ALU.mult))
                for n in range(2):
                    part = slice(n * ALL_SLOTS, (n + 1) * ALL_SLOTS)
                    link(dve.scalar_tensor_tensor(k.index[:, n, 0:ALL_SLOTS], v[:, part], -1.0, empty[:, part],
                                                  ALU.add, ALU.add))


def load_half(k, sp, q, e):
    name, c = (("w_gate_e", KC), ("w_up_e", KC), ("w_down_e", FC))[q // 2]
    rows = slice(q % 2 * c // 2, (q % 2 + 1) * c // 2)
    sp.dma_start(k.raw[:, q].rearrange("p (c n) -> p c n", c=c // 2),
                 k.io[name][0, bass.ds(e, 1)].rearrange("a (p c) n -> p (a c) n", c=c)[:, rows])\
        .then_inc(k.raw_in[q], 16)


def experts(k):
    nc = k.nc
    with ExitStack() as ctx:
        raw, raw_in = k.raw, k.raw_in
        hi = k.sb("ex_hi", [P, SPLITS, HALF], F32R, ctx=ctx)
        lo = k.sb("ex_lo", [P, SPLITS, HALF], F32R, ctx=ctx)
        xg = k.sb("ex_xg", [SLOT, 2, D], ctx=ctx)
        xT = k.sb("ex_xT", [P, KC, 2, SLOT], F32R, ctx=ctx)
        gu_low = k.sb("ex_gu_low", [SLOT, 2, FF], ctx=ctx)
        y_low = k.sb("ex_y_low", [SLOT, 2, 512], ctx=ctx)
        gu = k.sb("ex_gu", [SLOT, 2, FF], ctx=ctx)
        sg, hm = gu_low[:, 0], gu[:, 1]
        hmT = k.sb("ex_hmT", [P, FC, 2, SLOT], F32R, ctx=ctx)
        yg = k.sb("ex_yg", [SLOT, 2, D], ctx=ctx)
        opened = k.sb("ex_opened", [1, 2], ctx=ctx)
        from_row = k.sb("ex_from", [SLOT, 2, 1], U32, ctx=ctx)
        to_row = k.sb("ex_to", [SLOT, 2, 1], U32, ctx=ctx)
        xp = k.ps("ex_xp", [P, KC, SLOT], ctx)
        gp = k.ps("ex_gp", [P, 2, 2, FF], ctx)
        hp = k.ps("ex_hp", [P, FC, P], ctx)
        yp = k.ps("ex_yp", [P, 2, 512], ctx)
        x_in = [k.pool_sem(f"ex_x_in{j}") for j in range(2)]
        y_out = [k.pool_sem(f"ex_y_out{j}") for j in range(2)]
        from_laid = [k.sem(f"ex_from_laid{j}", ctx) for j in range(2)]
        hi_made = [k.sem(f"ex_hi_made{n}", ctx) for n in range(SPLITS)]
        lo_made = [k.sem(f"ex_lo_made{n}", ctx) for n in range(SPLITS)]
        split_used = [k.sem(f"ex_split_used{n}", ctx) for n in range(SPLITS)]
        s = {n: k.sem("ex_" + n, ctx) for n in (
            "cleared", "turned", "x_hi", "x_lo", "gu_low", "gu_kept", "silu", "h_made", "h_turned", "h_hi",
            "h_lo", "y_low", "y_kept", "to_laid")}
        go_pe, go_pool = k.sem("ex_go_pe", ctx), k.sem("ex_go_pool", ctx)
        TRIPS, ALL = EXPERTS // 2, ALL_SLOTS // 2
        USES = 2 * HALVES // SPLITS
        GU, DN = range(0, 4), range(4, HALVES)

        def split(at, n):
            f = at[1] + n
            return f % SPLITS, at[0] * USES + f // SPLITS

        def wait_product(eng, at, n):
            n, before = split(at, n)
            eng.wait_ge(split_used[n], before + 1 + OPEN)

        def passes(eng, gate_up, down, x_next, mix, hidden, keep):
            def pair(i, first, places):
                gate_up(i, 0, places[0])
                if not first:
                    down(i - 1, 1, places[1])
                x_next(i, 0)
                mix(i, 0, places[0])
                if not first:
                    keep(i - 1, 1, places[1])
                hidden(i, 0)
                gate_up(i, 1, places[2])
                down(i, 0, places[3])
                x_next(i, 1)
                mix(i, 1, places[2])
                keep(i, 0, places[3])
                hidden(i, 1)

            pair(0, True, ((0, 0), None, (0, 4), (0, 8)))
            with eng.Fori(1, TRIPS) as i:
                pair(i, False, ((i, -2), (i, 2), (i, 4), (i, 8)))
            down(TRIPS - 1, 1, (TRIPS, -2))
            keep(TRIPS - 1, 1, (TRIPS, -2))
            n = eng.value_load(k.n_more[0:1, 0:1], min_val=0, max_val=MORE)
            with eng.If(n > 0):
                with eng.Fori(TRIPS, ALL) as i:
                    for j in range(2):
                        gate_up(i, j, (i, HALVES * j))
                        x_next(i, j)
                        mix(i, j, (i, HALVES * j))
                        hidden(i, j)
                        down(i, j, (i, HALVES * j + 4))
                        keep(i, j, (i, HALVES * j + 4))

        none = lambda *_: None

        with nc.Block() as block:

            @block.sync
            def _(sp):
                def load(halves, i, j, before):
                    for n, q in enumerate(halves):
                        m, uses = split(before, n)
                        sp.wait_ge(lo_made[m], uses + 1)
                        load_half(k, sp, q, i * 2 + j)

                load(GU, 0, 1, (0, 0))
                with sp.Fori(1, TRIPS) as i:
                    load(GU, i, 0, (i - 1, 4))
                    load(DN, i - 1, 1, (i - 1, 8))
                    load(GU, i, 1, (i, -2))
                    load(DN, i, 0, (i, 2))
                load(DN, TRIPS - 1, 1, (TRIPS - 1, 8))
                n = sp.value_load(k.n_more[0:1, 0:1], min_val=0, max_val=MORE)
                with sp.If(n > 0):
                    for m in range(SPLITS):
                        sp.wait_ge(lo_made[m], TRIPS * USES)
                    with sp.Fori(TRIPS, ALL) as i:
                        for j in range(2):
                            e = sp.value_load(k.owner[0:1, bass.ds(i * 2 + (j - EXPERTS), 1)], min_val=0,
                                              max_val=EXPERTS - 1)
                            for q in range(HALVES):
                                if j:
                                    m, uses = split((i, 0), q)
                                else:
                                    m, uses = split((i - 1, HALVES), q)
                                sp.wait_ge(lo_made[m], uses + 1)
                                load_half(k, sp, q, e)

            @block.gpsimd
            def _(pool):
                for j in range(2):
                    pool.dma_start(opened[:, j:j + 1], k.io["g_final"].unsqueeze(0)[:, 0:1]).then_inc(y_out[j], 16)

                def gather(j):
                    pool.indirect_dma_start(xg[:, j, :], None, k.io["h2"], bass.IndirectOffsetOnAxis(
                        ap=from_row[:, j, :], axis=0), bounds_check=TOK - 1, oob_is_err=False).then_inc(x_in[j], 16)

                def x_next(i, j):
                    pool.wait_ge(from_laid[j], i + 2)
                    pool.wait_ge(s["turned"], i * 2 + (j + 1))
                    pool.sem_inc(go_pool, 1)
                    gather(j)

                def keep(i, j, at):
                    pool.wait_ge(s["y_kept"], i * 2 + (j + 1))
                    pool.wait_ge(s["to_laid"], i * 2 + (j + 1))
                    pool.sem_inc(go_pool, 1)
                    pool.indirect_dma_start(k.io["pairs"], bass.IndirectOffsetOnAxis(ap=to_row[:, j, :], axis=0),
                                            yg[:, j, :], None, bounds_check=2 * TOK - 1,
                                            oob_is_err=False).then_inc(y_out[j], 16)

                pool.wait_ge(s["cleared"], 1)
                for j in range(2):
                    pool.wait_ge(from_laid[j], 1)
                    gather(j)
                passes(pool, none, none, x_next, none, none, keep)
                for j in range(2):
                    pool.wait_ge(y_out[j], 16 * TRIPS + 16)
                    pool.wait_ge(x_in[j], 16 * (TRIPS + 1))
                n = pool.value_load(k.n_more[0:1, 0:1], min_val=0, max_val=MORE)
                with pool.If(n > 0):
                    for j in range(2):
                        pool.wait_ge(y_out[j], 16 * ALL + 16)
                        pool.wait_ge(x_in[j], 16 * (ALL + 1))

            @block.scalar
            def _(act):
                for sem in split_used:
                    act.sem_inc(sem, OPEN)

                def high(i, j, at, halves):
                    for n, q in enumerate(halves):
                        m, before = split(at, n)
                        act.wait_ge(raw_in[q], i * 32 + (j + 1) * 16)
                        act.wait_ge(split_used[m], before + OPEN)
                        act.activation(hi[:, m], raw[:, q], ACT.Copy).then_inc(hi_made[m], 1)

                def gate_up(i, j, at):
                    high(i, j, at, GU)

                def down(i, j, at):
                    high(i, j, at, DN)

                def x_high(e):
                    act.wait_ge(s["turned"], e + 1)
                    act.activation(xT[:, :, 0, :], xp[:], ACT.Copy).then_inc(s["x_hi"], 1)

                def mix(i, j, at):
                    wait_product(act, at, 3)
                    act.activation(gu_low[:], gp[SLOT:2 * SLOT, j], ACT.Copy).then_inc(s["gu_low"], 1)
                    act.wait_ge(s["gu_kept"], i * 2 + (j + 1))
                    act.activation(sg, gu[:, 0], ACT.Silu).then_inc(s["silu"], 1)

                def keep(i, j, at):
                    wait_product(act, at, 1)
                    act.activation(y_low[:], yp[SLOT:2 * SLOT], ACT.Copy).then_inc(s["y_low"], 1)

                def hidden(i, j):
                    act.wait_ge(s["h_turned"], i * 2 + (j + 1))
                    act.activation(hmT[:, :, 0, :], hp[:, :, 0:SLOT], ACT.Copy).then_inc(s["h_hi"], 1)

                x_high(0)
                passes(act, gate_up, down, lambda i, j: x_high(i * 2 + (j + 1)), mix, hidden, keep)

            @block.vector
            def _(dve):
                def lay(dst, n, slot, j, sem):
                    dve.tensor_copy(dst[:, j, :], k.index[:, n, bass.ds(slot, 1)]).then_inc(sem, 1)

                def low(at, halves):
                    for n, q in enumerate(halves):
                        m, before = split(at, n)
                        dve.wait_ge(hi_made[m], before + 1)
                        dve.tensor_tensor(lo[:, m], raw[:, q], hi[:, m], ALU.subtract).then_inc(lo_made[m], 1)

                def gate_up(i, j, at):
                    low(at, GU)

                def down(i, j, at):
                    low(at, DN)

                def x_low(e):
                    dve.wait_ge(s["x_hi"], e + 1)
                    dve.tensor_tensor(xT[:, :, 1, :], xp[:], xT[:, :, 0, :], ALU.subtract).then_inc(s["x_lo"], 1)

                def x_next(i, j):
                    dve.wait_ge(x_in[j], i * 16 + 16)
                    lay(from_row, 1, i * 2 + (j + 2), j, from_laid[j])
                    x_low(i * 2 + (j + 1))

                def mix(i, j, at):
                    dve.wait_ge(s["gu_low"], i * 2 + (j + 1))
                    dve.tensor_tensor(gu[:], gp[0:SLOT, j], gu_low[:], ALU.add).then_inc(s["gu_kept"], 1)
                    dve.wait_ge(s["silu"], i * 2 + (j + 1))
                    dve.tensor_tensor(hm, sg, gu[:, 1], ALU.mult).then_inc(s["h_made"], 1)

                def keep(i, j, at):
                    dve.wait_ge(s["y_low"], i * 2 + (j + 1))
                    dve.wait_ge(y_out[j], i * 16 + 16)
                    lay(to_row, 0, i * 2 + j, j, s["to_laid"])
                    dve.tensor_tensor(yg[:, j, :].rearrange("t (h n) -> t h n", h=2), yp[0:SLOT], y_low[:],
                                      ALU.add).then_inc(s["y_kept"], 1)

                def hidden(i, j):
                    dve.wait_ge(s["h_hi"], i * 2 + (j + 1))
                    dve.tensor_tensor(hmT[:, :, 1, :], hp[:, :, 0:SLOT], hmT[:, :, 0, :],
                                      ALU.subtract).then_inc(s["h_lo"], 1)

                dve.memset(xg[:], 0.0).then_inc(s["cleared"], 1)
                for j in range(2):
                    lay(from_row, 1, j, j, from_laid[j])
                x_low(0)
                passes(dve, gate_up, down, x_next, mix, hidden, keep)

            @block.tensor
            def _(pe):
                def turn(i, j):
                    pe.wait_ge(x_in[j], i * 16 + 16)
                    pe.sem_inc(go_pe, 1)
                    v = xg[:, j, :].rearrange("t (p c) -> t c p", c=KC)
                    for c in range(KC):
                        last = pe.transpose(xp[:, c, :], v[:, c, :], k.const("ident", SLOT)[:, 0:SLOT])
                    last.then_inc(s["turned"], 1)

                def multiply(at, n, q, out, x):
                    m, before = split(at, n)
                    pe.wait_ge(lo_made[m], before + 1)
                    c = FC // 2 if q >= 4 else KC // 2
                    width = HALF // c
                    for w in (hi, lo):
                        for c1 in range(c):
                            for h in range(width // 512):
                                o = c1 * width + h * 512
                                last = pe.matmul(out[:, h], x[:, q % 2 * c + c1].rearrange("p a t -> p (a t)"),
                                                 w[:, m, o:o + 512],
                                                 start=(q % 2 == 0 and w is hi and c1 == 0),
                                                 stop=(q % 2 == 1 and w is lo and c1 == c - 1))
                    last.then_inc(split_used[m], 1)

                def gate_up(i, j, at):
                    pe.wait_ge(s["x_lo"], i * 2 + (j + 1))
                    for n, q in enumerate(GU):
                        multiply(at, n, q, gp[:, j, q // 2:q // 2 + 1], xT)
                    turn(i + j, 1 - j)

                def down(i, j, at):
                    pe.wait_ge(s["h_lo"], i * 2 + (j + 1))
                    if not (isinstance(i, int) and i == j == 0):
                        pe.wait_ge(s["y_kept"], i * 2 + j)
                    for n, q in enumerate(DN):
                        multiply(at, n, q, yp, hmT)

                def hidden(i, j):
                    pe.wait_ge(s["h_made"], i * 2 + (j + 1))
                    pe.sem_inc(go_pe, 1)
                    v = hm.rearrange("t (p c) -> t c p", c=FC)
                    for c in range(FC):
                        last = pe.transpose(hp[:, c, 0:SLOT], v[:, c, :], k.const("ident", SLOT)[:, 0:SLOT])
                    last.then_inc(s["h_turned"], 1)

                turn(0, 0)
                passes(pe, gate_up, down, none, none, hidden, none)


def finish(k):
    nc = k.nc
    with ExitStack() as ctx:
        two = k.sb("fn_two", [P, NBLK, 2, D], ctx=ctx)
        gf = k.sb("fn_gf", [P, D], ctx=ctx)
        junk = k.sb("fn_junk", [P, D], ctx=ctx)
        ms = k.sb("fn_ms", [P, NBLK], ctx=ctx)
        rms = k.sb("fn_rms", [P, NBLK], ctx=ctx)
        rstd = k.sb("fn_rstd", [P, NBLK], ctx=ctx)
        two_in = [k.sem(f"fn_in{b}", ctx) for b in range(NBLK)]
        s = {n: k.sem("fn_" + n, ctx) for n in ("added", "squares", "roots", "scaled", "out")}
        own = k.sem("fn_dve", ctx)
        gf_in = k.pool_sem("fn_gf_in")
        with nc.Block() as block:

            @block.sync
            def _(sp):
                for b in range(NBLK):
                    r = rows_of(b)
                    sp.dma_start(two[0:r, b], k.io["pairs"].rearrange("(t k) n -> t k n", k=2)[b * P:b * P + r])\
                        .then_inc(two_in[b], 16)
                for b in range(NBLK):
                    r = rows_of(b)
                    out = k.io["o_y"][b * P:(b + 1) * P, :] if b < NB else k.io["o_ys"]
                    sp.wait_ge(s["scaled"], b + 1)
                    sp.dma_start(out, k.x1[0:r, b, :]).then_inc(s["out"], 16)
                sp.wait_ge(s["out"], 16 * NBLK)

            @block.gpsimd
            def _(pool):
                pool.dma_start(gf[:], k.io["g_final"].partition_broadcast(P)).then_inc(gf_in, 16)

            @block.vector
            def _(dve):
                link = Chain(dve, own)
                for b in range(NBLK):
                    r = rows_of(b)
                    x = k.x1[0:r, b, :]
                    dve.wait_ge(two_in[b], 16)
                    link(dve.scalar_tensor_tensor(x, two[0:r, b, 0, :], k.gate[0:r, b, 0:1], x, ALU.mult, ALU.add))
                    dve.scalar_tensor_tensor(x, two[0:r, b, 1, :], k.gate[0:r, b, 1:2], x, ALU.mult,
                                             ALU.add).then_inc(s["added"], 1)
                dve.wait_ge(gf_in, 16)
                for b in range(NBLK):
                    r = rows_of(b)
                    x = k.x1[0:r, b, :]
                    dve.wait_ge(s["roots"], b + 1)
                    link(dve.reciprocal(rstd[0:r, b:b + 1], rms[0:r, b:b + 1]))
                    dve.scalar_tensor_tensor(x, x, rstd[0:r, b:b + 1], gf[0:r, :], ALU.mult,
                                             ALU.mult).then_inc(s["scaled"], 1)

            @block.scalar
            def _(act):
                for b in range(NBLK):
                    r = rows_of(b)
                    act.wait_ge(s["added"], b + 1)
                    act.activation(junk[0:r, :], k.x1[0:r, b, :], ACT.Square,
                                   accum_out=ms[0:r, b:b + 1]).then_inc(s["squares"], 1)
                    act.wait_ge(s["squares"], b + 1)
                for b in range(NBLK):
                    r = rows_of(b)
                    act.activation(rms[0:r, b:b + 1], ms[0:r, b:b + 1], ACT.Sqrt, bias=k.const("eps", r),
                                   scale=1.0 / D).then_inc(s["roots"], 1)


STEPS = [prepare, project, weigh_a, attend_a, attend_b, decode_b, merge, route, experts, finish]


INPUTS = ["x_prompt", "x_sample", "cache_k_a", "cache_v_a", "page_table", "cache_kv_b0", "cache_kv_b1", "cache_kv_b2",
          "g_attn", "w_in", "b_sb", "w_br_a", "w_br_b", "w_o", "g_ffn", "w_group", "b_group", "w_expert", "b_expert",
          "w_gate_e", "w_up_e", "w_down_e", "g_final"]


def outputs():
    out = [("o_y", (SEQ, D)), ("o_ys", (DEC, D)), ("o_ka", (SEQ, WA)), ("o_va", (SEQ, WA)),
           ("o_kas", (DEC, WA)), ("o_vas", (DEC, WA))]
    out += [(f"o_kvp{g}", (min(w, SEQ), 2 * WBO)) for g, (w, _) in enumerate(GROUPS)]
    out += [(f"o_kvs{g}", (DEC, w, 2 * WBO)) for g, (w, _) in enumerate(GROUPS)]
    return out


def build(nc, io, at, stop=99):
    with ExitStack() as ctx:
        k = Kernel(nc, ctx, io, at)
        k.consts = k.sb("consts_sb", [P, io["consts"].shape[1]])
        k.g_attn = k.sb("g_attn_sb", [P, KC])
        k.b_sb = k.sb("b_sb_sb", [P, HA])
        k.pages = k.sb("pages_sb", [1, DEC * PAGES], I32)
        k.shifted = ctx.enter_context(nc.semaphore("shifted"))
        steps = STEPS[:stop]
        k.oT = k.sb("oT", [P, (WA + WBO) // P, TOK])
        with ExitStack() as inner:
            k.qk = k.sb("qk", [P, QK_TILES, SEQ], ctx=inner)
            k.v_rows = k.sb("v_rows", [P, NB, WA + WB], ctx=inner)
            k.samp = k.sb("samp", [DEC, TILES * P], ctx=inner)
            with ExitStack() as branch_a:
                k.scores = k.sb("scores", [P, DEC, HA, PAGES], ctx=branch_a)
                with ExitStack() as projecting:
                    k.hT = k.sb("hT", [P, KC, TOK], ctx=projecting)
                    for f in steps[:2]:
                        f(k)
                for f in steps[2:4]:
                    f(k)
            k.kv = k.sb("kv", [P, DEC, NG, 2 * WBO], ctx=inner)
            k.kv_in = [k.sem(f"kv_in{b}", inner) for b in range(DEC)]
            for f in steps[4:6]:
                f(k)
        k.x1 = k.sb("x1", [P, NBLK, D])
        k.gate = k.sb("gate", [P, NBLK, 2])
        k.index = k.sb("index", [SLOT, 2, ALL_SLOTS + 2], U32)
        k.owner = k.sb("owner", [1, MORE], I32)
        k.n_more = k.sb("n_more", [1, 1], I32)
        for f in steps[6:7]:
            f(k)
        k.raw = k.sb("raw", [P, HALVES, HALF])
        k.raw_in = [ctx.enter_context(nc.semaphore(f"raw_in{q}")) for q in range(HALVES)]
        for f in steps[7:8]:
            f(k)
        k.clear_semaphores()
        for f in steps[8:]:
            f(k)
        if stop > 4:
            with nc.Block() as block:
                @block.sync
                def _(sp):
                    sp.wait_ge(k.shifted, 16 * NG)


def kernel(**inputs):
    import concourse.bacc as bacc
    from concourse.bass_utils import run_bass_kernel_spmd

    nc = bacc.Bacc("TRN2", target_bir_lowering=False, num_devices=1)
    at, consts = constants()
    arrays = {"in_consts": consts}
    io = {"consts": nc.dram_tensor("in_consts", consts.shape, F32, kind="ExternalInput").ap()}
    for name in INPUTS:
        a = np.ascontiguousarray(inputs[name])
        arrays[f"in_{name}"] = a
        io[name] = nc.dram_tensor(f"in_{name}", a.shape, mybir.dt.from_np(a.dtype), kind="ExternalInput").ap()
    for name, shape in outputs():
        io[name] = nc.dram_tensor(name, shape, F32, kind="ExternalOutput").ap()
    io["h2"] = nc.dram_tensor("h2_rows", (TOK, D), F32).ap()
    io["gates"] = nc.dram_tensor("gate_rows", (P, GATE_TILES, TOK), F32).ap()
    io["pairs"] = nc.dram_tensor("pair_rows", (2 * TOK, D), F32).ap()
    build(nc, io, at)
    got = run_bass_kernel_spmd(nc, [arrays], core_ids=[0]).results[0]
    g = [got[name] for name, _ in outputs()]
    kv = (2, SLOTS_B, HD)
    return (g[0].reshape(1, SEQ, D), g[1].reshape(DEC, 1, D),
            g[2].reshape(1, 1, SEQ, HA, HD), g[3].reshape(1, 1, SEQ, HA, HD),
            g[4].reshape(1, DEC, 1, HA, HD), g[5].reshape(1, DEC, 1, HA, HD),
            *(g[6 + n].reshape(1, 1, min(w, SEQ), *kv) for n, (w, _) in enumerate(GROUPS)),
            *(g[9 + n].reshape(1, DEC, w, *kv) for n, (w, _) in enumerate(GROUPS)))
```

```python
from contextlib import ExitStack

import numpy as np

import concourse.bass as bass
from concourse import mybir

F32 = mybir.dt.float32
F32R = mybir.dt.float32r
I32 = mybir.dt.int32
U32 = mybir.dt.uint32
ALU = mybir.AluOpType
ACT = mybir.ActivationFunctionType
AX = mybir.AxisListType.X

P = 128
D = 1024
KC = D // P
SEQ = 512
NB = SEQ // P
DEC = 8
TOK = SEQ + DEC
HD = 64
HA = 8
WA = HA * HD
SLOTS_B = 4
GROUPS = ((128, 1), (512, 4), (2048, 16))
NG = len(GROUPS)
HB = NG * SLOTS_B
WB = HB * HD
WBO = SLOTS_B * HD
PAGES = 32
PPG = 4
PPV = 2
RING = 4
RAW = 8
TILES = (3 * WA + 3 * WB) // P
GATE_TILES = 2 * D // P
QK_TILES = 2 * (WA + WB) // P
SCALE = HD ** -0.5
EPS = 1e-6
CLAMP = 30.0
EXPERTS = 32
E_GROUPS = 4
E_PER = EXPERTS // E_GROUPS
FF = 512
FC = FF // P
SLOT = 64
MORE = 16
ALL_SLOTS = EXPERTS + MORE
HALVES = 6
HALF = KC // 2 * FF
SPLITS = 4
NONE = 1 << 20
FAR = 1e30
OPEN = 1
NBLK = NB + 1

SLOPES = [[2.0 ** (-8.0 * (g * SLOTS_B + s + 1) / HB) for s in range(SLOTS_B)] for g in range(NG)]


def constants():
    p = np.arange(P)[:, None]
    f = np.arange(P)[None, :]
    u = np.arange(SEQ)[None, :]
    rel = p - u + (SEQ - P)
    t = np.arange(NBLK)[None, :] * P + p
    parts = {
        "ident": (p == f),
        "later_eq": (p >= f),
        "before": (p < f),
        "ones": np.ones((P, P)),
        "own_head": (np.arange(WA)[None, :] // HD == p % HA),
        "iota": np.broadcast_to(np.arange(SLOT)[None, :], (P, SLOT)),
        "steps": np.broadcast_to(SLOT * (np.arange(TOK // SLOT)[None, :] + 1), (P, TOK // SLOT)),
        "pair0": (2 * t + 1) * (t < TOK),
        "pair1": (2 * t + 2) * (t < TOK),
        "token": (t + 1) * (t < TOK),
        "real": (t < TOK),
        "eps": np.full((P, 1), EPS),
        "rel": np.concatenate([
            np.where((rel >= 0) & (rel <= w) & (rel % d == 0), rel, FAR) if d > 1 else
            np.where((rel >= 0) & (rel <= w), rel, FAR) for w, d in GROUPS], axis=1),
        "slope": np.broadcast_to(-np.array(SLOPES).reshape(1, HB) / SCALE, (P, HB)),
        "row_bias": np.concatenate([-np.array(SLOPES[g])[None, :] * d * (P - p)
                                    for g, (_, d) in enumerate(GROUPS)], axis=1),
        "own_slot": (np.arange(WBO)[None, :] // HD == p % SLOTS_B),
        "one_sample": np.broadcast_to((np.arange(DEC)[:, None] == np.arange(DEC * SLOTS_B)[None, :] // SLOTS_B)
                                      .reshape(1, -1), (P, DEC * DEC * SLOTS_B)),
        "own_sample": (p // SLOTS_B == np.arange(DEC)[None, :]),
    }
    at, cols, n = {}, [], 0
    for name, a in parts.items():
        a = np.asarray(a, np.float32)
        at[name] = (n, n + a.shape[1])
        n += a.shape[1]
        cols.append(a)
    return at, np.ascontiguousarray(np.concatenate(cols, axis=1))


class Chain:

    def __init__(self, eng, sem):
        self.eng, self.sem, self.base, self.k = eng, sem, 0, 0

    def __call__(self, ins):
        self.k += 1
        ins.then_inc(self.sem, 1)
        self.eng.wait_ge(self.sem, self.base + self.k)

    def enter(self, i, per):
        self.before = self.base + self.k
        self.base, self.k = self.before + i * per, 0

    def leave(self, per, trips):
        assert self.k == per, (self.k, per)
        self.base, self.k = self.before + per * trips, 0


class Kernel:

    def __init__(self, nc, ctx, io, at):
        self.nc, self.ctx, self.io, self.at, self.sems = nc, ctx, io, at, []

    def sb(self, name, shape, dt=F32, ctx=None):
        return (ctx or self.ctx).enter_context(self.nc.sbuf_tensor(name, shape, dt))

    def ps(self, name, shape, ctx):
        return ctx.enter_context(self.nc.psum_tensor(name, shape, F32))

    def sem(self, name, ctx):
        sem = ctx.enter_context(self.nc.semaphore(name))
        self.sems.append(sem)
        return sem

    def pool_sem(self, name):
        return self.ctx.enter_context(self.nc.semaphore(name))

    def clear_semaphores(self):
        with self.nc.Block() as block:

            @block.gpsimd
            def _(pool):
                for sem in self.sems:
                    pool.sem_clear(sem)
        self.sems = []

    def const(self, name, rows=P):
        a, b = self.at[name]
        first = self.at["rel"][0]
        return self.consts[0:rows, a:b] if b <= first else self.tables_b[0:rows, a - first:b - first]


def rows_of(blk):
    return P if blk < NB else DEC


def x_rows(k, blk):
    return k.io["x_prompt"][0, blk * P:(blk + 1) * P, :] if blk < NB else k.io["x_sample"][:, 0, :]


def load_w_in(k, act, m, j):
    act.dma_start(k.w[:, j], k.io["w_in"][0].rearrange("(p c) n -> p c n", c=KC)[
        :, :, bass.ds(m * (2 * P) + j * P, P)]).then_inc(k.w_in[j], 16)


def prepare(k):
    nc = k.nc
    with ExitStack() as ctx:
        x = k.sb("prep_x", [P, NBLK, D], ctx=ctx)
        junk = k.sb("prep_junk", [P, D], ctx=ctx)
        ms = k.sb("prep_ms", [P, NBLK], ctx=ctx)
        rms = k.sb("prep_rms", [P, NBLK], ctx=ctx)
        rstd = k.sb("prep_rstd", [P, NBLK], ctx=ctx)
        tr = k.ps("prep_tr", [P, 2, KC, P], ctx)
        consts_in = k.pool_sem("consts_in")
        x_in = [k.sem(f"x_in{b}", ctx) for b in range(NBLK)]
        squares = k.sem("squares", ctx)
        roots = k.sem("roots", ctx)
        scaled = k.sem("scaled", ctx)
        turned = k.sem("turned", ctx)
        placed = k.sem("placed", ctx)
        own = k.sem("prep_dve", ctx)
        with nc.Block() as block:

            @block.sync
            def _(sp):
                for b in range(NBLK):
                    sp.dma_start(x[0:rows_of(b), b, :], x_rows(k, b)).then_inc(x_in[b], 16)

            @block.gpsimd
            def _(pool):
                pool.dma_start(k.consts[:], k.io["consts"][:, 0:k.at["rel"][0]]).then_inc(consts_in, 16)
                pool.dma_start(k.g_attn[:], k.io["g_attn"][0].rearrange("(p c) -> p c", c=KC)).then_inc(consts_in, 16)
                pool.dma_start(k.b_sb[:], k.io["b_sb"][0].partition_broadcast(P)).then_inc(consts_in, 16)
                pool.dma_start(k.pages[:], k.io["page_table"].rearrange("b n -> (b n)").unsqueeze(0))\
                    .then_inc(consts_in, 16)
                pool.wait_ge(consts_in, 64)

            @block.scalar
            def _(act):
                for b in range(NBLK):
                    r = rows_of(b)
                    act.wait_ge(x_in[b], 16)
                    act.activation(junk[0:r, :], x[0:r, b, :], ACT.Square,
                                   accum_out=ms[0:r, b:b + 1]).then_inc(squares, 1)
                    act.wait_ge(squares, b + 1)
                for j in range(2):
                    load_w_in(k, act, 0, j)
                act.wait_ge(consts_in, 64)
                for b in range(NBLK):
                    r = rows_of(b)
                    act.activation(rms[0:r, b:b + 1], ms[0:r, b:b + 1], ACT.Sqrt,
                                   bias=k.const("eps", r), scale=1.0 / D).then_inc(roots, 1)

            @block.vector
            def _(dve):
                link = Chain(dve, own)
                for b in range(NBLK):
                    r = rows_of(b)
                    dve.wait_ge(roots, b + 1)
                    link(dve.reciprocal(rstd[0:r, b:b + 1], rms[0:r, b:b + 1]))
                    dve.tensor_scalar(x[0:r, b, :], x[0:r, b, :], rstd[0:r, b:b + 1], None,
                                      ALU.mult).then_inc(scaled, 1)
                dve.wait_ge(consts_in, 64)
                for b in range(NBLK):
                    r = rows_of(b)
                    dve.wait_ge(turned, b + 1)
                    dve.tensor_tensor(k.hT[:, :, b * P:b * P + r], tr[:, b % 2, :, 0:r],
                                      k.g_attn[:].unsqueeze(2).to_broadcast([P, KC, r]),
                                      ALU.mult).then_inc(placed, 1)
                dve.wait_ge(placed, NBLK)

            @block.tensor
            def _(pe):
                pe.wait_ge(consts_in, 64)
                for b in range(NBLK):
                    r = rows_of(b)
                    pe.wait_ge(scaled, b + 1)
                    if b >= 2:
                        pe.wait_ge(placed, b - 1)
                    v = x[0:r, b, :].rearrange("t (p c) -> t c p", c=KC)
                    for c in range(KC):
                        last = pe.transpose(tr[:, b % 2, c, 0:r], v[:, c, :], k.const("ident", r)[:, 0:r])
                    last.then_inc(turned, 1)


def load_pages(k, eng, b, g, cache, ring, ring_in):
    per = ring.shape[2]
    s = g % ring.shape[1]
    for j in range(per):
        page = eng.value_load(k.pages[0:1, bass.ds(b * PAGES + (g * per + j), 1)],
                              min_val=0, max_val=cache.shape[1] - 1)
        eng.dma_start(ring[:, s, per - 1 - j, :], cache[0, bass.ds(page, 1)].rearrange("a p h d -> (a p) (h d)"))\
            .then_inc(ring_in[s], 16)


def project(k):
    nc = k.nc
    with ExitStack() as ctx:
        ring = k.sb("k_ring", [P, RING, PPG, WA], ctx=ctx)
        w, w_in = k.w, k.w_in
        stage = k.sb("stage", [P, 2, TOK], ctx=ctx)
        krows = k.sb("k_rows", [P, NB, WB], ctx=ctx)
        qrep = k.sb("q_rep", [P, DEC, WA], ctx=ctx)
        prod = k.sb("prod", [P, PPG, WA], ctx=ctx)
        pp = k.ps("proj_ps", [P, 2, 2, 512], ctx)
        tp = k.ps("turn_ps", [P, 2, 512], ctx)
        ts = k.ps("turn_sample_ps", [P, 2, 512], ctx)
        rp = tp
        made = [k.sem(f"made{j}", ctx) for j in range(2)]
        staged = [k.sem(f"staged{j}", ctx) for j in range(2)]
        turned = [k.sem(f"q_turned{j}", ctx) for j in range(2)]
        laid = [k.sem(f"laid{j}", ctx) for j in range(2)]
        kept = [k.sem(f"kept{j}", ctx) for j in range(2)]
        k_out = k.sem("k_out", ctx)
        v_out = k.sem("v_out", ctx)
        gate_out = [k.sem(f"gate_out{j}", ctx) for j in range(2)]
        multiplied = k.sem("multiplied", ctx)
        rep = k.sem("rep", ctx)
        rep_laid = k.sem("rep_laid", ctx)
        ring_in = [k.sem(f"k_ring_in{s}", ctx) for s in range(RING)]
        ring_used = [k.sem(f"k_ring_used{s}", ctx) for s in range(RING)]
        own = k.sem("proj_dve", ctx)
        go_pool = k.sem("proj_go_pool", ctx)
        H = TOK // 2
        BY_POOL = (3, 7)
        io = k.io
        secs = [(0, 4, None), (4, 4, "k"), (8, 4, "v"), (12, 6, None), (18, 6, "k"), (24, 6, "v")]

        def tiles_loop(eng, t0, n, body):
            with eng.Fori(0, n // 2) as i:
                body(i + t0 // 2, i)

        with nc.Block() as block:

            @block.sync
            def _(sp):
                with sp.Fori(0, DEC) as b:
                    for g in range(PAGES // PPG):
                        sp.wait_ge(ring_used[g % RING], b * (PAGES // PPG // RING) + g // RING + OPEN)
                        load_pages(k, sp, b, g, io["cache_k_a"], ring, ring_in)

            @block.scalar
            def _(act):
                for sem in (*staged, *laid, *kept, *gate_out):
                    act.sem_inc(sem, OPEN)
                at = 0
                for t0, n, what in secs:
                    wide = n * P
                    if what == "k":
                        rows = krows[:, :, 0:wide]
                        if t0 > 4:
                            act.wait_ge(k_out, 16)
                    elif what == "v":
                        rows = k.v_rows[:, :, 0:WA] if wide == WA else k.v_rows[:, :, WA:WA + WB]

                    def body(m, i):
                        for j in range(2):
                            act.wait_ge(made[j], m + 1)
                            load_w_in(k, act, m + 1, j)
                            act.wait_ge(turned[j], m + OPEN)
                            act.wait_ge(kept[j], m + OPEN)
                            act.activation(stage[:, j, :].rearrange("p (a n) -> p a n", a=2), pp[:, j, :, 0:H],
                                           ACT.Copy).then_inc(staged[j], 1)
                        for j in range(2):
                            act.wait_ge(turned[j], m + 1 + OPEN)
                            if what == "v":
                                act.sem_inc(kept[j], 1)
                            else:
                                act.activation(k.qk[:, bass.ds(i * 2 + (at + j), 1), :].rearrange("p a n -> p (a n)"),
                                               stage[:, j, 0:SEQ], ACT.Copy).then_inc(kept[j], 1)
                            if what:
                                act.activation(rows[:, :, bass.ds(i * (2 * P) + j * P, P)],
                                               tp[:, j, :].rearrange("p (b n) -> p b n", b=NB),
                                               ACT.Copy).then_inc(laid[j], 1)
                            else:
                                act.sem_inc(laid[j], 1)
                            act.activation(k.samp[0:DEC, bass.ds(m * (2 * P) + j * P, P)],
                                           ts[0:DEC, j, 0:P], ACT.Copy).then_inc(laid[j], 1)

                    tiles_loop(act, t0, n, body)
                    if what != "v":
                        at += n
                    for j in range(2):
                        act.wait_ge(laid[j], t0 + n + OPEN)
                    if what == "k":
                        if wide == WA:
                            act.dma_start(io["o_ka"].rearrange("(b p) n -> p b n", p=P), rows).then_inc(k_out, 16)
                        else:
                            for g in range(NG):
                                keep = min(GROUPS[g][0], SEQ) // P
                                act.dma_start(io[f"o_kvp{g}"][:, 0:WBO].rearrange("(b p) n -> p b n", p=P),
                                              rows[:, NB - keep:NB, g * WBO:(g + 1) * WBO]).then_inc(k_out, 16)
                    elif what == "v":
                        if wide == WA:
                            act.dma_start(io["o_va"].rearrange("(b p) n -> p b n", p=P), rows).then_inc(v_out, 16)
                        else:
                            for g in range(NG):
                                keep = min(GROUPS[g][0], SEQ) // P
                                act.dma_start(io[f"o_kvp{g}"][:, WBO:2 * WBO].rearrange("(b p) n -> p b n", p=P),
                                              rows[:, NB - keep:NB, g * WBO:(g + 1) * WBO]).then_inc(v_out, 16)
                    if t0 == 0:
                        for b in range(DEC):
                            act.wait_ge(rep, b + 1)
                            act.activation(qrep[:, b, :], rp[:, b % 2, :], ACT.Copy).then_inc(rep_laid, 1)
                act.dma_start(io["o_kas"], k.samp[0:DEC, WA:2 * WA]).then_inc(k_out, 16)
                act.dma_start(io["o_vas"], k.samp[0:DEC, 2 * WA:3 * WA]).then_inc(v_out, 16)
                for g, (wlen, _) in enumerate(GROUPS):
                    for c, s in ((0, k_out), (1, v_out)):
                        at = 3 * WA + (1 + c) * WB + g * WBO
                        act.dma_start(io[f"o_kvs{g}"][:, wlen - 1, c * WBO:(c + 1) * WBO],
                                      k.samp[0:DEC, at:at + WBO]).then_inc(s, 16)

                def gate(i, last=False):
                    m = i + TILES // 2
                    for j in range(2):
                        act.wait_ge(made[j], m + 1)
                        if not last:
                            load_w_in(k, act, m + 1, j)
                        act.wait_ge(gate_out[j], i * 16 + OPEN)
                        act.activation(stage[:, j, :].rearrange("p (a n) -> p a n", a=2), pp[:, j, :, 0:H],
                                       ACT.Sigmoid).then_inc(staged[j], 1)
                    for j in range(2):
                        act.wait_ge(staged[j], m + 1 + OPEN)
                        act.dma_start(io["gates"][:, bass.ds(i * 2 + j, 1), :].rearrange("p a n -> p (a n)"),
                                      stage[:, j, :]).then_inc(gate_out[j], 16)

                with act.Fori(0, GATE_TILES // 2 - 1) as i:
                    gate(i)
                gate(GATE_TILES // 2 - 1, last=True)
                for j in range(2):
                    act.wait_ge(gate_out[j], 16 * (GATE_TILES // 2) + OPEN)
                act.wait_ge(k_out, 16 * (2 + 2 * NG))
                act.wait_ge(v_out, 16 * (2 + 2 * NG))

            @block.gpsimd
            def _(pool):
                with pool.Fori(0, DEC) as b:
                    pool.wait_ge(rep_laid, b + 1)
                    for g in BY_POOL:
                        pool.wait_ge(ring_in[g % RING], b * (32 * PPG) + 16 * PPG * (g // RING + 1))
                        pool.sem_inc(go_pool, 1)
                        pool.tensor_tensor(ring[:, g % RING, :, :], ring[:, g % RING, :, :],
                                           qrep[:, bass.ds(b, 1), :].to_broadcast([P, PPG, WA]),
                                           ALU.mult).then_inc(multiplied, 1)

            @block.tensor
            def _(pe):
                for sem in (*turned,):
                    pe.sem_inc(sem, OPEN)

                def make(m):
                    for j in range(2):
                        pe.wait_ge(w_in[j], (m + 1) * 16)
                        pe.wait_ge(staged[j], m + OPEN)
                        for half in range(2):
                            for c in range(KC):
                                last = pe.matmul(pp[:, j, half, 0:H], w[:, j, c, :],
                                                 k.hT[:, c, half * H:(half + 1) * H],
                                                 start=(c == 0), stop=(c == KC - 1))
                        last.then_inc(made[j], 1)

                for t0, n, what in secs:
                    def body(m, i):
                        make(m)
                        for j in range(2):
                            pe.wait_ge(staged[j], m + 1 + OPEN)
                            pe.wait_ge(laid[j], m * 2 + OPEN)
                            if what:
                                for b in range(NB):
                                    pe.transpose(tp[:, j, b * P:(b + 1) * P], stage[:, j, b * P:(b + 1) * P],
                                                 k.const("ident"))
                            pe.transpose(ts[0:DEC, j, 0:P], stage[:, j, SEQ:TOK],
                                         k.const("ident")).then_inc(turned[j], 1)
                    tiles_loop(pe, t0, n, body)
                    if t0 == 0:
                        for j in range(2):
                            pe.wait_ge(laid[j], n + OPEN)
                        for b in range(DEC):
                            if b >= 2:
                                pe.wait_ge(rep_laid, b - 1)
                            pe.matmul(rp[:, b % 2, :], k.const("ident", DEC)[:, b:b + 1].to_broadcast([DEC, P]),
                                      k.samp[0:DEC, 0:WA], start=True, stop=True).then_inc(rep, 1)
                        pe.wait_ge(rep_laid, DEC)
                with pe.Fori(TILES // 2, (TILES + GATE_TILES) // 2) as m:
                    make(m)

            @block.vector
            def _(dve):
                for sem in (*ring_used,):
                    dve.sem_inc(sem, OPEN)
                link = Chain(dve, own)
                per = PAGES // PPG
                with dve.Fori(0, DEC) as b:
                    link.enter(b, per - len(BY_POOL))
                    dve.wait_ge(rep_laid, b + 1)
                    for g in range(per):
                        s = g % RING
                        at = PAGES - PPG * (g + 1)
                        scores = k.scores[:, bass.ds(b, 1), :, at:at + PPG].rearrange("p a h j -> p j (a h)")
                        by_head = lambda t: t.rearrange("p j (h d) -> p j h d", d=HD)
                        if g in BY_POOL:
                            dve.wait_ge(multiplied, b * len(BY_POOL) + (BY_POOL.index(g) + 1))
                            reduced = dve.tensor_reduce(scores, by_head(ring[:, s, :, :]), axis=AX, op=ALU.add)
                            reduced.then_inc(ring_used[s], 1)
                            continue
                        dve.wait_ge(ring_in[s], b * (32 * PPG) + 16 * PPG * (g // RING + 1))
                        link_ready = dve.tensor_tensor(
                            prod[:, :, :], ring[:, s, :, :],
                            qrep[:, bass.ds(b, 1), :].to_broadcast([P, PPG, WA]), ALU.mult)
                        link_ready.then_inc(ring_used[s], 1)
                        dve.wait_ge(ring_used[s], b * 2 + (g // RING + 1) + OPEN)
                        link(dve.tensor_reduce(scores, by_head(prod[:, :, :]), axis=AX, op=ALU.add))
                    link.leave(per - len(BY_POOL), DEC)


def shift(k, eng, g):
    wlen = GROUPS[g][0]
    eng.dma_start(k.io[f"o_kvs{g}"][:, 0:wlen - 1, :],
                  k.io[f"cache_kv_b{g}"][0].rearrange("b w k h d -> b w (k h d)")[:, 1:wlen, :])\
        .then_inc(k.shifted, 16)


def weigh_a(k):
    nc = k.nc
    N = DEC * HA * PAGES
    with ExitStack() as ctx:
        t = k.sb("wa_t", [P, N], ctx=ctx)
        later = k.sb("wa_later", [P, DEC * HA, PAGES], ctx=ctx)
        keep = k.sb("wa_keep", [P, DEC * HA, PAGES], ctx=ctx)
        within = k.ps("wa_within", [P, N], ctx)
        totals = k.ps("wa_totals", [P, N], ctx)
        own = k.sem("wa_dve", ctx)
        clamped = k.sem("wa_clamped", ctx)
        exped = k.sem("wa_exped", ctx)
        logged = k.sem("wa_logged", ctx)
        soft = k.sem("wa_soft", ctx)
        summed = k.sem("wa_summed", ctx)
        arg = k.sem("wa_arg", ctx)
        weighed = k.sem("wa_weighed", ctx)
        z = k.scores[:].rearrange("p b h n -> p (b h n)")
        zv = k.scores[:].rearrange("p b h n -> p b h n")
        with nc.Block() as block:

            @block.sync
            def _(sp):
                for g in range(NG - 1):
                    shift(k, sp, g)

            @block.vector
            def _(dve):
                link = Chain(dve, own)
                bias = k.b_sb[:].unsqueeze(2).to_broadcast([P, HA, PAGES])
                for b in range(DEC):
                    last = dve.scalar_tensor_tensor(zv[:, b], zv[:, b], SCALE, bias, ALU.mult, ALU.add)
                link(last)
                dve.tensor_scalar(t[:], z, CLAMP, None, ALU.min).then_inc(clamped, 1)
                link(dve.memset(keep[:], 1.0))
                link(dve.memset(keep[:, :, 0:1], 0.0))
                link(dve.memset(later[:, :, 0:1], 0.0))
                dve.wait_ge(logged, 1)
                dve.tensor_tensor(t[:], z, t[:], ALU.max).then_inc(soft, 1)
                dve.wait_ge(summed, 2)
                link(dve.tensor_copy(later[:, :, 1:PAGES],
                                     totals[:].rearrange("p (a n) -> p a n", n=PAGES)[:, :, 0:PAGES - 1]))
                lf = later[:].rearrange("p a n -> p (a n)")
                link(dve.tensor_tensor_scan(lf, keep[:].rearrange("p a n -> p (a n)"), lf, 0.0, ALU.mult, ALU.add))
                link(dve.tensor_tensor(z, z, within[:], ALU.subtract))
                dve.tensor_tensor(z, z, lf, ALU.subtract).then_inc(arg, 1)

            @block.scalar
            def _(act):
                act.wait_ge(clamped, 1)
                act.activation(t[:], t[:], ACT.Exp).then_inc(exped, 1)
                act.wait_ge(exped, 1)
                act.activation(t[:], t[:], ACT.Ln, bias=k.const("ones")[:, 0:1]).then_inc(logged, 1)
                act.wait_ge(arg, 1)
                act.activation(z, z, ACT.Exp).then_inc(weighed, 1)
                act.wait_ge(weighed, 1)

            @block.tensor
            def _(pe):
                pe.wait_ge(soft, 1)
                for out, table in ((within, "later_eq"), (totals, "ones")):
                    for c in range(N // 512):
                        last = pe.matmul(out[:, c * 512:(c + 1) * 512], k.const(table), t[:, c * 512:(c + 1) * 512],
                                         start=True, stop=True)
                    last.then_inc(summed, 1)


def attend_a(k):
    nc = k.nc
    OFF = {0: 0, 1: SEQ, 3: SEQ + 3 * P, 2: 2 * SEQ}
    W = 2 * SEQ + 2 * P
    UNITS = PAGES // PPV
    EARLY, MID, LATE = range(0, 5), range(5, 10), range(10, UNITS)
    with ExitStack() as ctx:
        qs = k.sb("aa_q", [HD, 2, SEQ], ctx=ctx)
        ks = k.sb("aa_k", [HD, 2, SEQ], ctx=ctx)
        vs = k.sb("aa_v", [P, 2, NB, HD], ctx=ctx)
        z = k.sb("aa_z", [P, 2, W], ctx=ctx)
        sp_ = k.sb("aa_soft", [P, 2, W], ctx=ctx)
        w_cur = k.sb("aa_w", [P, 2, PAGES, 2, HA], F32R, ctx=ctx)
        om = k.sb("aa_own", [2 * HA, WA], ctx=ctx)
        raw = k.sb("aa_raw", [P, RAW, PPV, WA], ctx=ctx)
        hi = k.sb("aa_hi", [P, RING, PPV, WA], F32R, ctx=ctx)
        lo = k.sb("aa_lo", [P, RING, PPV, WA], F32R, ctx=ctx)
        zp = k.ps("aa_zp", [P, 2, 3 * SEQ], ctx)
        op = k.ps("aa_op", [P, SEQ], ctx)
        vp = k.ps("aa_vp", [P, WA], ctx)
        s = {n: k.sem("aa_" + n, ctx) for n in (
            "staged", "scored", "z_kept", "clamped", "exped", "logged", "soft", "masked", "summed", "arg_done",
            "exp_a", "a_masked", "o_made", "o_kept", "w_hi", "w_laid", "own_kept", "col_made", "col_kept")}
        own = k.sem("aa_pool", ctx)
        ring_in = [k.sem(f"v_ring_in{n}", ctx) for n in range(RAW)]
        hi_made = [k.sem(f"v_hi_made{n}", ctx) for n in range(RING)]
        lo_made = [k.sem(f"v_lo_made{n}", ctx) for n in range(RING)]
        split_used = [k.sem(f"v_split_used{n}", ctx) for n in range(RING)]
        FILLS = UNITS // RING
        TRIPS = HA // 2
        AHEAD = 7
        LO_OPEN = RAW // RING
        BY_ACT = range(RAW - 1, UNITS, RAW)

        def load(eng, b, u):
            eng.wait_ge(lo_made[u % RING], b * FILLS + u // RING + 1 - RAW // RING + LO_OPEN)
            load_pages(k, eng, b, u, k.io["cache_v_a"], raw, ring_in)

        with nc.Block() as block:

            @block.sync
            def _(sp):
                with sp.Fori(0, DEC) as b:
                    for u in range(UNITS):
                        if u not in BY_ACT:
                            load(sp, b, u)

            @block.gpsimd
            def _(pool):
                link = Chain(pool, own)

                def stage(i, j, n):
                    if n is not None:
                        pool.wait_ge(s["o_made"], n + OPEN)
                    rows = slice(j * HD, (j + 1) * HD)
                    link(pool.tensor_copy(qs[:, j, :], k.qk[rows, bass.ds(i, 1), :].rearrange("p a n -> p (a n)")))
                    link(pool.tensor_copy(ks[:, j, :], k.qk[rows, bass.ds(i + HA // 2, 1), :].rearrange(
                        "p a n -> p (a n)")))
                    link(pool.tensor_copy(vs[:, j], k.v_rows[:, :, bass.ds(i * P + j * HD, HD)]))
                    pool.sem_inc(s["staged"], 1)

                stage(0, 0, None)
                with pool.Fori(0, TRIPS) as i:
                    link.enter(i, 6)
                    for j in range(2):
                        h = i * 2 + j
                        stage(i + j, 1 - j, h)
                        pool.wait_ge(s["soft"], h + 1)
                        for kb in range(NB):
                            d = sp_[:, j, OFF[kb]:OFF[kb] + P]
                            last = pool.tensor_tensor(d, d, k.const("before"), ALU.mult)
                        last.then_inc(s["masked"], 1)
                        pool.wait_ge(s["exp_a"], h + 1)
                        for kb in range(NB):
                            d = z[:, j, OFF[kb]:OFF[kb] + P]
                            last = pool.tensor_tensor(d, d, k.const("before"), ALU.mult)
                        last.then_inc(s["a_masked"], 1)
                        pool.wait_ge(s["a_masked"], h + 1)
                    link.leave(6, TRIPS)

            @block.vector
            def _(dve):
                for sem in (s["arg_done"], s["own_kept"]):
                    dve.sem_inc(sem, OPEN)
                for sem in lo_made:
                    dve.sem_inc(sem, LO_OPEN)

                def low(h, units):
                    for u in units:
                        n = u % RING
                        dve.wait_ge(hi_made[n], h * FILLS + (u // RING + 1))
                        dve.tensor_tensor(lo[:, n], raw[:, u % RAW], hi[:, n], ALU.subtract).then_inc(lo_made[n], 1)

                with dve.Fori(0, TRIPS) as i:
                    for j in range(2):
                        h = i * 2 + j
                        dve.wait_ge(s["w_hi"], h + 1)
                        dve.tensor_tensor(w_cur[:, j, :, 1, :].rearrange("p n h -> p h n"),
                                          k.scores[:, bass.ds(h, 1)].rearrange("p a h n -> p (a h) n"),
                                          w_cur[:, j, :, 0, :].rearrange("p n h -> p h n"),
                                          ALU.subtract).then_inc(s["w_laid"], 1)
                        low(h, range(0, 1))
                        dve.wait_ge(s["scored"], h + 1)
                        dve.wait_ge(s["o_made"], i * 2 + OPEN)
                        dve.tensor_scalar(z[:, j], zp[:, j, 0:W], SCALE, k.b_sb[:, bass.ds(h, 1)],
                                          ALU.mult, ALU.add).then_inc(s["z_kept"], 1)
                        dve.wait_ge(s["z_kept"], h + 1)
                        dve.tensor_scalar(sp_[:, j], z[:, j], CLAMP, None, ALU.min).then_inc(s["clamped"], 1)
                        low(h, range(1, 4))
                        dve.wait_ge(s["logged"], h + 1)
                        dve.tensor_tensor(sp_[:, j], z[:, j], sp_[:, j], ALU.max).then_inc(s["soft"], 1)
                        low(h, range(4, 9))
                        dve.wait_ge(s["summed"], h + 1)
                        dve.tensor_tensor(z[:, j], z[:, j], zp[:, j, 0:W], ALU.subtract).then_inc(s["arg_done"], 1)
                        low(h, range(9, UNITS))
                        dve.wait_ge(split_used[RING - 1], h * FILLS + FILLS + OPEN)
                        dve.wait_ge(s["col_made"], h + OPEN)
                        dve.tensor_tensor(om[:], vp[0:2 * HA, :], k.const("own_head", 2 * HA), ALU.mult)\
                            .then_inc(s["own_kept"], 1)

            @block.scalar
            def _(act):
                for sem in (s["col_kept"],):
                    act.sem_inc(sem, OPEN)

                def high(h, units):
                    for u in units:
                        n = u % RING
                        act.wait_ge(ring_in[u % RAW], (h * (UNITS // RAW) + (u // RAW + 1)) * (16 * PPV))
                        act.wait_ge(split_used[n], h * FILLS + u // RING + OPEN)
                        act.activation(hi[:, n], raw[:, u % RAW], ACT.Copy).then_inc(hi_made[n], 1)
                        if u + AHEAD in BY_ACT:
                            load(act, h, u + AHEAD)

                with act.Fori(0, TRIPS) as i:
                    for j in range(2):
                        h = i * 2 + j
                        act.activation(w_cur[:, j, :, 0, :].rearrange("p n h -> p h n"),
                                       k.scores[:, bass.ds(h, 1)].rearrange("p a h n -> p (a h) n"),
                                       ACT.Copy).then_inc(s["w_hi"], 1)
                        high(h, range(0, 4))
                        act.wait_ge(s["clamped"], h + 1)
                        act.activation(sp_[:, j], sp_[:, j], ACT.Exp).then_inc(s["exped"], 1)
                        act.wait_ge(s["exped"], h + 1)
                        act.activation(sp_[:, j], sp_[:, j], ACT.Ln, bias=k.const("ones")[:, 0:1])\
                            .then_inc(s["logged"], 1)
                        high(h, range(4, 9))
                        act.wait_ge(s["arg_done"], h + 1 + OPEN)
                        act.activation(z[:, j], z[:, j], ACT.Exp).then_inc(s["exp_a"], 1)
                        high(h, range(9, UNITS))
                        act.wait_ge(s["o_made"], h + 1 + OPEN)
                        rows = slice(j * HD, (j + 1) * HD)
                        act.activation(k.oT[rows, bass.ds(i, 1), 0:SEQ].rearrange("p a n -> p (a n)"), op[rows, :],
                                       ACT.Copy).then_inc(s["o_kept"], 1)
                        act.wait_ge(s["col_made"], h + 1 + OPEN)
                        act.activation(k.oT[:, 0:WA // P, bass.ds(h + SEQ, 1)].rearrange("p c a -> p (c a)"),
                                       op[:, 0:WA // P], ACT.Copy).then_inc(s["col_kept"], 1)
                act.wait_ge(s["col_kept"], HA + OPEN)

            @block.tensor
            def _(pe):
                for sem in (*split_used, s["o_made"], s["col_made"],):
                    pe.sem_inc(sem, OPEN)
                with pe.Fori(0, TRIPS) as i:
                    for j in range(2):
                        h = i * 2 + j

                        def values(units):
                            for u in units:
                                n = u % RING
                                pe.wait_ge(lo_made[n], h * FILLS + (u // RING + 1) + LO_OPEN)
                                for m in range(PPV):
                                    page = PAGES - PPV * (u + 1) + m
                                    for part in (hi, lo):
                                        last = pe.matmul(
                                            vp[0:2 * HA, :], w_cur[:, j, page].rearrange("p a h -> p (a h)"),
                                            part[:, n, m, :], start=(u == m == 0 and part is hi),
                                            stop=(u == UNITS - 1 and m == PPV - 1 and part is lo))
                                last.then_inc(split_used[n], 1)

                        pe.wait_ge(s["staged"], h + 1)
                        pe.wait_ge(s["arg_done"], (h if j == 0 else h - 1) + OPEN)
                        for kb in range(NB):
                            n = SEQ - kb * P
                            last = pe.matmul(zp[:, j, OFF[kb]:OFF[kb] + n], ks[:, j, kb * P:(kb + 1) * P],
                                             qs[:, j, kb * P:SEQ], start=True, stop=True)
                        last.then_inc(s["scored"], 1)
                        pe.wait_ge(s["w_laid"], h + 1)
                        pe.wait_ge(s["own_kept"], h + OPEN)
                        values(EARLY)
                        pe.wait_ge(s["masked"], h + 1)
                        for kb in range(NB):
                            for kb2 in range(kb, NB):
                                n, at = SEQ - kb2 * P, OFF[kb] + (kb2 - kb) * P
                                last = pe.matmul(zp[:, j, at:at + n], k.const("later_eq" if kb2 == kb else "ones"),
                                                 sp_[:, j, OFF[kb2]:OFF[kb2] + n], start=(kb2 == kb),
                                                 stop=(kb2 == NB - 1), skip_group_check=True)
                        last.then_inc(s["summed"], 1)
                        values(MID)
                        pe.wait_ge(s["a_masked"], h + 1)
                        pe.wait_ge(s["col_kept"], h + OPEN)
                        for kb in range(NB):
                            last = pe.matmul(op[j * HD:(j + 1) * HD, kb * P:SEQ], vs[:, j, kb, :],
                                             z[:, j, OFF[kb]:OFF[kb] + SEQ - kb * P], start=(kb == 0),
                                             stop=(kb == NB - 1), skip_group_check=True)
                        last.then_inc(s["o_made"], 1)
                        values(LATE)
                        pe.wait_ge(s["own_kept"], h + 1 + OPEN)
                        pe.wait_ge(s["o_kept"], h + 1)
                        for c in range(WA // P):
                            last = pe.matmul(op[:, c:c + 1], om[:, c * P:(c + 1) * P], k.const("ones", 2 * HA)[:, 0:1],
                                             start=True, stop=True)
                        last.then_inc(s["col_made"], 1)


def attend_b(k):
    nc = k.nc
    FIRST = [lambda qb: max(qb - 1, 0), lambda qb: 0, lambda qb: 0]
    WMAX = (2 + 2 * NB) * P
    with ExitStack() as ctx:
        qs = k.sb("ab_q", [HD, 2, NG, SEQ], ctx=ctx)
        ks = k.sb("ab_k", [HD, 2, NG, SEQ], ctx=ctx)
        sc = k.sb("ab_sc", [P, 2, WMAX], ctx=ctx)
        pt = k.sb("ab_pt", [P, WMAX], ctx=ctx)
        y = k.sb("ab_y", [P, NB, WBO], ctx=ctx)
        mx = k.sb("ab_mx", [P, 4], ctx=ctx)
        nm = k.sb("ab_nm", [P, 2], ctx=ctx)
        den = k.sb("ab_den", [P, 2], ctx=ctx)
        rd = k.sb("ab_rd", [P, 4], ctx=ctx)
        sps = k.ps("ab_sp", [P, NG, 512], ctx)
        mps = k.ps("ab_mp", [P, 2, 512], ctx)
        tps = k.ps("ab_tp", [P, 2, 512], ctx)
        s = {n: k.sem("ab_" + n, ctx) for n in (
            "tables_in", "staged", "keys_staged", "scored", "biased", "shifted", "exped", "turned", "laid", "mixed", "y_kept", "y_turned", "y_laid")}
        own = k.sem("ab_dve", ctx)
        moved = k.sem("ab_pool", ctx)
        rel = k.const("rel").rearrange("p (g n) -> p g n", g=NG)
        units = [(j, qb) for j in range(2) for qb in range(NB)]
        U = len(units)

        def pieces(qb):
            out, at = [], 0
            for g in range(NG):
                lo = FIRST[g](qb)
                out.append((g, lo, at, (qb + 1 - lo) * P))
                at += out[-1][3]
            return out, at

        def blocks_of(qb):
            return [(g, lo + n) for g, lo, _, w in pieces(qb)[0] for n in range(w // P)]

        def lots(qb):
            n = len(blocks_of(qb))
            return [range(a, min(a + 4, n)) for a in range(0, n, 4)]

        first_lot, n_lots = [], 0
        for _, qb in units:
            first_lot.append(n_lots)
            n_lots += len(lots(qb))
        assert n_lots % 2 == 0
        TRIPS = SLOTS_B // 2
        Q_TILE, K_TILE = 2 * WA // P, (2 * WA + WB) // P
        with nc.Block() as block:

            @block.sync
            def _(sp):
                sp.dma_start(k.tables_b[:], k.io["consts"][:, k.at["rel"][0]:]).then_inc(s["tables_in"], 16)
                for b in range(DEC):
                    for g, (_, d) in enumerate(GROUPS):
                        sp.dma_start(k.kv[:, b, g, :], k.io[f"cache_kv_b{g}"][0, b].rearrange(
                            "(n d) k h e -> n d (k h e)", d=d)[:, 0, :]).then_inc(k.kv_in, 16)
                shift(k, sp, NG - 1)

            @block.gpsimd
            def _(pool):
                link = Chain(pool, moved)
                with pool.Fori(0, TRIPS) as i:
                    link.enter(i, 3 * NG)
                    for j in range(2):
                        pool.wait_ge(s["scored"], i * U + NB * (j + 1))
                        rows = slice(j * HD, (j + 1) * HD)
                        for g in range(NG):
                            for dst, t0 in ((qs, Q_TILE), (ks, K_TILE))[:1 + j]:
                                link(pool.tensor_copy(dst[:, j, g, :], k.qk[
                                    rows, bass.ds(i + (t0 + 2 * g), 1), :].rearrange("p a n -> p (a n)")))
                        pool.sem_inc(s["staged"], 1)
                    link.leave(3 * NG, TRIPS)

            @block.vector
            def _(dve):
                for sem in (s["y_kept"], s["biased"]):
                    dve.sem_inc(sem, OPEN)
                link = Chain(dve, own)
                per = 2 * U
                dve.wait_ge(s["tables_in"], 16)

                def keep(i, u):
                    j, qb = units[u]
                    dve.wait_ge(s["exped"], i * U + (u + 1))
                    link(dve.reciprocal(rd[:, u % 2:u % 2 + 1], den[:, u % 2:u % 2 + 1]))
                    dve.wait_ge(s["mixed"], i * U + (u + 1) + OPEN)
                    dve.tensor_scalar(y[:, qb, bass.ds(i * P + j * HD, HD)], mps[:, u % 2, 0:HD],
                                      rd[:, u % 2:u % 2 + 1], None, ALU.mult).then_inc(s["y_kept"], 1)

                with dve.Fori(0, TRIPS) as i:
                    link.enter(i, per)
                    for u, (j, qb) in enumerate(units):
                        dve.wait_ge(s["scored"], i * U + (u + 1) + U)
                        ps_, W = pieces(qb)
                        for g, lo, at, w in ps_:
                            last = dve.scalar_tensor_tensor(
                                sc[:, u % 2, at:at + w], rel[:, g, SEQ - w:SEQ],
                                k.const("slope")[:, bass.ds(i * 2 + (j + g * SLOTS_B), 1)],
                                sps[:, g, 0:w], ALU.mult, ALU.add)
                        last.then_inc(s["biased"], 1)
                        dve.wait_ge(s["biased"], i * U + (u + 1) + OPEN)
                        link(dve.reduce_max(mx[:, u % 2:u % 2 + 1], sc[:, u % 2, 0:W], axis=AX))
                        dve.tensor_scalar(nm[:, u % 2:u % 2 + 1], mx[:, u % 2:u % 2 + 1], -SCALE, None,
                                          ALU.mult).then_inc(s["shifted"], 1)
                        if u:
                            keep(i, u - 1)
                    keep(i, U - 1)
                    link.leave(per, TRIPS)

            @block.scalar
            def _(act):
                for sem in (s["laid"],):
                    act.sem_inc(sem, OPEN)
                with act.Fori(0, TRIPS) as i:
                    def exp(u):
                        j, qb = units[u]
                        W = pieces(qb)[1]
                        act.wait_ge(s["shifted"], i * U + (u + 1))
                        act.activation(sc[:, u % 2, 0:W], sc[:, u % 2, 0:W], ACT.Exp, bias=nm[:, u % 2:u % 2 + 1],
                                       scale=SCALE, accum_out=den[:, u % 2:u % 2 + 1]).then_inc(s["exped"], 1)

                    act.wait_ge(s["scored"], i * U + NB)
                    for g in range(NG):
                        act.activation(ks[:, 0, g, :], k.qk[0:HD, bass.ds(i + (K_TILE + 2 * g), 1), :].rearrange(
                            "p a n -> p (a n)"), ACT.Copy).then_inc(s["keys_staged"], 1)
                    exp(0)
                    for u, (j, qb) in enumerate(units):
                        act.wait_ge(s["mixed"], i * U + u + OPEN)
                        for n, lot in enumerate(lots(qb)):
                            m = first_lot[u] + n
                            act.wait_ge(s["turned"], i * n_lots + (m + 1))
                            act.activation(pt[:, lot[0] * P:(lot[-1] + 1) * P], tps[:, m % 2, 0:len(lot) * P],
                                           ACT.Copy).then_inc(s["laid"], 1)
                        if u + 1 < U:
                            exp(u + 1)
                for n in range(NB):
                    act.wait_ge(s["y_turned"], n + 1)
                    act.activation(k.oT[:, WA // P:(WA + WBO) // P, n * P:(n + 1) * P],
                                   tps[:, n % 2, 0:WBO].rearrange("p (c n) -> p c n", c=WBO // P),
                                   ACT.Copy).then_inc(s["y_laid"], 1)
                act.wait_ge(s["y_laid"], NB)

            @block.tensor
            def _(pe):
                pe.sem_inc(s["mixed"], OPEN)
                pe.sem_inc(s["scored"], U)
                with pe.Fori(0, TRIPS) as i:
                    def score(u):
                        j, qb = units[u]
                        if qb == 0:
                            pe.wait_ge(s["staged"], i * 2 + (j + 1))
                            pe.wait_ge(s["keys_staged"], i * NG + NG)
                        pe.wait_ge(s["biased"], i * U + u + OPEN)
                        for g, lo, at, w in pieces(qb)[0]:
                            last = pe.matmul(sps[:, g, 0:w], qs[:, j, g, qb * P:(qb + 1) * P],
                                             ks[:, j, g, lo * P:lo * P + w], start=True, stop=True)
                        last.then_inc(s["scored"], 1)

                    score(0)
                    for u, (j, qb) in enumerate(units):
                        if u + 1 < U:
                            score(u + 1)
                        pe.wait_ge(s["exped"], i * U + (u + 1))
                        for n, lot in enumerate(lots(qb)):
                            m = first_lot[u] + n
                            if m >= 2:
                                pe.wait_ge(s["laid"], i * n_lots + (m - 1) + OPEN)
                            else:
                                pe.wait_ge(s["laid"], i * n_lots + OPEN)
                            for c, blk in enumerate(lot):
                                last = pe.transpose(tps[:, m % 2, c * P:(c + 1) * P],
                                                    sc[:, u % 2, blk * P:(blk + 1) * P], k.const("ident"))
                            last.then_inc(s["turned"], 1)
                        pe.wait_ge(s["laid"], i * n_lots + (first_lot[u] + len(lots(qb))) + OPEN)
                        pe.wait_ge(s["y_kept"], i * U + max(u - 1, 0) + OPEN)
                        bl = blocks_of(qb)
                        for n, (g, kb) in enumerate(bl):
                            last = pe.matmul(mps[:, u % 2, 0:HD], pt[:, n * P:(n + 1) * P],
                                             k.v_rows[:, kb, bass.ds(i * P + (WA + j * HD + g * WBO), HD)],
                                             start=(n == 0), stop=(n == len(bl) - 1))
                        last.then_inc(s["mixed"], 1)
                pe.wait_ge(s["y_kept"], U * TRIPS + OPEN)
                for n in range(NB):
                    if n >= 2:
                        pe.wait_ge(s["y_laid"], n - 1)
                    for c in range(WBO // P):
                        last = pe.transpose(tps[:, n % 2, c * P:(c + 1) * P], y[:, n, c * P:(c + 1) * P],
                                            k.const("ident"))
                    last.then_inc(s["y_turned"], 1)


def decode_b(k):
    nc = k.nc
    BS = DEC * SLOTS_B
    Q0, K0, V0 = 3 * WA, 3 * WA + WB, 3 * WA + 2 * WB
    with ExitStack() as ctx:
        kv = k.kv
        prod = k.sb("db_prod", [P, WB], ctx=ctx)
        sc = k.sb("db_sc", [P, NG, DEC, SLOTS_B], ctx=ctx)
        sn = k.sb("db_sn", [DEC, NG, SLOTS_B], ctx=ctx)
        dn = k.sb("db_dn", [DEC, NG, DEC, SLOTS_B], ctx=ctx)
        pr = k.sb("db_pr", [BS, NG, P + 1], ctx=ctx)
        pt = k.sb("db_pt", [P, NG, BS], ctx=ctx)
        alone = k.sb("db_alone", [P, DEC, NG, BS], ctx=ctx)
        xs = k.sb("db_xs", [BS, NG, DEC], ctx=ctx)
        pn = k.sb("db_pn", [DEC, NG, BS], ctx=ctx)
        om = k.sb("db_om", [BS, WBO], ctx=ctx)
        mx = k.sb("db_mx", [BS, 4], ctx=ctx)
        rep = k.ps("db_rep", [P, 2, 2, 512], ctx)
        row = k.ps("db_row", [P, 512], ctx)
        new = k.ps("db_new", [P, 512], ctx)
        vp = k.ps("db_vp", [P, 512], ctx)
        cp = k.ps("db_cp", [P, 512], ctx)
        s = {n: k.sem("db_" + n, ctx) for n in (
            "rep", "rep_used", "scores", "rows", "exped", "probs", "turned", "laid", "new_turned", "new_laid",
            "mixed", "own_kept", "cols", "cols_kept")}
        own = k.sem("db_dve", ctx)
        HW = WB // 2
        with nc.Block() as block:

            @block.tensor
            def _(pe):
                for b in range(DEC):
                    if b >= 2:
                        pe.wait_ge(s["rep_used"], b - 1)
                    for c in range(2):
                        last = pe.matmul(rep[:, b % 2, c, 0:HW], k.const("ident", DEC)[:, b:b + 1].to_broadcast([DEC, P]),
                                         k.samp[0:DEC, Q0 + c * HW:Q0 + (c + 1) * HW], start=True, stop=True)
                    last.then_inc(s["rep"], 1)
                pe.wait_ge(s["scores"], 1)
                for g in range(NG):
                    pe.transpose(row[0:BS, g * P:(g + 1) * P], sc[:, g].rearrange("p b s -> p (b s)"), k.const("ident"))
                for g in range(NG):
                    last = pe.matmul(new[0:BS, g:g + 1], dn[:, g].rearrange("p b s -> p (b s)"),
                                     k.const("ones", DEC)[:, 0:1], start=True, stop=True)
                last.then_inc(s["rows"], 1)
                pe.wait_ge(s["probs"], 1)
                for g in range(NG):
                    pe.transpose(row[:, g * BS:(g + 1) * BS], pr[:, g, 0:P], k.const("ident", BS)[:, 0:BS])
                for g in range(NG):
                    last = pe.matmul(new[0:DEC, g * BS:(g + 1) * BS], xs[:, g], k.const("ident", BS)[:, 0:BS],
                                     start=True, stop=True)
                last.then_inc(s["turned"], 1)
                pe.wait_ge(s["laid"], 1)
                for g in range(NG):
                    pe.matmul(vp[0:BS, 0:WBO], pn[:, g, :], k.samp[0:DEC, V0 + g * WBO:V0 + (g + 1) * WBO],
                              start=(g == 0), stop=False)
                for b in range(DEC):
                    for g in range(NG):
                        last = pe.matmul(vp[0:BS, 0:WBO], alone[:, b, g, :], kv[:, b, g, WBO:], start=False,
                                         stop=(b == DEC - 1 and g == NG - 1))
                last.then_inc(s["mixed"], 1)
                pe.wait_ge(s["own_kept"], 1)
                for c in range(WBO // P):
                    last = pe.matmul(cp[:, c * DEC:(c + 1) * DEC], om[:, c * P:(c + 1) * P],
                                     k.const("own_sample", BS), start=True, stop=True)
                last.then_inc(s["cols"], 1)

            @block.scalar
            def _(act):
                act.wait_ge(s["scores"], 2)
                act.activation(pr[:].rearrange("p g n -> p (g n)"), pr[:].rearrange("p g n -> p (g n)"), ACT.Exp,
                               bias=mx[:, 1:2], accum_out=mx[:, 2:3]).then_inc(s["exped"], 1)
                act.wait_ge(s["cols"], 1)
                act.activation(k.oT[:, WA // P:(WA + WBO) // P, SEQ:TOK],
                               cp[:, 0:WBO // P * DEC].rearrange("p (c b) -> p c b", b=DEC),
                               ACT.Copy).then_inc(s["cols_kept"], 1)
                act.wait_ge(s["cols_kept"], 1)

            @block.vector
            def _(dve):
                link = Chain(dve, own)
                link(dve.tensor_tensor(prod[0:DEC, :], k.samp[0:DEC, Q0:Q0 + WB], k.samp[0:DEC, K0:K0 + WB], ALU.mult))
                link(dve.tensor_reduce(sn[:].rearrange("p g s -> p (g s)"),
                                       prod[0:DEC, :].rearrange("p (n d) -> p n d", d=HD), axis=AX, op=ALU.add))
                for g in range(NG):
                    link(dve.tensor_tensor(dn[:, g], sn[:, g].unsqueeze(1).to_broadcast([DEC, DEC, SLOTS_B]),
                                           k.const("ident", DEC)[:, 0:DEC].unsqueeze(2).to_broadcast(
                                               [DEC, DEC, SLOTS_B]), ALU.mult))
                dve.wait_ge(k.kv_in, 16 * DEC * NG)
                for b in range(DEC):
                    dve.wait_ge(s["rep"], b + 1)
                    for g in range(NG):
                        for c in range(2):
                            lo, hi = max(g * WBO, c * HW), min((g + 1) * WBO, (c + 1) * HW)
                            if lo < hi:
                                last = dve.tensor_tensor(prod[:, lo:hi], kv[:, b, g, lo - g * WBO:hi - g * WBO],
                                                         rep[:, b % 2, c, lo - c * HW:hi - c * HW], ALU.mult)
                    last.then_inc(s["rep_used"], 1)
                    dve.wait_ge(s["rep_used"], b + 1)
                    link(dve.tensor_reduce(sc[:, :, b, :], prod[:].rearrange("p (g s d) -> p g s d", g=NG, s=SLOTS_B),
                                           axis=AX, op=ALU.add))
                for g in range(NG):
                    last = dve.scalar_tensor_tensor(
                        sc[:, g], sc[:, g], SCALE,
                        k.const("row_bias")[:, g * SLOTS_B:(g + 1) * SLOTS_B].unsqueeze(1).to_broadcast(
                            [P, DEC, SLOTS_B]), ALU.mult, ALU.add)
                last.then_inc(s["scores"], 1)
                dve.wait_ge(s["rows"], 1)
                link(dve.tensor_copy(pr[:, :, 0:P], row[0:BS, 0:NG * P].rearrange("p (g n) -> p g n", g=NG)))
                link(dve.tensor_scalar(pr[:, :, P:P + 1], new[0:BS, 0:NG].unsqueeze(2), SCALE, None, ALU.mult))
                link(dve.reduce_max(mx[:, 0:1], pr[:].rearrange("p g n -> p (g n)"), axis=AX))
                dve.tensor_scalar(mx[:, 1:2], mx[:, 0:1], -1.0, None, ALU.mult).then_inc(s["scores"], 1)
                dve.wait_ge(s["exped"], 1)
                link(dve.reciprocal(mx[:, 3:4], mx[:, 2:3]))
                flat = pr[:].rearrange("p g n -> p (g n)")
                link(dve.tensor_scalar(flat, flat, mx[:, 3:4], None, ALU.mult))
                dve.tensor_tensor(xs[:], pr[:, :, P:P + 1].to_broadcast([BS, NG, DEC]),
                                  k.const("own_sample", BS).unsqueeze(1).to_broadcast([BS, NG, DEC]),
                                  ALU.mult).then_inc(s["probs"], 1)
                dve.wait_ge(s["turned"], 1)
                link(dve.tensor_copy(pt[:].rearrange("p g n -> p (g n)"), row[:, 0:NG * BS]))
                link(dve.tensor_copy(pn[:].rearrange("p g n -> p (g n)"), new[0:DEC, 0:NG * BS]))
                wide = [P, DEC, NG, BS]
                dve.tensor_tensor(alone[:], pt[:].unsqueeze(1).to_broadcast(wide),
                                  k.const("one_sample").rearrange("p (b n) -> p b n", b=DEC).unsqueeze(2)
                                  .to_broadcast(wide), ALU.mult).then_inc(s["laid"], 1)
                dve.wait_ge(s["mixed"], 1)
                dve.tensor_tensor(om[:], vp[0:BS, 0:WBO], k.const("own_slot", BS), ALU.mult)\
                    .then_inc(s["own_kept"], 1)


def merge(k):
    nc = k.nc
    CA, CB = WA // P, WBO // P
    H = TOK // 2
    with ExitStack() as ctx:
        BUFS = 4
        BANKS = 2
        wb = k.sb("mg_wb", [P, BUFS, CA + CB, P], ctx=ctx)
        wo = k.sb("mg_wo", [P, KC, D], ctx=ctx)
        gate = k.sb("mg_gate", [P, 2, KC, TOK], ctx=ctx)
        part = k.sb("mg_part", [P, 2, H], ctx=ctx)
        junk = k.sb("mg_junk", [P, D], ctx=ctx)
        ms = k.sb("mg_ms", [P, NBLK], ctx=ctx)
        mixT = k.sb("mg_mix", [P, KC, TOK], ctx=ctx)
        ps = k.ps("mg_ps", [P, 8, 512], ctx)
        w_in = [k.sem(f"mg_w_in{j}", ctx) for j in range(BUFS)]
        s = {n: k.sem("mg_" + n, ctx) for n in (
            "ya", "yb", "part_a", "part_b", "mixed", "proj", "kept", "gates_in", "squares", "roots")}
        x_in = k.pool_sem("mg_x_in")
        wo_in = k.pool_sem("mg_wo_in")
        TRIPS = KC // BUFS
        with nc.Block() as block:

            @block.sync
            def _(sp):
                with sp.Fori(0, TRIPS) as i:
                    for j in range(BUFS):
                        sp.wait_ge(s["yb"], i * BUFS + (j + 1))
                        at = i * (BUFS * P) + j * P
                        sp.dma_start(wb[:, j, 0:CA], k.io["w_br_a"][0].rearrange("(c p) n -> p c n", p=P)[
                            :, :, bass.ds(at, P)]).then_inc(w_in[j], 16)
                        sp.dma_start(wb[:, j, CA:CA + CB], k.io["w_br_b"][0].rearrange("(c p) n -> p c n", p=P)[
                            :, :, bass.ds(at, P)]).then_inc(w_in[j], 16)

            @block.scalar
            def _(act):
                act.wait_ge(w_in[BUFS - 1], 32)
                for i in range(TRIPS):
                    if i:
                        act.wait_ge(s["gates_in"], 16 * i)
                    c = slice(i * BUFS, (i + 1) * BUFS)
                    act.dma_start(gate[:, :, c], k.io["gates"].rearrange("p (k c) n -> p k c n", k=2)[:, :, c])\
                        .then_inc(s["gates_in"], 16)
                for b in range(NBLK):
                    r = rows_of(b)
                    act.wait_ge(s["kept"], 2 * b + 2)
                    act.activation(junk[0:r, :], k.x1[0:r, b, :], ACT.Square,
                                   accum_out=ms[0:r, b:b + 1]).then_inc(s["squares"], 1)
                    act.wait_ge(s["squares"], b + 1)
                    act.activation(k.rms[0:r, b:b + 1], ms[0:r, b:b + 1], ACT.Sqrt, bias=k.const("eps", r),
                                   scale=1.0 / D).then_inc(s["roots"], 1)
                act.wait_ge(s["roots"], NBLK)

            @block.gpsimd
            def _(pool):
                pool.wait_ge(s["gates_in"], 16 * TRIPS)
                pool.dma_start(wo[:], k.io["w_o"][0].rearrange("(c p) n -> p c n", p=P)).then_inc(wo_in, 16)
                pool.dma_start(k.x1[:, 0:NB, :], k.io["x_prompt"][0].rearrange("(b p) n -> p b n", p=P))\
                    .then_inc(x_in, 16)
                pool.dma_start(k.x1[0:DEC, NB, :], x_rows(k, NB)).then_inc(x_in, 16)

            @block.vector
            def _(dve):
                dve.sem_inc(s["part_b"], BANKS)
                dve.sem_inc(s["mixed"], OPEN)
                with dve.Fori(0, TRIPS) as i:
                    dve.wait_ge(s["gates_in"], i * 16 + 16)
                    for j in range(BUFS):
                        t = i * BUFS + j
                        at = 4 * (j % BANKS)
                        g = lambda n: gate[:, n, bass.ds(t, 1), :].rearrange("p a (h n) -> p (a h) n", h=2)
                        mix = mixT[:, bass.ds(t, 1), :].rearrange("p a (h n) -> p (a h) n", h=2)
                        dve.wait_ge(s["ya"], t + 1)
                        dve.tensor_tensor(mix, g(0), ps[:, at:at + 2, 0:H], ALU.mult).then_inc(s["part_a"], 1)
                        dve.wait_ge(s["yb"], t + 1 + BUFS)
                        dve.tensor_tensor(part[:], g(1), ps[:, at + 2:at + 4, 0:H], ALU.mult)\
                            .then_inc(s["part_b"], 1)
                        dve.wait_ge(s["part_a"], t + 1)
                        dve.wait_ge(s["part_b"], t + 1 + BANKS)
                        dve.tensor_tensor(mix, mix, part[:], ALU.add).then_inc(s["mixed"], 1)
                        dve.wait_ge(s["mixed"], t + 1 + OPEN)
                dve.wait_ge(x_in, 32)
                for b in range(NBLK):
                    r = rows_of(b)
                    for h in range(2):
                        n = 2 * b + h
                        dve.wait_ge(s["proj"], n + 1)
                        x = k.x1[0:r, b, h * 512:(h + 1) * 512]
                        dve.tensor_tensor(x, x, ps[0:r, n % 8, :], ALU.add).then_inc(s["kept"], 1)
                dve.wait_ge(s["kept"], 2 * NBLK)

            @block.tensor
            def _(pe):
                pe.sem_inc(s["yb"], BUFS)
                def tile(dst, w, src, pieces):
                    for h in range(2):
                        for c in range(pieces):
                            last = pe.matmul(ps[:, dst + h, 0:H], w[:, c, :], src[:, c, h * H:(h + 1) * H],
                                             start=(c == 0), stop=(c == pieces - 1))
                    return last

                with pe.Fori(0, TRIPS) as i:
                    for j in range(BUFS):
                        t = i * BUFS + j
                        at = 4 * (j % BANKS)
                        pe.wait_ge(w_in[j], i * 32 + 32)
                        pe.wait_ge(s["part_b"], t + 1)
                        tile(at, wb[:, j, 0:CA], k.oT[:, 0:CA], CA).then_inc(s["ya"], 1)
                        tile(at + 2, wb[:, j, CA:CA + CB], k.oT[:, CA:CA + CB], CB).then_inc(s["yb"], 1)
                pe.wait_ge(wo_in, 16)
                pe.wait_ge(s["mixed"], KC + OPEN)
                for b in range(NBLK):
                    r = rows_of(b)
                    for h in range(2):
                        n = 2 * b + h
                        if n >= 8:
                            pe.wait_ge(s["kept"], n - 7)
                        for c in range(KC):
                            last = pe.matmul(ps[0:r, n % 8, :], mixT[:, c, b * P:b * P + r],
                                             wo[:, c, h * 512:(h + 1) * 512], start=(c == 0), stop=(c == KC - 1))
                        last.then_inc(s["proj"], 1)


def route(k):
    nc = k.nc
    NR = E_GROUPS + EXPERTS
    MUL = TOK // SLOT
    BIG = 64.0
    with ExitStack() as ctx:
        hn = k.sb("rt_hn", [P, NBLK, D], ctx=ctx)
        hT = k.sb("rt_hT", [P, KC, TOK], ctx=ctx)
        g_row = k.sb("rt_g_row", [P, D], ctx=ctx)
        rstd = k.sb("rt_rstd", [P, NBLK], ctx=ctx)
        wr = k.sb("rt_wr", [P, KC, NR], ctx=ctx)
        bias = k.sb("rt_bias", [P, NR], ctx=ctx)
        small = lambda name, *shape: k.sb("rt_" + name, [P, NBLK, *shape], ctx=ctx)
        lg = small("lg", NR)
        pick = small("pick", 8)
        mx = [small(f"mx{n}", 1) for n in range(3)]
        low = small("low", 1)
        oh_g = small("oh_g", E_GROUPS)
        oh_k = [small(f"oh{n}", E_PER) for n in range(2)]
        shifted = small("shifted", E_GROUPS)
        eg = small("eg", E_GROUPS)
        pg = small("pg", 1)
        e2 = small("e2", 1)
        by_g = small("by_g", E_GROUPS, E_PER)
        ing = small("ing", E_PER)
        ing2 = small("ing2", E_PER)
        one = [small(f"one{n}", E_GROUPS, E_PER) for n in range(2)]
        both = small("both", EXPERTS)
        rank = small("rank", EXPERTS)
        tmp = small("tmp", EXPERTS)
        col = {n: small("col_" + n, 1) for n in ("rank", "full", "pos", "eid", "base", "slot", "some")}
        at_pos = [small(f"at_pos{n}", SLOT) for n in range(2)]
        at_slot = [small(f"at_slot{n}", 2 * ALL_SLOTS) for n in range(2)]
        cmp_ = k.sb("rt_cmp", [P, EXPERTS, MUL], ctx=ctx)
        more = k.sb("rt_more", [P, EXPERTS], ctx=ctx)
        upto = k.sb("rt_upto", [P, EXPERTS], ctx=ctx)
        base = k.sb("rt_base", [P, EXPERTS], ctx=ctx)
        which = k.sb("rt_which", [1, MORE, EXPERTS], ctx=ctx)
        eid = k.sb("rt_eid", [1, MORE], ctx=ctx)
        empty = k.sb("rt_empty", [SLOT, 2 * ALL_SLOTS], ctx=ctx)
        tr = k.ps("rt_tr", [P, 2, KC, P], ctx)
        lp = k.ps("rt_lp", [P, 512], ctx)
        rp = k.ps("rt_rp", [P, 512], ctx)
        cp = k.ps("rt_cp", [P, 512], ctx)
        tp = k.ps("rt_tp", [P, 512], ctx)
        s = {n: k.sem("rt_" + n, ctx) for n in (
            "in", "g_in", "scaled", "turned", "placed", "h2_out", "logits", "chosen", "exped", "ranks",
            "tables", "slots")}
        own = k.sem("rt_dve", ctx)
        with nc.Block() as block:

            @block.sync
            def _(sp):
                v = lambda name: k.io[name][0].rearrange("(p c) n -> p c n", c=KC)
                sp.dma_start(g_row[:], k.io["g_ffn"][0].partition_broadcast(P)).then_inc(s["g_in"], 16)
                sp.dma_start(wr[:, :, 0:E_GROUPS], v("w_group")).then_inc(s["in"], 16)
                sp.dma_start(wr[:, :, E_GROUPS:NR], v("w_expert")).then_inc(s["in"], 16)
                sp.dma_start(bias[:, 0:E_GROUPS], k.io["b_group"][0].partition_broadcast(P)).then_inc(s["in"], 16)
                sp.dma_start(bias[:, E_GROUPS:NR], k.io["b_expert"][0].partition_broadcast(P)).then_inc(s["in"], 16)
                for q in range(HALVES):
                    load_half(k, sp, q, 0)
                for b in range(NBLK):
                    r = rows_of(b)
                    sp.wait_ge(s["scaled"], b + 1)
                    sp.dma_start(k.io["h2"][b * P:b * P + r, :], hn[0:r, b, :]).then_inc(s["h2_out"], 16)
                sp.wait_ge(s["h2_out"], 16 * NBLK)

            @block.scalar
            def _(act):
                act.wait_ge(s["chosen"], 1)
                act.activation(eg[:], shifted[:], ACT.Exp).then_inc(s["exped"], 1)
                act.wait_ge(s["chosen"], 2)
                act.activation(e2[:], e2[:], ACT.Exp).then_inc(s["exped"], 1)

            @block.tensor
            def _(pe):
                for b in range(NBLK):
                    r = rows_of(b)
                    pe.wait_ge(s["scaled"], b + 1)
                    if b >= 2:
                        pe.wait_ge(s["placed"], b - 1)
                    v = hn[0:r, b, :].rearrange("t (p c) -> t c p", c=KC)
                    for c in range(KC):
                        last = pe.transpose(tr[:, b % 2, c, 0:r], v[:, c, :], k.const("ident", r)[:, 0:r])
                    last.then_inc(s["turned"], 1)
                pe.wait_ge(s["in"], 64)
                pe.wait_ge(s["placed"], NBLK)
                for b in range(NBLK):
                    r = rows_of(b)
                    for c in range(KC):
                        last = pe.matmul(lp[0:r, b * NR:(b + 1) * NR], hT[:, c, b * P:b * P + r], wr[:, c, :],
                                         start=(c == 0), stop=(c == KC - 1))
                last.then_inc(s["logits"], 1)
                pe.wait_ge(s["chosen"], 3)
                for b in range(NBLK):
                    for b2 in range(b + 1):
                        pe.matmul(rp[:, b * EXPERTS:(b + 1) * EXPERTS], k.const("before" if b2 == b else "ones"),
                                  both[:, b2, :], start=(b2 == 0), stop=(b2 == b))
                for b in range(NBLK):
                    last = pe.matmul(cp[:, 0:EXPERTS], k.const("ones"), both[:, b, :], start=(b == 0),
                                     stop=(b == NBLK - 1))
                last.then_inc(s["ranks"], 1)
                pe.wait_ge(s["slots"], 1)
                n = 0
                for q in range(2):
                    for b in range(NBLK):
                        last = pe.matmul(tp[0:SLOT, 0:2 * ALL_SLOTS], at_pos[q][:, b, :], at_slot[q][:, b, :],
                                         start=(n == 0), stop=(n == 2 * NBLK - 1))
                        n += 1
                last.then_inc(s["tables"], 1)

            @block.vector
            def _(dve):
                link = Chain(dve, own)
                tt = lambda o, a, b, op: link(dve.tensor_tensor(o, a, b, op))
                wide = lambda ap, n: ap.to_broadcast([P, NBLK, n])
                real = k.const("real").unsqueeze(2)
                iota = lambda n: k.const("iota")[:, 0:n].unsqueeze(1).to_broadcast([P, NBLK, n])
                link(dve.memset(lg[:], 0.0))
                dve.wait_ge(s["g_in"], 16)
                for b in range(NBLK):
                    r = rows_of(b)
                    link(dve.reciprocal(rstd[0:r, b:b + 1], k.rms[0:r, b:b + 1]))
                    dve.scalar_tensor_tensor(hn[0:r, b, :], k.x1[0:r, b, :], rstd[0:r, b:b + 1], g_row[0:r, :],
                                             ALU.mult, ALU.mult).then_inc(s["scaled"], 1)
                for b in range(NBLK):
                    r = rows_of(b)
                    dve.wait_ge(s["turned"], b + 1)
                    dve.tensor_copy(hT[:, :, b * P:b * P + r], tr[:, b % 2, :, 0:r]).then_inc(s["placed"], 1)
                dve.wait_ge(s["logits"], 1)
                dve.wait_ge(s["in"], 64)
                for b in range(NBLK):
                    r = rows_of(b)
                    last = dve.tensor_tensor(lg[0:r, b, :], lp[0:r, b * NR:(b + 1) * NR], bias[0:r, :], ALU.add)
                link(last)

                def first_largest(vals, n, most, onehot):
                    link(dve.tensor_reduce(most[:], vals, axis=AX, op=ALU.max))
                    tt(pick[:, :, 0:n], vals, wide(most[:], n), ALU.is_equal)
                    link(dve.scalar_tensor_tensor(pick[:, :, 0:n], pick[:, :, 0:n], -BIG, iota(n), ALU.mult, ALU.add))
                    link(dve.tensor_reduce(low[:], pick[:, :, 0:n], axis=AX, op=ALU.min))
                    tt(onehot[:], pick[:, :, 0:n], wide(low[:], n), ALU.is_equal)

                first_largest(lg[:, :, 0:E_GROUPS], E_GROUPS, mx[0], oh_g)
                dve.tensor_tensor(shifted[:], lg[:, :, 0:E_GROUPS], wide(mx[0][:], E_GROUPS), ALU.subtract)\
                    .then_inc(s["chosen"], 1)
                flat = [P, NBLK, E_GROUPS, E_PER]
                tt(by_g[:], lg[:, :, E_GROUPS:NR].rearrange("p b (g e) -> p b g e", g=E_GROUPS),
                   oh_g[:].unsqueeze(3).to_broadcast(flat), ALU.mult)
                link(dve.tensor_reduce(ing[:], by_g[:].rearrange("p b g e -> p b e g"), axis=AX, op=ALU.add))
                first_largest(ing[:], E_PER, mx[1], oh_k[0])
                link(dve.scalar_tensor_tensor(ing2[:], oh_k[0][:], -FAR, ing[:], ALU.mult, ALU.add))
                first_largest(ing2[:], E_PER, mx[2], oh_k[1])
                dve.tensor_tensor(e2[:], mx[2][:], mx[1][:], ALU.subtract).then_inc(s["chosen"], 1)
                for q in range(2):
                    tt(one[q][:], oh_g[:].unsqueeze(3).to_broadcast(flat),
                       oh_k[q][:].unsqueeze(2).to_broadcast(flat), ALU.mult)
                    f = one[q][:].rearrange("p b g e -> p b (g e)")
                    tt(f, f, wide(real, EXPERTS), ALU.mult)
                oh = [o[:].rearrange("p b g e -> p b (g e)") for o in one]
                dve.tensor_tensor(both[:], oh[0], oh[1], ALU.add).then_inc(s["chosen"], 1)
                dve.wait_ge(s["exped"], 2)
                link(dve.tensor_reduce(pg[:], eg[:], axis=AX, op=ALU.add))
                link(dve.reciprocal(pg[:], pg[:]))
                link(dve.tensor_scalar(col["some"][:], e2[:], 1.0, None, ALU.add))
                link(dve.reciprocal(col["some"][:], col["some"][:]))
                tt(k.gate[:, :, 0:1], pg[:], col["some"][:], ALU.mult)
                tt(k.gate[:, :, 1:2], k.gate[:, :, 0:1], e2[:], ALU.mult)
                dve.wait_ge(s["ranks"], 1)
                steps = k.const("steps")
                link(dve.tensor_copy(rank[:].rearrange("p b e -> p (b e)"), rp[:, 0:NBLK * EXPERTS]))
                tt(cmp_[:], cp[:, 0:EXPERTS].unsqueeze(2).to_broadcast([P, EXPERTS, MUL]),
                   steps.unsqueeze(1).to_broadcast([P, EXPERTS, MUL]), ALU.is_gt)
                link(dve.tensor_reduce(more[:], cmp_[:], axis=AX, op=ALU.add))
                link(dve.tensor_tensor_scan(upto[:], k.const("ones")[:, 0:EXPERTS], more[:], 0.0, ALU.mult, ALU.add))
                tt(base[:], upto[:], more[:], ALU.subtract)
                tt(which[:], upto[0:1, :].unsqueeze(1).to_broadcast([1, MORE, EXPERTS]),
                   k.const("iota", 1)[:, 0:MORE].unsqueeze(2).to_broadcast([1, MORE, EXPERTS]), ALU.is_le)
                link(dve.tensor_reduce(eid[:], which[:], axis=AX, op=ALU.add))
                link(dve.tensor_scalar(k.owner[:], eid[:], float(EXPERTS - 1), None, ALU.min))
                link(dve.tensor_copy(k.n_more[:], upto[0:1, EXPERTS - 1:EXPERTS]))
                for q in range(2):
                    def total(out, table):
                        tt(tmp[:], oh[q], table, ALU.mult)
                        link(dve.tensor_reduce(out[:], tmp[:], axis=AX, op=ALU.add))

                    c = col
                    total(c["rank"], rank[:])
                    total(c["eid"], iota(EXPERTS))
                    total(c["base"], base[:].unsqueeze(1).to_broadcast([P, NBLK, EXPERTS]))
                    tt(pick[:], wide(c["rank"][:], MUL), steps.unsqueeze(1).to_broadcast([P, NBLK, MUL]), ALU.is_ge)
                    link(dve.tensor_reduce(c["full"][:], pick[:], axis=AX, op=ALU.add))
                    link(dve.scalar_tensor_tensor(c["pos"][:], c["full"][:], -float(SLOT), c["rank"][:],
                                                  ALU.mult, ALU.add))
                    link(dve.tensor_scalar(c["some"][:], c["full"][:], 0.5, None, ALU.is_ge))
                    tt(c["slot"][:], c["base"][:], c["full"][:], ALU.add)
                    tt(c["slot"][:], c["slot"][:], c["eid"][:], ALU.subtract)
                    link(dve.tensor_scalar(c["slot"][:], c["slot"][:], float(EXPERTS - 1), None, ALU.add))
                    tt(c["slot"][:], c["slot"][:], c["some"][:], ALU.mult)
                    tt(c["slot"][:], c["slot"][:], c["eid"][:], ALU.add)
                    tt(at_pos[q][:], iota(SLOT), wide(c["pos"][:], SLOT), ALU.is_equal)
                    sl = at_slot[q][:, :, 0:ALL_SLOTS]
                    sl2 = at_slot[q][:, :, ALL_SLOTS:2 * ALL_SLOTS]
                    tt(sl, iota(ALL_SLOTS), wide(c["slot"][:], ALL_SLOTS), ALU.is_equal)
                    tt(sl2, sl, wide(k.const("token").unsqueeze(2), ALL_SLOTS), ALU.mult)
                    tt(sl, sl, wide(k.const(f"pair{q}").unsqueeze(2), ALL_SLOTS), ALU.mult)
                dve.sem_inc(s["slots"], 1)
                dve.wait_ge(s["tables"], 1)
                v = tp[0:SLOT, 0:2 * ALL_SLOTS]
                link(dve.memset(k.index[:], NONE))
                link(dve.tensor_scalar(empty[:], v, 0.0, float(NONE), ALU.is_equal, ALU.mult))
                for n in range(2):
                    part = slice(n * ALL_SLOTS, (n + 1) * ALL_SLOTS)
                    link(dve.scalar_tensor_tensor(k.index[:, n, 0:ALL_SLOTS], v[:, part], -1.0, empty[:, part],
                                                  ALU.add, ALU.add))


def load_half(k, sp, q, e):
    name, c = (("w_gate_e", KC), ("w_up_e", KC), ("w_down_e", FC))[q // 2]
    rows = slice(q % 2 * c // 2, (q % 2 + 1) * c // 2)
    sp.dma_start(k.raw[:, q].rearrange("p (c n) -> p c n", c=c // 2),
                 k.io[name][0, bass.ds(e, 1)].rearrange("a (p c) n -> p (a c) n", c=c)[:, rows])\
        .then_inc(k.raw_in[q], 16)


def experts(k):
    nc = k.nc
    with ExitStack() as ctx:
        raw, raw_in = k.raw, k.raw_in
        hi = k.sb("ex_hi", [P, SPLITS, HALF], F32R, ctx=ctx)
        lo = k.sb("ex_lo", [P, SPLITS, HALF], F32R, ctx=ctx)
        xg = k.sb("ex_xg", [SLOT, 2, D], ctx=ctx)
        xT = k.sb("ex_xT", [P, KC, 2, SLOT], F32R, ctx=ctx)
        gu_low = k.sb("ex_gu_low", [SLOT, 2, FF], ctx=ctx)
        y_low = k.sb("ex_y_low", [SLOT, 2, 512], ctx=ctx)
        gu = k.sb("ex_gu", [SLOT, 2, FF], ctx=ctx)
        sg, hm = gu_low[:, 0], gu[:, 1]
        hmT = k.sb("ex_hmT", [P, FC, 2, SLOT], F32R, ctx=ctx)
        yg = k.sb("ex_yg", [SLOT, 2, D], ctx=ctx)
        opened = k.sb("ex_opened", [1, 2], ctx=ctx)
        from_row = k.sb("ex_from", [SLOT, 2, 1], U32, ctx=ctx)
        to_row = k.sb("ex_to", [SLOT, 2, 1], U32, ctx=ctx)
        xp = k.ps("ex_xp", [P, KC, SLOT], ctx)
        gp = k.ps("ex_gp", [P, 2, 2, FF], ctx)
        hp = k.ps("ex_hp", [P, FC, P], ctx)
        yp = k.ps("ex_yp", [P, 2, 512], ctx)
        x_in = [k.pool_sem(f"ex_x_in{j}") for j in range(2)]
        y_out = [k.pool_sem(f"ex_y_out{j}") for j in range(2)]
        from_laid = [k.sem(f"ex_from_laid{j}", ctx) for j in range(2)]
        hi_made = [k.sem(f"ex_hi_made{n}", ctx) for n in range(SPLITS)]
        lo_made = [k.sem(f"ex_lo_made{n}", ctx) for n in range(SPLITS)]
        split_used = [k.sem(f"ex_split_used{n}", ctx) for n in range(SPLITS)]
        s = {n: k.sem("ex_" + n, ctx) for n in (
            "cleared", "turned", "x_hi", "x_lo", "gu_low", "gu_kept", "silu", "h_made", "h_turned", "h_hi",
            "h_lo", "y_low", "y_kept", "to_laid")}
        go_pe, go_pool = k.sem("ex_go_pe", ctx), k.sem("ex_go_pool", ctx)
        TRIPS, ALL = EXPERTS // 2, ALL_SLOTS // 2
        USES = 2 * HALVES // SPLITS
        GU, DN = range(0, 4), range(4, HALVES)
        GATE, UP = GU[:2], GU[2:]

        def split(at, n):
            f = at[1] + n
            return f % SPLITS, at[0] * USES + f // SPLITS

        def wait_product(eng, at, n):
            n, before = split(at, n)
            eng.wait_ge(split_used[n], before + 1 + OPEN)

        def passes(eng, gate, up, down, x_next, mix, hidden, keep):
            def pair(i, first, places):
                own0, down1, own1, down0 = places
                gate(i, 0, own0)
                if not first:
                    keep(i - 1, 0, (i - 1, down0[1]))
                    hidden(i - 1, 1)
                up(i, 0, own0)
                if not first:
                    down(i - 1, 1, down1)
                x_next(i, 0)
                mix(i, 0, own0)
                gate(i, 1, own1)
                if not first:
                    keep(i - 1, 1, down1)
                hidden(i, 0)
                up(i, 1, own1)
                down(i, 0, down0)
                x_next(i, 1)
                mix(i, 1, own1)

            pair(0, True, ((0, 0), None, (0, 4), (0, 8)))
            with eng.Fori(1, TRIPS) as i:
                pair(i, False, ((i, -2), (i, 2), (i, 4), (i, 8)))
            keep(TRIPS - 1, 0, (TRIPS - 1, 8))
            hidden(TRIPS - 1, 1)
            down(TRIPS - 1, 1, (TRIPS, -2))
            keep(TRIPS - 1, 1, (TRIPS, -2))
            n = eng.value_load(k.n_more[0:1, 0:1], min_val=0, max_val=MORE)
            with eng.If(n > 0):
                with eng.Fori(TRIPS, ALL) as i:
                    for j in range(2):
                        gate(i, j, (i, HALVES * j))
                        up(i, j, (i, HALVES * j))
                        x_next(i, j)
                        mix(i, j, (i, HALVES * j))
                        hidden(i, j)
                        down(i, j, (i, HALVES * j + 4))
                        keep(i, j, (i, HALVES * j + 4))

        none = lambda *_: None

        with nc.Block() as block:

            @block.sync
            def _(sp):
                def load(halves, i, j, before):
                    for n, q in enumerate(halves):
                        m, uses = split(before, n)
                        sp.wait_ge(lo_made[m], uses + 1)
                        load_half(k, sp, q, i * 2 + j)

                load(GU, 0, 1, (0, 0))
                with sp.Fori(1, TRIPS) as i:
                    load(GU, i, 0, (i - 1, 4))
                    load(DN, i - 1, 1, (i - 1, 8))
                    load(GU, i, 1, (i, -2))
                    load(DN, i, 0, (i, 2))
                load(DN, TRIPS - 1, 1, (TRIPS - 1, 8))
                n = sp.value_load(k.n_more[0:1, 0:1], min_val=0, max_val=MORE)
                with sp.If(n > 0):
                    for m in range(SPLITS):
                        sp.wait_ge(lo_made[m], TRIPS * USES)
                    with sp.Fori(TRIPS, ALL) as i:
                        for j in range(2):
                            e = sp.value_load(k.owner[0:1, bass.ds(i * 2 + (j - EXPERTS), 1)], min_val=0,
                                              max_val=EXPERTS - 1)
                            for q in range(HALVES):
                                if j:
                                    m, uses = split((i, 0), q)
                                else:
                                    m, uses = split((i - 1, HALVES), q)
                                sp.wait_ge(lo_made[m], uses + 1)
                                load_half(k, sp, q, e)

            @block.gpsimd
            def _(pool):
                for j in range(2):
                    pool.dma_start(opened[:, j:j + 1], k.io["g_final"].unsqueeze(0)[:, 0:1]).then_inc(y_out[j], 16)

                def gather(j):
                    pool.indirect_dma_start(xg[:, j, :], None, k.io["h2"], bass.IndirectOffsetOnAxis(
                        ap=from_row[:, j, :], axis=0), bounds_check=TOK - 1, oob_is_err=False).then_inc(x_in[j], 16)

                def x_next(i, j):
                    pool.wait_ge(from_laid[j], i + 2)
                    pool.wait_ge(s["turned"], i * 2 + (j + 1))
                    pool.sem_inc(go_pool, 1)
                    gather(j)

                def keep(i, j, at):
                    pool.wait_ge(s["y_kept"], i * 2 + (j + 1))
                    pool.wait_ge(s["to_laid"], i * 2 + (j + 1))
                    pool.sem_inc(go_pool, 1)
                    pool.indirect_dma_start(k.io["pairs"], bass.IndirectOffsetOnAxis(ap=to_row[:, j, :], axis=0),
                                            yg[:, j, :], None, bounds_check=2 * TOK - 1,
                                            oob_is_err=False).then_inc(y_out[j], 16)

                pool.wait_ge(s["cleared"], 1)
                for j in range(2):
                    pool.wait_ge(from_laid[j], 1)
                    gather(j)
                passes(pool, none, none, none, x_next, none, none, keep)
                for j in range(2):
                    pool.wait_ge(y_out[j], 16 * TRIPS + 16)
                    pool.wait_ge(x_in[j], 16 * (TRIPS + 1))
                n = pool.value_load(k.n_more[0:1, 0:1], min_val=0, max_val=MORE)
                with pool.If(n > 0):
                    for j in range(2):
                        pool.wait_ge(y_out[j], 16 * ALL + 16)
                        pool.wait_ge(x_in[j], 16 * (ALL + 1))

            @block.scalar
            def _(act):
                for sem in split_used:
                    act.sem_inc(sem, OPEN)

                def high(i, j, at, halves, skip=0):
                    for n, q in enumerate(halves):
                        m, before = split(at, skip + n)
                        act.wait_ge(raw_in[q], i * 32 + (j + 1) * 16)
                        act.wait_ge(split_used[m], before + OPEN)
                        act.activation(hi[:, m], raw[:, q], ACT.Copy).then_inc(hi_made[m], 1)

                def gate(i, j, at):
                    high(i, j, at, GATE)

                def up(i, j, at):
                    high(i, j, at, UP, skip=2)

                def down(i, j, at):
                    high(i, j, at, DN)

                def x_high(e):
                    act.wait_ge(s["turned"], e + 1)
                    act.activation(xT[:, :, 0, :], xp[:], ACT.Copy).then_inc(s["x_hi"], 1)

                def mix(i, j, at):
                    wait_product(act, at, 3)
                    act.activation(gu_low[:], gp[SLOT:2 * SLOT, j], ACT.Copy).then_inc(s["gu_low"], 1)
                    act.wait_ge(s["gu_kept"], i * 2 + (j + 1))
                    act.activation(sg, gu[:, 0], ACT.Silu).then_inc(s["silu"], 1)

                def keep(i, j, at):
                    wait_product(act, at, 1)
                    act.activation(y_low[:], yp[SLOT:2 * SLOT], ACT.Copy).then_inc(s["y_low"], 1)

                def hidden(i, j):
                    act.wait_ge(s["h_turned"], i * 2 + (j + 1))
                    act.activation(hmT[:, :, 0, :], hp[:, :, 0:SLOT], ACT.Copy).then_inc(s["h_hi"], 1)

                x_high(0)
                passes(act, gate, up, down, lambda i, j: x_high(i * 2 + (j + 1)), mix, hidden, keep)

            @block.vector
            def _(dve):
                def lay(dst, n, slot, j, sem):
                    dve.tensor_copy(dst[:, j, :], k.index[:, n, bass.ds(slot, 1)]).then_inc(sem, 1)

                def low(at, halves, skip=0):
                    for n, q in enumerate(halves):
                        m, before = split(at, skip + n)
                        dve.wait_ge(hi_made[m], before + 1)
                        dve.tensor_tensor(lo[:, m], raw[:, q], hi[:, m], ALU.subtract).then_inc(lo_made[m], 1)

                def gate(i, j, at):
                    low(at, GATE)

                def up(i, j, at):
                    low(at, UP, skip=2)

                def down(i, j, at):
                    low(at, DN)

                def x_low(e):
                    dve.wait_ge(s["x_hi"], e + 1)
                    dve.tensor_tensor(xT[:, :, 1, :], xp[:], xT[:, :, 0, :], ALU.subtract).then_inc(s["x_lo"], 1)

                def x_next(i, j):
                    dve.wait_ge(x_in[j], i * 16 + 16)
                    lay(from_row, 1, i * 2 + (j + 2), j, from_laid[j])
                    x_low(i * 2 + (j + 1))

                def mix(i, j, at):
                    dve.wait_ge(s["gu_low"], i * 2 + (j + 1))
                    dve.tensor_tensor(gu[:], gp[0:SLOT, j], gu_low[:], ALU.add).then_inc(s["gu_kept"], 1)
                    dve.wait_ge(s["silu"], i * 2 + (j + 1))
                    dve.tensor_tensor(hm, sg, gu[:, 1], ALU.mult).then_inc(s["h_made"], 1)

                def keep(i, j, at):
                    dve.wait_ge(s["y_low"], i * 2 + (j + 1))
                    dve.wait_ge(y_out[j], i * 16 + 16)
                    lay(to_row, 0, i * 2 + j, j, s["to_laid"])
                    dve.tensor_tensor(yg[:, j, :].rearrange("t (h n) -> t h n", h=2), yp[0:SLOT], y_low[:],
                                      ALU.add).then_inc(s["y_kept"], 1)

                def hidden(i, j):
                    dve.wait_ge(s["h_hi"], i * 2 + (j + 1))
                    dve.tensor_tensor(hmT[:, :, 1, :], hp[:, :, 0:SLOT], hmT[:, :, 0, :],
                                      ALU.subtract).then_inc(s["h_lo"], 1)

                dve.memset(xg[:], 0.0).then_inc(s["cleared"], 1)
                for j in range(2):
                    lay(from_row, 1, j, j, from_laid[j])
                x_low(0)
                passes(dve, gate, up, down, x_next, mix, hidden, keep)

            @block.tensor
            def _(pe):
                def turn(i, j):
                    pe.wait_ge(x_in[j], i * 16 + 16)
                    pe.sem_inc(go_pe, 1)
                    v = xg[:, j, :].rearrange("t (p c) -> t c p", c=KC)
                    for c in range(KC):
                        last = pe.transpose(xp[:, c, :], v[:, c, :], k.const("ident", SLOT)[:, 0:SLOT])
                    last.then_inc(s["turned"], 1)

                def multiply(at, n, q, out, x):
                    m, before = split(at, n)
                    pe.wait_ge(lo_made[m], before + 1)
                    c = FC // 2 if q >= 4 else KC // 2
                    width = HALF // c
                    for w in (hi, lo):
                        for c1 in range(c):
                            for h in range(width // 512):
                                o = c1 * width + h * 512
                                last = pe.matmul(out[:, h], x[:, q % 2 * c + c1].rearrange("p a t -> p (a t)"),
                                                 w[:, m, o:o + 512],
                                                 start=(q % 2 == 0 and w is hi and c1 == 0),
                                                 stop=(q % 2 == 1 and w is lo and c1 == c - 1))
                    last.then_inc(split_used[m], 1)

                def gate(i, j, at):
                    pe.wait_ge(s["x_lo"], i * 2 + (j + 1))
                    for n, q in enumerate(GATE):
                        multiply(at, n, q, gp[:, j, 0:1], xT)

                def up(i, j, at):
                    for n, q in enumerate(UP):
                        multiply(at, 2 + n, q, gp[:, j, 1:2], xT)
                    turn(i + j, 1 - j)

                def down(i, j, at):
                    pe.wait_ge(s["h_lo"], i * 2 + (j + 1))
                    if not (isinstance(i, int) and i == j == 0):
                        pe.wait_ge(s["y_kept"], i * 2 + j)
                    for n, q in enumerate(DN):
                        multiply(at, n, q, yp, hmT)

                def mix(i, j, at):
                    pe.wait_ge(s["h_made"], i * 2 + (j + 1))
                    pe.sem_inc(go_pe, 1)
                    v = hm.rearrange("t (p c) -> t c p", c=FC)
                    for c in range(FC):
                        last = pe.transpose(hp[:, c, 0:SLOT], v[:, c, :], k.const("ident", SLOT)[:, 0:SLOT])
                    last.then_inc(s["h_turned"], 1)

                turn(0, 0)
                passes(pe, gate, up, down, none, mix, none, none)


def finish(k):
    nc = k.nc
    with ExitStack() as ctx:
        two = k.sb("fn_two", [P, NBLK, 2, D], ctx=ctx)
        gf = k.sb("fn_gf", [P, D], ctx=ctx)
        junk = k.sb("fn_junk", [P, D], ctx=ctx)
        ms = k.sb("fn_ms", [P, NBLK], ctx=ctx)
        rms = k.sb("fn_rms", [P, NBLK], ctx=ctx)
        rstd = k.sb("fn_rstd", [P, NBLK], ctx=ctx)
        two_in = [k.sem(f"fn_in{b}", ctx) for b in range(NBLK)]
        s = {n: k.sem("fn_" + n, ctx) for n in ("added", "squares", "roots", "scaled", "out")}
        own = k.sem("fn_dve", ctx)
        gf_in = k.pool_sem("fn_gf_in")
        with nc.Block() as block:

            @block.sync
            def _(sp):
                for b in range(NBLK):
                    r = rows_of(b)
                    sp.dma_start(two[0:r, b], k.io["pairs"].rearrange("(t k) n -> t k n", k=2)[b * P:b * P + r])\
                        .then_inc(two_in[b], 16)
                for b in range(NBLK):
                    r = rows_of(b)
                    out = k.io["o_y"][b * P:(b + 1) * P, :] if b < NB else k.io["o_ys"]
                    sp.wait_ge(s["scaled"], b + 1)
                    sp.dma_start(out, k.x1[0:r, b, :]).then_inc(s["out"], 16)
                sp.wait_ge(s["out"], 16 * NBLK)

            @block.gpsimd
            def _(pool):
                pool.dma_start(gf[:], k.io["g_final"].partition_broadcast(P)).then_inc(gf_in, 16)

            @block.vector
            def _(dve):
                link = Chain(dve, own)

                def add(b):
                    r = rows_of(b)
                    x = k.x1[0:r, b, :]
                    dve.wait_ge(two_in[b], 16)
                    link(dve.scalar_tensor_tensor(x, two[0:r, b, 0, :], k.gate[0:r, b, 0:1], x, ALU.mult, ALU.add))
                    dve.scalar_tensor_tensor(x, two[0:r, b, 1, :], k.gate[0:r, b, 1:2], x, ALU.mult,
                                             ALU.add).then_inc(s["added"], 1)

                def scale(b):
                    r = rows_of(b)
                    x = k.x1[0:r, b, :]
                    dve.wait_ge(s["roots"], b + 1)
                    link(dve.reciprocal(rstd[0:r, b:b + 1], rms[0:r, b:b + 1]))
                    dve.scalar_tensor_tensor(x, x, rstd[0:r, b:b + 1], gf[0:r, :], ALU.mult,
                                             ALU.mult).then_inc(s["scaled"], 1)

                add(0)
                dve.wait_ge(gf_in, 16)
                for b in range(1, NBLK):
                    add(b)
                    scale(b - 1)
                scale(NBLK - 1)

            @block.scalar
            def _(act):
                for b in range(NBLK):
                    r = rows_of(b)
                    act.wait_ge(s["added"], b + 1)
                    act.activation(junk[0:r, :], k.x1[0:r, b, :], ACT.Square,
                                   accum_out=ms[0:r, b:b + 1]).then_inc(s["squares"], 1)
                    act.wait_ge(s["squares"], b + 1)
                    act.activation(rms[0:r, b:b + 1], ms[0:r, b:b + 1], ACT.Sqrt, bias=k.const("eps", r),
                                   scale=1.0 / D).then_inc(s["roots"], 1)


STEPS = [prepare, project, weigh_a, attend_a, attend_b, decode_b, merge, route, experts, finish]


INPUTS = ["x_prompt", "x_sample", "cache_k_a", "cache_v_a", "page_table", "cache_kv_b0", "cache_kv_b1", "cache_kv_b2",
          "g_attn", "w_in", "b_sb", "w_br_a", "w_br_b", "w_o", "g_ffn", "w_group", "b_group", "w_expert", "b_expert",
          "w_gate_e", "w_up_e", "w_down_e", "g_final"]


def outputs():
    out = [("o_y", (SEQ, D)), ("o_ys", (DEC, D)), ("o_ka", (SEQ, WA)), ("o_va", (SEQ, WA)),
           ("o_kas", (DEC, WA)), ("o_vas", (DEC, WA))]
    out += [(f"o_kvp{g}", (min(w, SEQ), 2 * WBO)) for g, (w, _) in enumerate(GROUPS)]
    out += [(f"o_kvs{g}", (DEC, w, 2 * WBO)) for g, (w, _) in enumerate(GROUPS)]
    return out


def build(nc, io, at, stop=99):
    with ExitStack() as ctx:
        k = Kernel(nc, ctx, io, at)
        k.consts = k.sb("consts_sb", [P, at["rel"][0]])
        k.g_attn = k.sb("g_attn_sb", [P, KC])
        k.b_sb = k.sb("b_sb_sb", [P, HA])
        k.pages = k.sb("pages_sb", [1, DEC * PAGES], I32)
        k.shifted = ctx.enter_context(nc.semaphore("shifted"))
        steps = STEPS[:stop]
        k.oT = k.sb("oT", [P, (WA + WBO) // P, TOK])
        with ExitStack() as inner:
            k.qk = k.sb("qk", [P, QK_TILES, SEQ], ctx=inner)
            k.v_rows = k.sb("v_rows", [P, NB, WA + WB], ctx=inner)
            k.samp = k.sb("samp", [DEC, TILES * P], ctx=inner)
            with ExitStack() as branch_a:
                k.scores = k.sb("scores", [P, DEC, HA, PAGES], ctx=branch_a)
                with ExitStack() as projecting:
                    k.hT = k.sb("hT", [P, KC, TOK], ctx=projecting)
                    k.w = k.sb("w_slots", [P, 2, KC, P], ctx=projecting)
                    k.w_in = [k.sem(f"w_in{j}", projecting) for j in range(2)]
                    for f in steps[:2]:
                        f(k)
                for f in steps[2:4]:
                    f(k)
            k.kv = k.sb("kv", [P, DEC, NG, 2 * WBO], ctx=inner)
            k.tables_b = k.sb("tables_b", [P, io["consts"].shape[1] - at["rel"][0]], ctx=inner)
            k.kv_in = k.sem("kv_in", inner)
            for f in steps[4:6]:
                f(k)
        k.x1 = k.sb("x1", [P, NBLK, D])
        k.rms = k.sb("rms", [P, NBLK])
        k.gate = k.sb("gate", [P, NBLK, 2])
        k.index = k.sb("index", [SLOT, 2, ALL_SLOTS + 2], U32)
        k.owner = k.sb("owner", [1, MORE], I32)
        k.n_more = k.sb("n_more", [1, 1], I32)
        for f in steps[6:7]:
            f(k)
        k.raw = k.sb("raw", [P, HALVES, HALF])
        k.raw_in = [ctx.enter_context(nc.semaphore(f"raw_in{q}")) for q in range(HALVES)]
        for f in steps[7:8]:
            f(k)
        k.clear_semaphores()
        for f in steps[8:]:
            f(k)
        if stop > 4:
            with nc.Block() as block:
                @block.sync
                def _(sp):
                    sp.wait_ge(k.shifted, 16 * NG)


def kernel(**inputs):
    import concourse.bacc as bacc
    from concourse.bass_utils import run_bass_kernel_spmd

    nc = bacc.Bacc("TRN2", target_bir_lowering=False, num_devices=1)
    at, consts = constants()
    arrays = {"in_consts": consts}
    io = {"consts": nc.dram_tensor("in_consts", consts.shape, F32, kind="ExternalInput").ap()}
    for name in INPUTS:
        a = np.ascontiguousarray(inputs[name])
        arrays[f"in_{name}"] = a
        io[name] = nc.dram_tensor(f"in_{name}", a.shape, mybir.dt.from_np(a.dtype), kind="ExternalInput").ap()
    for name, shape in outputs():
        io[name] = nc.dram_tensor(name, shape, F32, kind="ExternalOutput").ap()
    io["h2"] = nc.dram_tensor("h2_rows", (TOK, D), F32).ap()
    io["gates"] = nc.dram_tensor("gate_rows", (P, GATE_TILES, TOK), F32).ap()
    io["pairs"] = nc.dram_tensor("pair_rows", (2 * TOK, D), F32).ap()
    build(nc, io, at)
    got = run_bass_kernel_spmd(nc, [arrays], core_ids=[0]).results[0]
    g = [got[name] for name, _ in outputs()]
    kv = (2, SLOTS_B, HD)
    return (g[0].reshape(1, SEQ, D), g[1].reshape(DEC, 1, D),
            g[2].reshape(1, 1, SEQ, HA, HD), g[3].reshape(1, 1, SEQ, HA, HD),
            g[4].reshape(1, DEC, 1, HA, HD), g[5].reshape(1, DEC, 1, HA, HD),
            *(g[6 + n].reshape(1, 1, min(w, SEQ), *kv) for n, (w, _) in enumerate(GROUPS)),
            *(g[9 + n].reshape(1, DEC, w, *kv) for n, (w, _) in enumerate(GROUPS)))
```
